# Optimizing a Trainium2 kernel written in Bass

```python
import jax, jax.numpy as jnp
from jax import lax
import numpy as np

D_MODEL = 1024
BATCH = 1
SEQ = 2048
DEPTH = 2

EPS = 1e-6
GLA_HEADS = 4
GLA_DK = 64
GLA_DV = 128
GLA_GATE_RANK = 16
GLA_TAU = 16.0
GLA_CHUNK = 64
GLA_WIDTH = GLA_HEADS * GLA_DV
MLA_HEADS = 4
MLA_Q_RANK = 256
MLA_KV_RANK = 128
MLA_NOPE = 128
MLA_ROPE = 64
MLA_V = 128
MLA_QBLOCK = 128
MLA_WIDTH = MLA_HEADS * MLA_V
ROPE_THETA = 10000.0
SG_GROUPS = 8
SG_WIDTH = 2 * D_MODEL
SG_CHUNK = 128

N_EVEN = (DEPTH + 1) // 2
N_ODD = DEPTH // 2

EVEN_SPLITS = (GLA_HEADS * GLA_DK, GLA_HEADS * GLA_DK, GLA_WIDTH, GLA_GATE_RANK, GLA_GATE_RANK, GLA_WIDTH,
               MLA_Q_RANK, MLA_KV_RANK, MLA_ROPE, MLA_WIDTH)
EVEN_IN = sum(EVEN_SPLITS)
ODD_IN = 3 * SG_WIDTH

kernel_name = "hybrid_gla_mla_gmlp_encoder"

def _split(x, sizes):
    out, o = [], 0
    for s in sizes:
        out.append(x[..., o:o + s])
        o += s
    return out

def rms_norm(x, g):
    xf = x.astype(jnp.float32)
    y = xf * lax.rsqrt(jnp.mean(xf * xf, axis=-1, keepdims=True) + EPS)
    return (y * g.astype(jnp.float32)).astype(x.dtype)

def layer_norm(x, g, b):
    xf = x.astype(jnp.float32)
    mu = jnp.mean(xf, axis=-1, keepdims=True)
    var = jnp.mean(jnp.square(xf - mu), axis=-1, keepdims=True)
    y = (xf - mu) * lax.rsqrt(var + EPS)
    return (y * g.astype(jnp.float32) + b.astype(jnp.float32)).astype(x.dtype)

def apply_rope(x, cos, sin):
    x1, x2 = jnp.split(x, 2, axis=-1)
    return jnp.concatenate([x1 * cos - x2 * sin, x2 * cos + x1 * sin], axis=-1)

def gla_scan(q, k, v, g, strict):
    B, S, H, dk = q.shape
    dv = v.shape[-1]
    N = S // GLA_CHUNK

    def to_chunks(t):
        return t.reshape(B, N, GLA_CHUNK, H, t.shape[-1]).transpose(1, 0, 3, 2, 4)

    mask = jnp.tril(jnp.ones((GLA_CHUNK, GLA_CHUNK), bool), k=-1 if strict else 0)

    def step(state, inp):
        qc, kc, vc, gc = inp
        b = jnp.cumsum(gc, axis=2)
        diff = b[:, :, :, None, :] - b[:, :, None, :, :]
        decay = jnp.exp(jnp.where(mask[None, None, :, :, None], diff, -jnp.inf))
        att = jnp.einsum('bhid,bhjd,bhijd->bhij', qc, kc, decay)
        o = jnp.einsum('bhij,bhjv->bhiv', att, vc) + jnp.einsum('bhid,bhdv->bhiv', qc * jnp.exp(b), state)
        b_last = b[:, :, -1, :]
        state = jnp.exp(b_last)[..., None] * state + jnp.einsum(
            'bhjd,bhjv->bhdv', kc * jnp.exp(b_last[:, :, None, :] - b), vc)
        return state, o

    s0 = jnp.zeros((B, H, dk, dv), jnp.float32)
    _, outs = lax.scan(step, s0, (to_chunks(q), to_chunks(k), to_chunks(v), to_chunks(g)))
    return outs.transpose(1, 0, 3, 2, 4).reshape(B, S, H, dv)

def gla_branch(q, k, v, a_f, a_b, z, w2_f, b_f, w2_b, b_b, g_norm):
    B, S, _ = q.shape
    q = q.reshape(B, S, GLA_HEADS, GLA_DK) * (GLA_DK ** -0.5)
    k = k.reshape(B, S, GLA_HEADS, GLA_DK)
    v = v.reshape(B, S, GLA_HEADS, GLA_DV)
    g_f = (jax.nn.log_sigmoid((a_f @ w2_f + b_f).astype(jnp.float32)) / GLA_TAU).reshape(B, S, GLA_HEADS, GLA_DK)
    g_b = (jax.nn.log_sigmoid((a_b @ w2_b + b_b).astype(jnp.float32)) / GLA_TAU).reshape(B, S, GLA_HEADS, GLA_DK)
    o_f = gla_scan(q, k, v, g_f, False)
    flip = lambda t: jnp.flip(t, axis=1)
    o_b = flip(gla_scan(flip(q), flip(k), flip(v), flip(g_b), True))
    o = rms_norm((o_f + o_b).astype(z.dtype), g_norm).reshape(B, S, GLA_WIDTH)
    return o * jax.nn.silu(z)

def mla_branch(cq, ckv, kr, z, g_q, w_uq, g_kv, w_ukv, cos, sin):
    B, S, _ = cq.shape
    q = (rms_norm(cq, g_q) @ w_uq).reshape(B, S, MLA_HEADS, MLA_NOPE + MLA_ROPE)
    qn, qr = q[..., :MLA_NOPE], q[..., MLA_NOPE:]
    qr = apply_rope(qr, cos[:, :, None, :], sin[:, :, None, :])
    kv = (rms_norm(ckv, g_kv) @ w_ukv).reshape(B, S, MLA_HEADS, MLA_NOPE + MLA_V)
    kn, v = kv[..., :MLA_NOPE], kv[..., MLA_NOPE:]
    kr = apply_rope(kr, cos, sin)
    scale = (MLA_NOPE + MLA_ROPE) ** -0.5
    nb = S // MLA_QBLOCK
    qn_b = (qn * scale).reshape(B, nb, MLA_QBLOCK, MLA_HEADS, MLA_NOPE).transpose(1, 0, 2, 3, 4)
    qr_b = (qr * scale).reshape(B, nb, MLA_QBLOCK, MLA_HEADS, MLA_ROPE).transpose(1, 0, 2, 3, 4)

    def attend(blk):
        qn_i, qr_i = blk
        s = jnp.einsum('bqhd,bkhd->bhqk', qn_i, kn) + jnp.einsum('bqhr,bkr->bhqk', qr_i, kr)
        p = jax.nn.softmax(s.astype(jnp.float32), axis=-1).astype(v.dtype)
        return jnp.einsum('bhqk,bkhd->bqhd', p, v)

    o = lax.map(attend, (qn_b, qr_b))
    o = o.transpose(1, 0, 2, 3, 4).reshape(B, S, MLA_WIDTH)
    return o * jax.nn.silu(z)

def sgmlp_branch(p, g_ln, b_ln, w_s, b_s):
    B, S, _ = p.shape
    uv, z = p[..., :2 * SG_WIDTH], p[..., 2 * SG_WIDTH:]
    uv = jax.nn.gelu(uv, approximate=False)
    u, v = uv[..., :SG_WIDTH], uv[..., SG_WIDTH:]
    v = layer_norm(v, g_ln, b_ln)
    n = S // SG_CHUNK
    vc = v.reshape(B, n, SG_CHUNK, SG_GROUPS, SG_WIDTH // SG_GROUPS)
    mixed = jnp.einsum('gij,bnjgc->bnigc', w_s, vc) + b_s.T[:, :, None]
    return u * mixed.reshape(B, S, SG_WIDTH) * jax.nn.silu(z)

def setup_inputs(seed: int = 0) -> dict:
    key = jax.random.key(seed)
    ks = jax.random.split(key, 32)
    nrm = lambda k, shape, s: jax.random.normal(k, shape, jnp.float32) * s
    gain = lambda k, shape: 1.0 + nrm(k, shape, 0.02)
    D = D_MODEL
    x = nrm(ks[0], (BATCH, SEQ, D), 1.0)
    c = nrm(ks[1], (BATCH, D), 1.0)
    positions = jnp.arange(SEQ, dtype=jnp.int32)[None, :] + jax.random.randint(ks[2], (BATCH, 1), 0, 1024, jnp.int32)
    return {
        "x": x,
        "c": c,
        "positions": positions,
        "w_mod": nrm(ks[3], (DEPTH, D, 3 * D), 0.5 * D ** -0.5),
        "b_mod": nrm(ks[4], (DEPTH, 3 * D), 0.1),
        "g_pre": gain(ks[5], (DEPTH, D)),
        "g_post": gain(ks[6], (DEPTH, D)),
        "w_in_e": nrm(ks[7], (N_EVEN, D, EVEN_IN), D ** -0.5),
        "gla_w_gate_f": nrm(ks[8], (N_EVEN, GLA_GATE_RANK, GLA_HEADS * GLA_DK), GLA_GATE_RANK ** -0.5),
        "gla_b_gate_f": nrm(ks[9], (N_EVEN, GLA_HEADS * GLA_DK), 0.5),
        "gla_w_gate_b": nrm(ks[10], (N_EVEN, GLA_GATE_RANK, GLA_HEADS * GLA_DK), GLA_GATE_RANK ** -0.5),
        "gla_b_gate_b": nrm(ks[11], (N_EVEN, GLA_HEADS * GLA_DK), 0.5),
        "gla_g_norm": gain(ks[12], (N_EVEN, GLA_DV)),
        "mla_g_q": gain(ks[13], (N_EVEN, MLA_Q_RANK)),
        "mla_w_uq": nrm(ks[14], (N_EVEN, MLA_Q_RANK, MLA_HEADS * (MLA_NOPE + MLA_ROPE)), MLA_Q_RANK ** -0.5),
        "mla_g_kv": gain(ks[15], (N_EVEN, MLA_KV_RANK)),
        "mla_w_ukv": nrm(ks[16], (N_EVEN, MLA_KV_RANK, MLA_HEADS * (MLA_NOPE + MLA_V)), MLA_KV_RANK ** -0.5),
        "w_out_e": nrm(ks[17], (N_EVEN, GLA_WIDTH + MLA_WIDTH, D), (GLA_WIDTH + MLA_WIDTH) ** -0.5),
        "w_in_o": nrm(ks[18], (N_ODD, D, ODD_IN), D ** -0.5),
        "sg_g_norm": gain(ks[19], (N_ODD, SG_WIDTH)),
        "sg_b_norm": nrm(ks[20], (N_ODD, SG_WIDTH), 0.02),
        "sg_w_s": nrm(ks[21], (N_ODD, SG_GROUPS, SG_CHUNK, SG_CHUNK), SG_CHUNK ** -0.5),
        "sg_b_s": 1.0 + nrm(ks[22], (N_ODD, SG_GROUPS, SG_CHUNK), 0.1),
        "w_out_o": nrm(ks[23], (N_ODD, SG_WIDTH, D), SG_WIDTH ** -0.5),
    }

def reference(x, c, positions, w_mod, b_mod, g_pre, g_post, w_in_e, gla_w_gate_f, gla_b_gate_f,
              gla_w_gate_b, gla_b_gate_b, gla_g_norm, mla_g_q, mla_w_uq, mla_g_kv, mla_w_ukv, w_out_e,
              w_in_o, sg_g_norm, sg_b_norm, sg_w_s, sg_b_s, w_out_o):
    inv_freq = 1.0 / (ROPE_THETA ** (jnp.arange(0, MLA_ROPE, 2, dtype=jnp.float32) / MLA_ROPE))
    ang = positions.astype(jnp.float32)[..., None] * inv_freq
    cos, sin = jnp.cos(ang).astype(x.dtype), jnp.sin(ang).astype(x.dtype)
    c_act = jax.nn.silu(c)
    for l in range(DEPTH):
        mod = c_act @ w_mod[l] + b_mod[l]
        shift, scale, gate = jnp.split(mod[:, None, :], 3, axis=-1)
        h = rms_norm(x, g_pre[l]) * (1.0 + scale) + shift
        if l % 2 == 0:
            e = l // 2
            (gq, gk, gv, ga_f, ga_b, gz, cq, ckv, kr, mz) = _split(h @ w_in_e[e], EVEN_SPLITS)
            o_a = gla_branch(gq, gk, gv, ga_f, ga_b, gz, gla_w_gate_f[e], gla_b_gate_f[e],
                             gla_w_gate_b[e], gla_b_gate_b[e], gla_g_norm[e])
            o_b = mla_branch(cq, ckv, kr, mz, mla_g_q[e], mla_w_uq[e], mla_g_kv[e], mla_w_ukv[e], cos, sin)
            y = jnp.concatenate([o_a, o_b], axis=-1) @ w_out_e[e]
        else:
            o = l // 2
            y = sgmlp_branch(h @ w_in_o[o], sg_g_norm[o], sg_b_norm[o], sg_w_s[o], sg_b_s[o]) @ w_out_o[o]
        x = x + gate * rms_norm(y, g_post[l])
    return x


_drawn_inputs = setup_inputs


def setup_inputs(seed=0):
    import zlib

    import numpy as np

    out = dict(_drawn_inputs(seed))
    spreads = {}
    factors = {'g_pre': 3.381,
     'g_post': 6.079,
     'gla_g_norm': 8.0,
     'mla_g_q': 8.0,
     'mla_g_kv': 8.0,
     'sg_g_norm': 8.0,
     'sg_b_norm': 8.0,
     'sg_b_s': 2.708}
    for name, (base, spread) in spreads.items():
        noise = np.random.default_rng([zlib.crc32(name.encode()), seed]).standard_normal(out[name].shape)
        drawn = base * np.exp(spread * noise) if base else spread * noise
        out[name] = __import__('jax').numpy.asarray(drawn.astype(out[name].dtype))
    for name, factor in factors.items():
        out[name] = (out[name] * factor).astype(out[name].dtype)
    return out
```

```python
from contextlib import ExitStack

import numpy as np

import concourse.bass as bass
from concourse import mybir

F32 = mybir.dt.float32
F32R = mybir.dt.float32r
I32 = mybir.dt.int32
ALU = mybir.AluOpType
ACT = mybir.ActivationFunctionType
AX = mybir.AxisListType.X
ds = bass.ds

P = 128
D = 1024
S = 2048
KD = D // P
NT = S // P
NB = S // 512
EPS = 1e-6
TAU = 16.0
GH, DK, DV, RANK = 4, 64, 128, 16
MH, NOPE, ROPE, MV = 4, 128, 64, 128
QR, KVR = 256, 128
SGW = 2048
CT = SGW // P
SG_G = 8
LEVELS = [64, 32, 16, 8, 4, 2, 1]
NLV = len(LEVELS)
SM_SCALE = float(NOPE + ROPE) ** -0.5

O_GQ, O_GK, O_GV = 0, 256, 512
O_GA, O_GZ = 1024, 1056
O_CQ, O_CKV, O_KR, O_MZ = 1568, 1824, 1952, 2016

T_GZ, T_MZ, T_GQ, T_GK, T_GV = 0, 8, 1, 5, 9
T_GA, T_CQ, T_CKV = 16, 17, 19
O_RKR = 2 * RANK
N_TILES = 20
NPAIR = N_TILES // 2
NSILU = 8

C_ID, C_MASK = 0, P
C_INVF = C_MASK + (NLV + 1) * P
C_N = C_INVF + 3


def emit(nc, a, out, dbg=()):
    def scratch(name, shape):
        return nc.dram_tensor(name, shape, F32, kind="ExternalOutput" if name in dbg else "Internal").ap()

    projT = scratch("projT", (N_TILES, P, S))
    cumT = scratch("cumT", (4, P, S))
    mixT = scratch("mixT", (KD, P, S))
    q_all = scratch("q_all", (MH * NT, P, 2, P))
    x1 = scratch("x1", (S, D))
    gla_v = scratch("gla_v", (NT, P, GH * DV))
    gla_sb = scratch("gla_sb", (NT, P, GH * DV))
    sg_v = scratch("sg_v", (S, SGW))
    sgT = scratch("sgT", (CT, P, S))

    with ExitStack() as ctx:
        def sem(name):
            return ctx.enter_context(nc.semaphore(name))

        def at(name, off, shape, dt=F32):
            return nc.alloc_sbuf_tensor_at(name, shape, dt, offset=off)

        K = 1024
        base = (nc.sbuf_base + 63) // 64 * 64
        ident = at("ident", base, [P, P])
        ones = at("ones", base + 512, [P, P])
        mod_a = at("mod_a", base + 1024, [P, 2, KD])
        mod_b = at("mod_b", base + 1088, [P, 2, KD])
        cvec = at("cvec", base + 1152, [P, KD])
        gpre = at("gpre", base + 1184, [P, 2, KD])
        small = at("small", base + 1248, [P, 80])
        gate = at("gate", base + 1568, [P, 2, D])
        negh = at("negh", base + 1568 + 8 * K, [P, 16])
        zero = at("zero", base + 1632 + 8 * K, [P, 8])
        eps = small[:, 52:53]
        H0 = base + 1664 + 8 * K
        hTh = at("hTh", H0, [P, KD, S], F32R)
        hTl = at("hTl", H0 + 64 * K, [P, KD, S], F32R)
        X0 = H0 + 128 * K
        macc = at("macc", X0, [P, 3 * D])
        mw = at("mw", X0 + 12 * K, [P, 2, 3 * D // 2])
        xt = at("xt", X0 + 24 * K, [P, 2, 4, D])
        nj = at("nj", X0 + 56 * K, [P, D])
        nt32 = at("nt32", X0 + 60 * K, [P, 4, 512])
        wraw = at("wraw", X0 + 24 * K, [P, 2, D])
        whi = at("whi", X0 + 32 * K, [P, 2, KD, P], F32R)
        wlo = at("wlo", X0 + 40 * K, [P, 2, KD, P], F32R)
        pev = at("pev", X0 + 48 * K, [P, 2, S])

        PS = ctx.enter_context(nc.psum_tensor("PS", [P, 8, 512], F32))

        s_const = sem("s_const")
        s_set = sem("s_set")
        s_csl = sem("s_csl")

        def const_load(sp):
            sp.dma_start(cvec[:, :], a["cvec"]).then_inc(s_const, 16)
            sp.dma_start(ident[:, :], a["cst"][:, C_ID:C_ID + P]).then_inc(s_const, 16)
            sp.dma_start(gpre[:, :, :], a["gpre"]).then_inc(s_const, 16)

        def const_pool(pool):
            pool.memset(ones[:, :], 1.0).then_inc(s_set, 1)
            pool.memset(negh[:, :], -0.5).then_inc(s_set, 1)
            pool.memset(zero[:, :], 0.0).then_inc(s_set, 1)
            pool.memset(eps, EPS).then_inc(s_set, 1)

        def const_act(act):
            act.wait_ge(s_const, 48)
            act.activation(cvec[:, :], cvec[:, :], ACT.Silu).then_inc(s_csl, 1)

        s_gp = sem("s_gp")
        s_mw = [sem("s_mw0"), sem("s_mw1")]
        s_mz = sem("s_mz")
        s_macc = sem("s_macc")
        s_mps = sem("s_mps")
        s_modr = sem("s_modr")
        s_mod = sem("s_mod")

        def mod_rows(sp, l):
            sp.dma_start(gate[:, l, :], a["gpost"][l:l + 1, :].broadcast_to([P, D])).then_inc(s_gp, 16)
            sp.wait_ge(s_mz, l + 1)
            sp.dma_start(macc[0:1, :], a["bmod"][l:l + 1, :]).then_inc(s_gp, 16)

        def mod_slice(sp, l, k):
            for half in range(2):
                if l or k:
                    sp.wait_ge(s_macc, 2 * KD * l + 2 * k + half - 1)
                sp.dma_start(mw[:, half, :], a["wmod"][l:l + 1, ds(k * P, P), half * 1536:(half + 1) * 1536]
                             .rearrange("a p f -> (a p) f")).then_inc(s_mw[half], 16)

        def mod_start(dve, l):
            if l:
                dve.wait_ge(s_mps, l)
            dve.memset(macc[:, :], 0.0).then_inc(s_mz, 1)

        def mod_sum(dve, l, k):
            for half in range(2):
                dve.wait_ge(s_mw[half], (KD * l + k + 1) * 16)
                if l or k:
                    dve.wait_ge(s_macc, 2 * KD * l + 2 * k + half - 1)
                h = slice(half * 1536, (half + 1) * 1536)
                dve.scalar_tensor_tensor(macc[:, h], mw[:, half, :], cvec[:, ds(k, 1)], macc[:, h],
                                         ALU.mult, ALU.add).then_inc(s_macc, 1)

        def mod_pe(pe, l):
            pe.wait_ge(s_macc, 2 * KD * (l + 1))
            pe.wait_ge(s_set, 1)
            for j in range(6):
                mm = pe.matmul(PS[:, j, :], ones[:, :], macc[:, j * 512:(j + 1) * 512], start=True, stop=True)
            mm.then_inc(s_mps, 1)

        def mod_end(dve, l):
            dve.wait_ge(s_mps, l + 1)
            tmp = mw[:, 0, 0:512].rearrange("p (k i) -> p k i", k=4)
            col = small[:, 16 * l:16 * l + 16]
            for j in range(4):
                if l or j:
                    dve.wait_ge(s_modr, 8 * l + 2 * j)
                dve.tensor_tensor(tmp, PS[:, j, :].rearrange("p (k i) -> p k i", k=4),
                                  ident[:, :].unsqueeze(1).broadcast_to([P, 4, P]), ALU.mult).then_inc(s_modr, 1)
                dve.wait_ge(s_modr, 8 * l + 2 * j + 1)
                dve.tensor_reduce(col[:, 4 * j:4 * j + 4], tmp, AX, ALU.add).then_inc(s_modr, 1)
            dve.wait_ge(s_modr, 8 * l + 8)
            dve.scalar_tensor_tensor(mod_a[:, l, :], col[:, 8:16], 1.0, gpre[:, l, :], ALU.add, ALU.mult
                                     ).then_inc(s_mod, 1)
            dve.tensor_copy(mod_b[:, l, :], col[:, 0:8]).then_inc(s_mod, 1)
            for j in range(2):
                g = gate[:, l, j * 512:(j + 1) * 512]
                dve.tensor_tensor(g, PS[:, 4 + j, :], g, ALU.mult).then_inc(s_mod, 1)

        s_x = [sem("s_x0"), sem("s_x1")]
        s_sq = sem("s_sq")
        s_rs = sem("s_rs")
        s_xn = sem("s_xn")
        s_tp = sem("s_tp")
        s_hh = sem("s_hh")
        s_h32 = sem("s_h32")
        s_hl = sem("s_hl")

        def norm_load(sp, l, groups):
            src = a["x"] if l == 0 else x1
            for g in groups:
                q = g % 4
                if g >= 2:
                    sp.wait_ge(s_tp, 8 * (g - 1))
                if l:
                    for u in range(2):
                        sp.wait_ge(s_ost[u], 32 * (q + 1))
                sp.dma_start(xt[:, g % 2, :, :], src[q * 512:(q + 1) * 512, :].rearrange("(t p) d -> p t d", p=P)
                             ).then_inc(s_x[g % 2], 16)

        def norm_act_front(act, g):
            act.wait_ge(s_x[g % 2], 16 * (g // 2 + 1))
            for t in range(4):
                n = 4 * g + t
                if n:
                    act.wait_ge(s_sq, n)
                c = 32 + 4 * (g % 2) + t
                act.activation(nj[:, :], xt[:, g % 2, t, :], ACT.Square, accum_out=small[:, c:c + 1]).then_inc(s_sq, 1)

        def norm_act(act, l):
            for g in range(4 * l, 4 * l + 4):
                if g % 4 < 3:
                    norm_act_front(act, g + 1)
                for k in range(KD):
                    m = 8 * g + k
                    act.wait_ge(s_tp, m + 1)
                    if m == 32 * l:
                        act.wait_ge(s_mod, 4 * l + 2)
                    if m >= 4:
                        act.wait_ge(s_hl, m - 3)
                    act.activation(nt32[:, m % 4, :], PS[:, k, :], ACT.Identity, bias=mod_b[:, l, k:k + 1],
                                   scale=mod_a[:, l, k:k + 1]).then_inc(s_h32, 1)

        def h_block(m):
            return (m % 8, slice((m // 8 % 4) * 512, (m // 8 % 4 + 1) * 512))

        def norm_pool_front(pool, g):
            c = slice(32 + 4 * (g % 2), 36 + 4 * (g % 2))
            r = slice(40 + 4 * (g % 2), 44 + 4 * (g % 2))
            pool.wait_ge(s_sq, 4 * (g + 1))
            if g >= 2:
                pool.wait_ge(s_xn, 4 * (g - 1))
            pool.tensor_scalar(small[:, r], small[:, c], 1.0 / D, EPS, ALU.mult, ALU.add).then_inc(s_rs, 1)
            pool.wait_ge(s_rs, 2 * g + 1)
            pool.tensor_tensor(small[:, r], small[:, r], negh[:, 0:4], ALU.pow).then_inc(s_rs, 1)

        def norm_pool(pool, l):
            for g in range(4 * l, 4 * l + 4):
                if g % 4 < 3:
                    norm_pool_front(pool, g + 1)
                for m in range(8 * g, 8 * g + 8):
                    k, b = h_block(m)
                    pool.wait_ge(s_h32, m + 1)
                    pool.tensor_tensor(hTh[:, k, b], nt32[:, m % 4, :], zero[:, 0:1].broadcast_to([P, 512]), ALU.add
                                       ).then_inc(s_hh, 1)

        def norm_dve_front(dve, g):
            dve.wait_ge(s_rs, 2 * g + 2)
            for t in range(4):
                r = 40 + 4 * (g % 2) + t
                dve.tensor_scalar(xt[:, g % 2, t, :], xt[:, g % 2, t, :], small[:, r:r + 1], None, ALU.mult
                                  ).then_inc(s_xn, 1)

        def norm_dve(dve, l):
            if l:
                for u in range(2):
                    dve.wait_ge(s_ost[u], 8 * NT)
            for g in range(4 * l, 4 * l + 4):
                if g % 4 < 3:
                    norm_dve_front(dve, g + 1)
                for m in range(8 * g, 8 * g + 8):
                    k, b = h_block(m)
                    dve.wait_ge(s_hh, m + 1)
                    dve.tensor_tensor(hTl[:, k, b], nt32[:, m % 4, :], hTh[:, k, b].bitcast(F32), ALU.subtract
                                      ).then_inc(s_hl, 1)

        def norm_pe(pe, l):
            pe.wait_ge(s_const, 48)
            for g in range(4 * l, 4 * l + 4):
                pe.wait_ge(s_xn, 4 * (g + 1))
                for k in range(KD):
                    m = 8 * g + k
                    if g % 4:
                        pe.wait_ge(s_h32, m - 7)
                    elif l == 0 and k == 0:
                        pe.wait_ge(s_mod, 4)
                    elif l and k in (0, 4):
                        pe.wait_ge(s_oz, 2 * NT + k // 2 + 2)
                    for t in range(4):
                        mm = pe.transpose(PS[:, k, t * P:(t + 1) * P], xt[:, g % 2, t, k * P:(k + 1) * P], ident[:, :])
                    mm.then_inc(s_tp, 1)

        s_wr = [sem("s_wr0"), sem("s_wr1")]
        s_whi = sem("s_whi")
        s_wlo = sem("s_wlo")
        s_pb = sem("s_pb")
        s_pev = [sem("s_pev0"), sem("s_pev1")]
        s_pst = [sem("s_pst0"), sem("s_pst1")]

        def tile_load(sp, name, g, i, s):
            sp.wait_ge(s_wlo, g + 1)
            sp.dma_start(wraw[:, s, :], a[name][ds(2 * i + s, 1), :, :].rearrange("a p f -> p (a f)")
                         ).then_inc(s_wr[s], 16)

        def tile_split(pool, g, h, s):
            hi = whi[:, s, :, :].rearrange("p k c -> p (k c)")
            lo = wlo[:, s, :, :].rearrange("p k c -> p (k c)")
            pool.wait_ge(s_wr[s], (h + 1) * 16)
            pool.wait_ge(s_pb, 4 * g + 4)
            pool.tensor_tensor(hi, wraw[:, s, :], zero[:, 0:1].broadcast_to([P, D]), ALU.add).then_inc(s_whi, 1)
            pool.wait_ge(s_whi, g + 1)
            pool.tensor_tensor(lo, wraw[:, s, :], hi.bitcast(F32), ALU.subtract).then_inc(s_wlo, 1)

        def tile_block(pe, s, tb, bank):
            b = slice(tb * 512, (tb + 1) * 512)
            for k in range(KD):
                pe.matmul(PS[:, bank, :], whi[:, s, k, :], hTh[:, k, b], start=(k == 0), stop=False)
                pe.matmul(PS[:, bank, :], whi[:, s, k, :], hTl[:, k, b], start=False, stop=False)
                mm = pe.matmul(PS[:, bank, :], wlo[:, s, k, :], hTh[:, k, b], start=False, stop=(k == KD - 1))
            mm.then_inc(s_pb, 1)

        def proj_sp(sp):
            def store(i):
                sp.wait_ge(s_pev[1], 4 * i + 8)
                sp.dma_start(projT[ds(2 * i + 1, 1), :, :].rearrange("a p f -> p (a f)"), pev[:, 1, :]
                             ).then_inc(s_pst[1], 16)
            sp.wait_ge(s_tp, 32)
            sp.wait_ge(s_sq, 16)
            sp.wait_ge(s_hl, 32)
            for s in range(2):
                tile_load(sp, "wT", s, 0, s)
            mod_rows(sp, 1)
            with sp.Fori(0, NSILU) as i:
                for s in range(2):
                    tile_load(sp, "wT", 2 * i + 2 + s, i + 1, s)
                store(i)
                mod_slice(sp, 1, i)
            with sp.Fori(NSILU, NPAIR - 1) as i:
                for s in range(2):
                    tile_load(sp, "wT", 2 * i + 2 + s, i + 1, s)
                store(i)
            store(NPAIR - 1)

        def proj_pool(pool):
            pool.wait_ge(s_hl, 32)
            with pool.Fori(0, NPAIR) as i:
                for s in range(2):
                    tile_split(pool, 2 * i + s, i, s)

        def proj_pe(pe):
            pe.wait_ge(s_hl, 32)
            pe.wait_ge(s_hh, 32)
            with pe.Fori(0, NPAIR) as i:
                for s in range(2):
                    pe.wait_ge(s_wlo, 2 * i + s + 3)
                    for tb in range(NB):
                        pe.wait_ge(s_pev[s], 4 * i + tb + 1)
                        tile_block(pe, s, tb, 4 * s + tb)

        def proj_act(act):
            def tile(i, func):
                act.wait_ge(s_pst[0], 16 * i)
                for tb in range(NB):
                    act.wait_ge(s_pb, 8 * i + tb + 9)
                    act.activation(pev[:, 0, tb * 512:(tb + 1) * 512], PS[:, tb, :], func).then_inc(s_pev[0], 1)
                act.wait_ge(s_pev[0], 4 * i + 8)
                act.dma_start(projT[ds(2 * i, 1), :, :].rearrange("a p f -> p (a f)"), pev[:, 0, :]
                              ).then_inc(s_pst[0], 16)
            with act.Fori(0, NSILU) as i:
                tile(i, ACT.Silu)
            with act.Fori(NSILU, NPAIR) as i:
                tile(i, ACT.Copy)

        def proj_dve(dve):
            def tile(i):
                dve.wait_ge(s_pst[1], 16 * i)
                for tb in range(NB):
                    dve.wait_ge(s_pb, 8 * i + 4 + tb + 9)
                    dve.tensor_copy(pev[:, 1, tb * 512:(tb + 1) * 512], PS[:, 4 + tb, :]).then_inc(s_pev[1], 1)
            mod_start(dve, 1)
            dve.wait_ge(s_gp, 64)
            with dve.Fori(0, NSILU) as i:
                tile(i)
                mod_sum(dve, 1, i)
            with dve.Fori(NSILU, NPAIR) as i:
                tile(i)

        G0 = H0
        gmask = at("gmask", G0, [P, (NLV + 1) * P])
        gw2 = at("gw2", G0 + 4 * K, [2 * RANK, 4 * P])
        gb2 = at("gb2", G0 + 6 * K, [P, 4])
        ggn = at("ggn", G0 + 6 * K + 32, [P, 1])
        gtot = at("gtot", G0 + 6 * K + 64, [P, 4, NT])
        gtots = at("gtots", G0 + 6 * K + 320, [P, 4, NT])
        G1 = G0 + 7 * K
        ga = at("ga", G1, [2 * RANK, S])
        greset = at("greset", G1 + 8 * K, [P, S])
        gt1 = at("gt1", G1 + 16 * K, [P, S])
        gt2 = at("gt2", G1 + 24 * K, [P, S])
        gcum = at("gcum", G1 + 32 * K, [P, S])
        kt = at("kt", G1, [P, 2, 2, P])
        et = at("et", G1 + 2 * K, [P, 2, 2, P])
        vt = at("vt", G1 + 4 * K, [P, 2, GH, P])
        vv = at("vv", G1 + 8 * K, [P, 2, GH * DV])
        xe = at("xe", G1 + 12 * K, [P, 2, 2, P])
        kb2 = at("kb2", G1 + 14 * K, [P, 2, 2, P])
        kfT = at("kfT", G1 + 16 * K, [P, 2 * P])
        st = at("st", G1 + 17 * K, [P, 2, GH, DV])
        G2 = G1 + 40 * K
        m_k = at("m_k", G2, [P, 4, 2, P])
        m_q = at("m_q", G2 + 4 * K, [P, 4, 2, P])
        m_f = at("m_f", G2 + 8 * K, [P, 4, 2, P])
        m_e = at("m_e", G2 + 12 * K, [P, 4, 2, P])
        m_v = at("m_v", G2 + 16 * K, [P, 4, GH * DV])
        m_s = at("m_s", G2 + 24 * K, [P, 4, GH, DV])
        m_z = at("m_z", G2 + 32 * K, [P, 4, GH, P])
        m_x = at("m_x", G2 + 40 * K, [P, 2, 3, 2, P])
        m_kf = at("m_kf", G2 + 46 * K, [P, 2, 2, P])
        m_kT = at("m_kT", G2 + 48 * K, [P, 2, 2 * P])
        m_st = at("m_st", G2 + 50 * K, [P, 2, GH, DV])
        xa = at("xa", G2 + 54 * K, [P, 2, 2, NLV, 2, P])
        tmp_l = at("tmp_l", G2 + 82 * K, [P, 2, NLV + 1, P])
        attT = at("attT", G2 + 90 * K, [P, 2, GH, P])
        qf = at("qf", G2 + 94 * K, [P, 2, 2, 2, P])
        osq = at("osq", G2 + 98 * K, [P, GH * P])
        orr = at("orr", G2 + 100 * K, [P, GH * P])
        og = at("og", G2 + 102 * K, [P, 2, GH, P])
        ocol = at("ocol", G2 + 106 * K, [P, 2, GH])

        s_gc = sem("s_gc")
        s_gm = sem("s_gm")
        s_gl = sem("s_gl")
        s_ga = sem("s_ga")
        s_gmin = sem("s_gmin")
        s_gcum = sem("s_gcum")
        s_gtot = sem("s_gtot")
        s_gst = sem("s_gst")

        def gates_sp(sp):
            sp.wait_ge(s_pst[0], 16 * NPAIR)
            sp.wait_ge(s_pst[1], 16 * NPAIR)
            sp.wait_ge(s_pb, 8 + 4 * N_TILES)
            for dst, src in ((ga[:, :], projT[T_GA, 0:2 * RANK, :]), (gw2[:, :], a["w2"]), (gb2[:, :], a["b2"]),
                             (ggn[:, :], a["gnorm"]), (gmask[:, :], a["cst"][:, C_MASK:C_INVF])):
                sp.dma_start(dst, src).then_inc(s_gc, 16)
            for n in range(4):
                sp.wait_ge(s_gcum, (1, 2, 3, 5)[n])
                sp.dma_start(cumT[n], gcum[:, :]).then_inc(s_gst, 16)

        def gates_pe(pe):
            pe.wait_ge(s_gc, 80)
            pe.wait_ge(s_mod, 8)
            for n in range(4):
                for tb in range(NB):
                    if n >= 2:
                        pe.wait_ge(s_gmin, 5 * (n - 2) + tb + 1)
                    pe.matmul(PS[:, 4 * (n % 2) + tb, :], gw2[:, n * P:(n + 1) * P], ga[:, tb * 512:(tb + 1) * 512],
                              start=True, stop=True).then_inc(s_gl, 1)

        def gates_act(act):
            act.wait_ge(s_gc, 80)
            act.wait_ge(s_gm, 3)
            for n in range(4):
                if n:
                    act.wait_ge(s_gmin, 5 * n)
                for tb in range(NB):
                    act.wait_ge(s_gl, 4 * n + tb + 1)
                    act.activation(gt1[:, tb * 512:(tb + 1) * 512], PS[:, 4 * (n % 2) + tb, :], ACT.Abs,
                                   bias=gb2[:, n:n + 1]).then_inc(s_ga, 1)
                act.wait_ge(s_ga, 6 * n + 4)
                act.activation(gt1[:, :], gt1[:, :], ACT.Exp, scale=-1.0).then_inc(s_ga, 1)
                act.wait_ge(s_ga, 6 * n + 5)
                act.activation(gt1[:, :], gt1[:, :], ACT.Ln, bias=1.0).then_inc(s_ga, 1)
            act.wait_ge(s_gtot, 4)
            act.activation(gtot[:, :, :], gtots[:, :, :], ACT.Exp).then_inc(s_gtot, 1)

        def gates_dve(dve):
            dve.wait_ge(s_pb, 8 + 4 * N_TILES)
            dve.memset(greset[:, :], 1.0).then_inc(s_gm, 1)
            dve.wait_ge(s_gm, 1)
            dve.memset(greset[:, 0:S:P], 0.0).then_inc(s_gm, 1)
            dve.memset(gcum[:, 0:1], 0.0).then_inc(s_gm, 1)
            for n in range(4):
                for tb in range(NB):
                    dve.wait_ge(s_ga, 6 * n + tb + 1)
                    if n:
                        dve.wait_ge(s_gtot, n)
                    dve.tensor_scalar(gt2[:, tb * 512:(tb + 1) * 512], PS[:, 4 * (n % 2) + tb, :], gb2[:, n:n + 1], 0.0,
                                      ALU.add, ALU.min).then_inc(s_gmin, 1)
                dve.wait_ge(s_gmin, 5 * n + 4)
                dve.wait_ge(s_ga, 6 * n + 6)
                dve.tensor_tensor(gt2[:, :], gt2[:, :], gt1[:, :], ALU.subtract).then_inc(s_gmin, 1)
                dve.wait_ge(s_gmin, 5 * n + 5)
                dve.wait_ge(s_gm, 3)
                if n:
                    dve.wait_ge(s_gst, 16 * n)
                if n == 2:
                    dve.memset(gcum[:, 0:1], 0.0).then_inc(s_gm, 1)
                    dve.wait_ge(s_gm, 4)
                if n < 2:
                    dve.tensor_tensor_scan(gcum[:, :], greset[:, :], gt2[:, :], 0.0, ALU.mult, ALU.add
                                           ).then_inc(s_gcum, 1)
                    dve.wait_ge(s_gcum, n + 1)
                    dve.tensor_scalar(gtots[:, n, :], gcum[:, P - 1:S:P], 1.0 / TAU, None, ALU.mult).then_inc(s_gtot, 1)
                else:
                    dve.tensor_tensor_scan(gcum[:, 1:S], gt2[:, 0:S - 1], greset[:, 1:S], 0.0, ALU.add, ALU.mult
                                           ).then_inc(s_gcum, 1)
                    dve.wait_ge(s_gcum, 2 * n - 1)
                    dve.tensor_tensor(gtots[:, n, :], gcum[:, P - 1:S:P], gt2[:, P - 1:S:P], ALU.add).then_inc(s_gcum, 1)
                    dve.wait_ge(s_gcum, 2 * n)
                    dve.tensor_scalar(gtots[:, n, :], gtots[:, n, :], 1.0 / TAU, None, ALU.mult).then_inc(s_gtot, 1)

        s_bl = [sem("s_bl0"), sem("s_bl1")]
        s_bx = sem("s_bx")
        s_bk = sem("s_bk")
        s_bt = sem("s_bt")
        s_bkT = sem("s_bkT")
        s_bv = sem("s_bv")
        s_bc = sem("s_bc")
        s_bs = sem("s_bs")
        s_bvs = [sem("s_bvs0"), sem("s_bvs1")]
        s_bss = [sem("s_bss0"), sem("s_bss1")]

        def back_sp(sp):
            sp.wait_ge(s_gst, 64)
            sp.wait_ge(s_gtot, 5)
            with sp.Fori(0, NT // 2) as i:
                for u in range(2):
                    n = 2 * i + u
                    tok = ds(i * (-2 * P) + (NT - 1 - u) * P, P)
                    sp.wait_ge(s_bk, n + 1)
                    sp.wait_ge(s_bt, n + 1)
                    sp.dma_start(kt[:, u, :, :], projT[T_GK:T_GK + 4:2, :, tok].rearrange("h p c -> p h c")).then_inc(s_bl[u], 16)
                    sp.dma_start(et[:, u, :, :], cumT[2:4, :, tok].rearrange("h p c -> p h c")).then_inc(s_bl[u], 16)
                    sp.dma_start(vt[:, u, :, :], projT[T_GV:T_GV + 8:2, :, tok].rearrange("h p c -> p h c")).then_inc(s_bl[u], 16)

        def back_act(act):
            with act.Fori(0, NT // 2) as i:
                for u in range(2):
                    n = 2 * i + u
                    act.wait_ge(s_bl[u], 48 * i + 48)
                    act.wait_ge(s_bk, n + 1)
                    act.activation(xe[:, u, :, :], et[:, u, :, :], ACT.Exp, scale=1.0 / TAU).then_inc(s_bx, 1)
                    act.wait_ge(s_bt, n + 3)
                    act.wait_ge(s_bvs[u], 16 * i)
                    act.activation(vv[:, u, :], PS[:, 3 * u + 1, :], ACT.Copy).then_inc(s_bv, 1)
                    act.wait_ge(s_bv, n + 1)
                    act.dma_start(gla_v[ds(i * -2 + (NT - 1 - u), 1), :, :].rearrange("a p f -> p (a f)"), vv[:, u, :]
                                  ).then_inc(s_bvs[u], 16)
                    act.wait_ge(s_bs, 4 * n + 4)
                    act.dma_start(gla_sb[ds(i * -2 + (NT - 1 - u), 1), :, :].rearrange("a p f -> p (a f)"),
                                  st[:, u, :, :].rearrange("p h v -> p (h v)")).then_inc(s_bss[u], 16)

        def state_step(dve, old, new, bank, pair0, tok, done):
            for h in range(GH):
                r = slice(DK * (h % 2), DK * (h % 2) + DK)
                c = (h // 2) * 2 * DV + (h % 2) * DV
                dve.scalar_tensor_tensor(new[r, h, :], old[r, h, :], gtot[r, pair0 + h // 2, tok], PS[r, bank, c:c + DV],
                                         ALU.mult, ALU.add).then_inc(done, 1)

        def back_dve(dve):
            dve.wait_ge(s_gst, 64)
            dve.wait_ge(s_gtot, 4)
            dve.memset(st[:, :, :, :], 0.0).then_inc(s_gm, 1)
            dve.wait_ge(s_gm, 5)
            dve.sem_inc(s_bs, 4)
            with dve.Fori(0, NT // 2) as i:
                for u in range(2):
                    n = 2 * i + u
                    dve.wait_ge(s_bx, n + 1)
                    dve.wait_ge(s_bt, n + 1)
                    dve.tensor_tensor(kb2[:, u, :, :], kt[:, u, :, :], xe[:, u, :, :], ALU.mult).then_inc(s_bk, 1)
                    dve.wait_ge(s_bt, n + 3)
                    dve.wait_ge(s_bc, n)
                    dve.tensor_copy(kfT[:, :], PS[:, 3 * u, 0:2 * P]).then_inc(s_bkT, 1)
                    dve.wait_ge(s_bc, n + 1)
                    dve.wait_ge(s_bss[1 - u], 16 * (i + u))
                    dve.wait_ge(s_bs, 4 * n + 4)
                    state_step(dve, st[:, u], st[:, 1 - u], 3 * u + 2, 2, ds(i * -2 + (NT - 1 - u), 1), s_bs)

        def back_pe(pe):
            pe.wait_ge(s_gmin, 20)
            with pe.Fori(0, NT // 2) as i:
                for u in range(2):
                    n = 2 * i + u
                    pe.wait_ge(s_bl[u], 48 * i + 48)
                    pe.wait_ge(s_bk, n + 3)
                    pe.wait_ge(s_bkT, n)
                    pe.wait_ge(s_bv, n)
                    for p in range(2):
                        pe.transpose(PS[:, 3 * u, p * P:(p + 1) * P], kb2[:, u, p, :], ident[:, :])
                    for h in range(GH):
                        mm = pe.transpose(PS[:, 3 * u + 1, h * P:(h + 1) * P], vt[:, u, h, :], ident[:, :])
                    mm.then_inc(s_bt, 1)
                    pe.wait_ge(s_bkT, n + 1)
                    pe.wait_ge(s_bv, n + 1)
                    pe.wait_ge(s_bs, 4 * n + 4)
                    for p in range(2):
                        mm = pe.matmul(PS[:, 3 * u + 2, p * 2 * DV:(p + 1) * 2 * DV], kfT[:, p * P:(p + 1) * P],
                                       vv[:, u, p * 2 * DV:(p + 1) * 2 * DV], start=True, stop=True)
                    mm.then_inc(s_bc, 1)

        s_ml = [sem("s_ml%d" % s) for s in range(4)]
        s_mf = sem("s_mf")
        s_me = sem("s_me")
        s_mx = sem("s_mx")
        s_mq = sem("s_mq")
        s_mk = sem("s_mk")
        s_msx = sem("s_msx")
        s_mqf = sem("s_mqf")
        s_mkf = sem("s_mkf")
        s_mkt = sem("s_mkt")
        s_mkT = sem("s_mkT")
        s_mc = sem("s_mc")
        s_ms = sem("s_ms")
        s_mlv = sem("s_mlv")
        s_mm = sem("s_mm")
        s_ma = sem("s_ma")
        s_mo = sem("s_mo")
        s_mos = sem("s_mos")
        s_mss = sem("s_mss")
        s_mrr = sem("s_mrr")
        s_mrb = sem("s_mrb")
        s_mor = sem("s_mor")
        s_mog = sem("s_mog")
        s_mgz = sem("s_mgz")
        s_mst = [sem("s_mst0"), sem("s_mst1")]

        def near(tile, d):
            t, q, s = tile
            return (t + d, q + (s + d) // 4, (s + d) % 4)

        def main_tiles(eng, step):
            with eng.Fori(0, NT // 4 - 1) as i:
                for u in range(1, 5):
                    step((i * 4 + u, i + u // 4, u % 4), False)
            for t in range(NT - 3, NT):
                step((t, t // 4, t % 4), t == NT - 1)

        def halves(tile, s):
            v = tile.rearrange("p h (b c s) -> p h b c s", c=2, s=s)
            n = P // (2 * s)
            return (v[:, :, :, 0, :], v[:, :, :, 1, :], v[:, :, :, 0, s - 1:s].broadcast_to([P, 2, n, s]),
                    v[:, :, :, 1, 0:1].broadcast_to([P, 2, n, s]))

        def main_sp(sp):
            def load(tile, parts=(0, 1)):
                t, q, s = tile
                tok = ds(t * P, P)
                if 0 in parts:
                    for dst, src in ((m_q, projT[T_GQ:T_GQ + 4:2, :, tok]), (m_k, projT[T_GK:T_GK + 4:2, :, tok]),
                                     (m_f, cumT[0:2, :, tok]), (m_e, cumT[2:4, :, tok]), (m_z, projT[T_GZ:T_GZ + 8:2, :, tok])):
                        sp.dma_start(dst[:, s, :, :], src.rearrange("h p c -> p h c")).then_inc(s_ml[s], 16)
                if 1 in parts:
                    sp.dma_start(m_v[:, s, :], gla_v[ds(t, 1), :, :].rearrange("a p f -> p (a f)")).then_inc(s_ml[s], 16)
                    sp.dma_start(m_s[:, s, :, :].rearrange("p h v -> p (h v)"),
                                 gla_sb[ds(t, 1), :, :].rearrange("a p f -> p (a f)")).then_inc(s_ml[s], 16)

            def store(tile):
                t, q, s = tile
                sp.wait_ge(s_mgz, t + 1)
                sp.dma_start(mixT[0:GH, :, ds(t * P, P)].rearrange("h p c -> p h c"), og[:, s % 2, :, :]
                             ).then_inc(s_mst[s % 2], 16)

            for t in range(4):
                load((t, 0, t), (0,))
            for q in range(2):
                sp.wait_ge(s_bvs[q], 16 * (NT // 2))
                sp.wait_ge(s_bss[q], 16 * (NT // 2))
            for t in range(4):
                load((t, 0, t), (1,))
            sp.wait_ge(s_bc, NT)
            sp.wait_ge(s_bs, 4 * NT + 4)
            latents_sp(sp)
            with sp.Fori(0, NT // 4 - 1) as i:
                for u in range(4):
                    tile = (i * 4 + u, i, u)
                    store(tile)
                    load(near(tile, 4))
            for t in range(NT - 4, NT):
                store((t, t // 4, t % 4))

        def main_act(act):
            def factors(tile):
                t, q, s = tile
                p = s % 2
                act.wait_ge(s_ml[s], q * 112 + 112)
                act.wait_ge(s_mqf, t * 2 + 2)
                act.wait_ge(s_mkf, t + 1)
                act.activation(m_x[:, p, 0, :, :], m_f[:, s, :, :], ACT.Exp, scale=1.0 / TAU).then_inc(s_msx, 1)
                for h in range(2):
                    act.activation(m_x[:, p, 1, h, :], m_e[:, s, h, :], ACT.Exp, bias=gtots[:, 2 + h, ds(t, 1)],
                                   scale=-1.0 / TAU).then_inc(s_msx, 1)
                    act.activation(m_x[:, p, 2, h, :], m_f[:, s, h, :], ACT.Exp, bias=gtots[:, h, ds(t, 1)],
                                   scale=-1.0 / TAU).then_inc(s_msx, 1)

            def decays(tile):
                t, q, s = tile
                act.wait_ge(s_mf, t * (2 * NLV) + 2 * NLV)
                act.wait_ge(s_me, t * (2 * NLV) + 2 * NLV)
                act.activation(xa[:, s % 2], xa[:, s % 2], ACT.Exp, scale=1.0 / TAU).then_inc(s_mx, 1)

            def turned(tile):
                t, q, s = tile
                act.wait_ge(s_mkt, t + 3)
                act.wait_ge(s_mc, t + 1)
                act.activation(m_kT[:, s % 2, :], PS[:, 6, 0:2 * P], ACT.Copy).then_inc(s_mkT, 1)

            def squares(tile):
                t, q, s = tile
                act.wait_ge(s_mo, t + 3)
                act.wait_ge(s_mss, t)
                act.activation(osq[:, :], PS[:, 4, :], ACT.Square).then_inc(s_mos, 1)

            def rstd(tile):
                t, q, s = tile
                act.wait_ge(s_mrb, t + 3)
                act.wait_ge(s_mog, t + 2)
                act.activation(orr[:, :], PS[:, 7, :], ACT.Copy).then_inc(s_mor, 1)

            def step(tile, last):
                turned(tile)
                if not last:
                    factors(near(tile, 1))
                rstd(near(tile, -1))
                if not last:
                    decays(near(tile, 1))
                squares(tile)
            factors((0, 0, 0))
            decays((0, 0, 0))
            turned((0, 0, 0))
            factors((1, 0, 1))
            decays((1, 0, 1))
            squares((0, 0, 0))
            main_tiles(act, step)
            rstd((NT - 1, NT // 4 - 1, 3))

        def main_dve(dve):
            dve.memset(m_st[:, 0, :, :], 0.0).then_inc(s_gm, 1)
            dve.memset(m_st[:, 1, :, :], 0.0).then_inc(s_gm, 1)
            dve.tensor_scalar(ggn[:, :], ggn[:, :], float(DK) ** -0.5, None, ALU.mult).then_inc(s_gm, 1)
            dve.wait_ge(s_gm, 8)

            def distances(tile):
                t, q, s = tile
                dve.wait_ge(s_ml[s], q * 112 + 112)
                dve.wait_ge(s_mlv, t * 4 + 4)
                for l, w in enumerate(LEVELS):
                    left, right, mid, _ = halves(m_f[:, s, :, :], w)
                    ql, qr, _, _ = halves(xa[:, s % 2, 0, l, :, :], w)
                    kl, _, _, _ = halves(xa[:, s % 2, 1, l, :, :], w)
                    dve.tensor_tensor(qr, right, mid, ALU.subtract).then_inc(s_mf, 1)
                    dve.tensor_tensor(kl, mid, left, ALU.subtract).then_inc(s_mf, 1)

            def q_states(tile):
                t, q, s = tile
                dve.wait_ge(s_msx, t * 5 + 5)
                dve.wait_ge(s_mo, t + 1)
                for d in range(2):
                    dve.tensor_tensor(qf[:, s % 2, d, :, :], m_q[:, s, :, :], m_x[:, s % 2, d, :, :], ALU.mult
                                      ).then_inc(s_mqf, 1)

            def q_levels(tile):
                t, q, s = tile
                x = xa[:, s % 2, 0, :, :, :].rearrange("p l h c -> p l (h c)")
                dve.wait_ge(s_mx, t + 1)
                dve.tensor_tensor(x, x, m_q[:, s, :, :].rearrange("p h c -> p (h c)").unsqueeze(1)
                                  .broadcast_to([P, NLV, 2 * P]), ALU.mult).then_inc(s_mq, 1)

            def matrix(tile, h):
                t, q, s = tile
                b = 2 * (h % 2)
                dve.wait_ge(s_mlv, t * 4 + h + 9)
                dve.wait_ge(s_ma, t * 4 + h + 1)
                dve.tensor_tensor(tmp_l[:, h % 2, :, :].rearrange("p l c -> p (l c)"),
                                  PS[:, b:b + 2, :].rearrange("p b c -> p (b c)"), gmask[:, :], ALU.mult
                                  ).then_inc(s_mm, 1)
                dve.wait_ge(s_mm, t * 4 + h + 3)
                dve.wait_ge(s_mo, t + 1)
                dve.tensor_reduce(attT[:, s % 2, h, :], tmp_l[:, h % 2, :, :].rearrange("p l c -> p c l"), AX, ALU.add
                                  ).then_inc(s_ma, 1)

            def state(tile):
                t, q, s = tile
                dve.wait_ge(s_mc, t + 3)
                dve.wait_ge(s_mo, t + 2)
                dve.wait_ge(s_ms, t * 4 + 4)
                state_step(dve, m_st[:, s % 2], m_st[:, 1 - s % 2], 5, 0, ds(t, 1), s_ms)

            def mean(tile):
                t, q, s = tile
                dve.wait_ge(s_mss, t + 1)
                dve.wait_ge(s_mrb, t + 1)
                dve.tensor_scalar(ocol[:, s % 2, :], PS[:, 7, 0:GH], 1.0 / (DK * DV), EPS, ALU.mult, ALU.add).then_inc(s_mrr, 1)

            def normed(tile):
                t, q, s = tile
                dve.wait_ge(s_mor, t + 3)
                dve.wait_ge(s_mst[s % 2], q * 32 + (16 * (s // 2) + 16))
                dve.scalar_tensor_tensor(og[:, s % 2, :, :].rearrange("p h c -> p (h c)"), PS[:, 4, :], ggn[:, 0:1], orr[:, :],
                                         ALU.mult, ALU.mult).then_inc(s_mog, 1)

            def step(tile, last):
                if not last:
                    distances(near(tile, 1))
                mean(near(tile, -1))
                matrix(tile, 0)
                matrix(tile, 1)
                normed(near(tile, -1))
                if not last:
                    q_states(near(tile, 1))
                    q_levels(near(tile, 1))
                matrix(tile, 2)
                matrix(tile, 3)
                state(tile)
            distances((0, 0, 0))
            q_states((0, 0, 0))
            q_levels((0, 0, 0))
            distances((1, 0, 1))
            matrix((0, 0, 0), 0)
            matrix((0, 0, 0), 1)
            q_states((1, 0, 1))
            q_levels((1, 0, 1))
            matrix((0, 0, 0), 2)
            matrix((0, 0, 0), 3)
            state((0, 0, 0))
            main_tiles(dve, step)
            mean((NT - 1, NT // 4 - 1, 3))
            normed((NT - 1, NT // 4 - 1, 3))

        def main_pool(pool):
            def distances(tile, levels):
                t, q, s = tile
                pool.wait_ge(s_ml[s], q * 112 + 112)
                pool.wait_ge(s_mlv, t * 4 + 4)
                for l in levels:
                    left, right, _, mid = halves(m_e[:, s, :, :], LEVELS[l])
                    ql, _, _, _ = halves(xa[:, s % 2, 0, l, :, :], LEVELS[l])
                    _, kr, _, _ = halves(xa[:, s % 2, 1, l, :, :], LEVELS[l])
                    pool.tensor_tensor(ql, mid, left, ALU.subtract).then_inc(s_me, 1)
                    pool.tensor_tensor(kr, right, mid, ALU.subtract).then_inc(s_me, 1)

            def k_state(tile):
                t, q, s = tile
                pool.wait_ge(s_msx, t * 5 + 5)
                pool.wait_ge(s_mkt, t + 1)
                pool.tensor_tensor(m_kf[:, s % 2, :, :], m_k[:, s, :, :], m_x[:, s % 2, 2, :, :], ALU.mult).then_inc(s_mkf, 1)

            def k_levels(tile):
                t, q, s = tile
                x = xa[:, s % 2, 1, :, :, :].rearrange("p l h c -> p l (h c)")
                pool.wait_ge(s_mx, t + 1)
                pool.tensor_tensor(x, x, m_k[:, s, :, :].rearrange("p h c -> p (h c)").unsqueeze(1)
                                   .broadcast_to([P, NLV, 2 * P]), ALU.mult).then_inc(s_mk, 1)

            def rstd(tile):
                t, q, s = tile
                pool.wait_ge(s_mrr, t * 2 + 1)
                pool.tensor_tensor(ocol[:, s % 2, :], ocol[:, s % 2, :], negh[:, 0:GH], ALU.pow).then_inc(s_mrr, 1)

            def gated(tile):
                t, q, s = tile
                pool.wait_ge(s_mog, t + 3)
                pool.tensor_tensor(og[:, s % 2, :, :], og[:, s % 2, :, :], m_z[:, s, :, :], ALU.mult).then_inc(s_mgz, 1)

            def step(tile, last):
                if not last:
                    distances(near(tile, 1), range(0, 3))
                rstd(near(tile, -1))
                if not last:
                    distances(near(tile, 1), range(3, NLV))
                    k_state(near(tile, 1))
                gated(near(tile, -1))
                if not last:
                    k_levels(near(tile, 1))
            for t in range(2):
                distances((t, 0, t), range(NLV))
                k_state((t, 0, t))
                k_levels((t, 0, t))
            main_tiles(pool, step)
            rstd((NT - 1, NT // 4 - 1, 3))
            gated((NT - 1, NT // 4 - 1, 3))

        def main_pe(pe):
            pe.wait_ge(s_bs, 4 * NT + 4)
            pe.wait_ge(s_bkT, NT)
            pe.wait_ge(s_bv, NT)

            def turn(tile):
                t, q, s = tile
                pe.wait_ge(s_mkf, t + 3)
                pe.wait_ge(s_mkT, t + 2)
                for p in range(2):
                    mm = pe.transpose(PS[:, 6, p * P:(p + 1) * P], m_kf[:, s % 2, p, :], ident[:, :])
                mm.then_inc(s_mkt, 1)

            def levels(tile, h):
                t, q, s = tile
                r, p, b = slice(DK * (h % 2), DK * (h % 2) + DK), h // 2, 2 * (h % 2)
                if h == 0:
                    pe.wait_ge(s_mq, t + 1)
                    pe.wait_ge(s_mk, t + 1)
                pe.wait_ge(s_mm, t * 4 + h + 1)
                for l in range(NLV + 1):
                    kk = xa[r, s % 2, 1, l, p, :] if l < NLV else m_k[r, s, p, :]
                    qq = xa[r, s % 2, 0, l, p, :] if l < NLV else m_q[r, s, p, :]
                    mm = pe.matmul(PS[:, b + l // 4, (l % 4) * P:(l % 4 + 1) * P], kk, qq, start=True, stop=True)
                mm.then_inc(s_mlv, 1)

            def contribution(tile):
                t, q, s = tile
                pe.wait_ge(s_mkT, t + 3)
                pe.wait_ge(s_ms, t * 4 + 4)
                for p in range(2):
                    mm = pe.matmul(PS[:, 5, p * 2 * DV:(p + 1) * 2 * DV], m_kT[:, s % 2, p * P:(p + 1) * P],
                                   m_v[:, s, p * 2 * DV:(p + 1) * 2 * DV], start=True, stop=True)
                mm.then_inc(s_mc, 1)

            def outputs(tile, h):
                t, q, s = tile
                o = PS[:, 4, h * P:(h + 1) * P]
                if h == 0:
                    pe.wait_ge(s_mog, t + 2)
                    pe.wait_ge(s_mqf, t * 2 + 6)
                pe.wait_ge(s_ma, t * 4 + h + 3)
                pe.matmul(o, m_v[:, s, h * DV:(h + 1) * DV], attT[:, s % 2, h, :], start=True, stop=False)
                pe.matmul(o, m_st[:, s % 2, h, :], qf[:, s % 2, 0, h // 2, :], start=False, stop=False)
                mm = pe.matmul(o, m_s[:, s, h, :], qf[:, s % 2, 1, h // 2, :], start=False, stop=True)
                if h == GH - 1:
                    mm.then_inc(s_mo, 1)

            def sums(tile):
                t, q, s = tile
                pe.wait_ge(s_mos, t + 1)
                pe.wait_ge(s_mor, t + 2)
                for h in range(GH):
                    mm = pe.matmul(PS[:, 7, h:h + 1], osq[:, h * P:(h + 1) * P], ones[:, 0:1], start=True, stop=True)
                mm.then_inc(s_mss, 1)

            def spread(tile):
                t, q, s = tile
                pe.wait_ge(s_mrr, t * 2 + 2)
                for h in range(GH):
                    mm = pe.matmul(PS[:, 7, h * P:(h + 1) * P], ocol[:, s % 2, h:h + 1].broadcast_to([P, P]), ident[:, :],
                                   start=True, stop=True)
                mm.then_inc(s_mrb, 1)

            def step(tile, last, first=False):
                if not first:
                    sums(near(tile, -1))
                levels(tile, 1)
                if not first:
                    spread(near(tile, -1))
                contribution(tile)
                levels(tile, 2)
                outputs(tile, 0)
                levels(tile, 3)
                outputs(tile, 1)
                if not last:
                    turn(near(tile, 1))
                    levels(near(tile, 1), 0)
                outputs(tile, 2)
                outputs(tile, 3)
            turn((0, 0, 0))
            levels((0, 0, 0), 0)
            step((0, 0, 0), False, first=True)
            main_tiles(pe, step)
            sums((NT - 1, NT // 4 - 1, 3))
            spread((NT - 1, NT // 4 - 1, 3))

        M0 = H0
        raw5 = at("raw5", M0 + 7 * K, [P, 5, S])
        cqh = at("cqh", M0 + 47 * K, [P, 2, S], F32R)
        cql = at("cql", M0 + 63 * K, [P, 2, S], F32R)
        ckh = at("ckh", M0 + 79 * K, [P, S], F32R)
        ckl = at("ckl", M0 + 87 * K, [P, S], F32R)
        krh = at("krh", M0 + 95 * K, [P, S], F32R)
        krl = at("krl", M0 + 103 * K, [P, S], F32R)
        wqh = at("wqh", M0 + 111 * K, [P, 2, D], F32R)
        wql = at("wql", M0 + 119 * K, [P, 2, D], F32R)
        sq3 = at("sq3", M0 + 127 * K, [P, 2, 3, 512])
        nst = at("nst", M0 + 139 * K, [P, MH, 512])
        rst = at("rst", M0 + 147 * K, [P, 2, 512])
        rsw = at("rsw", M0 + 151 * K, [P, 2, 512])
        wq = at("wq", M0 + 156 * K, [P, 2, D])
        cosT = at("cosT", M0 + 164 * K, [P, S])
        turns = at("turns", M0 + 172 * K, [P, S])
        sinT = at("sinT", M0 + 180 * K, [P, S])
        posi = at("posi", M0 + 180 * K, [P, S], I32)
        mturn = at("mturn", M0 + 156 * K, [P, S])
        wkv = at("wkv", M0 + 188 * K, [P, MH, NOPE + MV])
        wkh = at("wkh", M0 + 192 * K, [P, MH, NOPE], F32R)
        wkl = at("wkl", M0 + 194 * K, [P, MH, NOPE], F32R)
        mcol = at("mcol", M0 + 196 * K, [P, 8])
        rcol = at("rcol", M0 + 196 * K + 32, [P, NB, 8])
        kvh = [at("kvh%d" % s, M0 + 32 * s * K, [P, 2, S], F32R) for s in range(2)]
        kvl = [at("kvl%d" % s, M0 + (32 * s + 16) * K, [P, 2, S], F32R) for s in range(2)]
        pb_ = at("pb_", M0 + 111 * K, [P, 2, S])
        pth = at("pth", M0 + 127 * K, [P, NT, 2 * P], F32R)
        ptl = at("ptl", M0 + 143 * K, [P, NT, 2 * P], F32R)
        qraw = at("qraw", M0 + 164 * K, [P, 2, 2, P])
        qsl = at("qsl", M0 + 166 * K, [P, 2, 3, P], F32R)
        diag = at("diag", M0 + 169 * K, [P, 2, P])
        mzt = at("mzt", M0 + 170 * K, [P, 2 * P])
        ost = at("ost", M0 + 171 * K, [P, 2 * P])
        mx4 = at("mx4", M0 + 172 * K, [P, 2, 4])
        rs4 = at("rs4", M0 + 172 * K + 32, [P, 2, 4])
        mx1 = at("mx1", M0 + 172 * K + 64, [P, 2])
        nm = at("nm", M0 + 172 * K + 96, [P, 2])
        rsm = at("rsm", M0 + 172 * K + 128, [P, 2])
        rinv = at("rinv", M0 + 172 * K + 160, [P, 2])

        s_rot = sem("s_rot")
        s_ang = sem("s_ang")
        s_pl = sem("s_pl")
        s_pw = sem("s_pw")
        s_pwh = sem("s_pwh")
        s_psq = sem("s_psq")
        s_pss = sem("s_pss")
        s_pr = sem("s_pr")
        s_prb = sem("s_prb")
        s_pn = sem("s_pn")
        s_ph = sem("s_ph")
        s_pk = sem("s_pk")
        s_plo = sem("s_plo")
        s_qp = sem("s_qp")
        s_qa = sem("s_qa")
        s_qd = sem("s_qd")
        s_qn = sem("s_qn")
        s_qr = sem("s_qr")

        def rot_sp(sp):
            sp.dma_start(posi[:, :], a["pos"].broadcast_to([P, S])).then_inc(s_rot, 16)
            sp.dma_start(mcol[:, 0:3], a["cst"][:, C_INVF:C_N]).then_inc(s_rot, 16)
            sp.dma_start(mcol[:, 3:5], a["gq"]).then_inc(s_rot, 16)
            sp.dma_start(mcol[:, 5:6], a["gkv"]).then_inc(s_rot, 16)
            sp.dma_start(wkv[:, :, :], a["wkv"]).then_inc(s_pw, 16)

        def latents_sp(sp):
            sp.dma_start(raw5[:, 0:3, :], projT[T_CQ:T_CQ + 3].rearrange("n p c -> p n c")).then_inc(s_pl, 16)
            for k, r in ((3, 0), (4, 1)):
                for half in range(4):
                    src = O_RKR + ROPE // 2 * ((half + r) % 2)
                    sp.dma_start(raw5[half * 32:half * 32 + 32, k, :], projT[T_GA, src:src + 32, :]).then_inc(s_pl, 16)
            sp.wait_ge(s_ang, A_ALL)
            sp.dma_start(wq[:, :, :], a["wq"]).then_inc(s_pw, 16)

        A_ALL = 11

        def rot_pool(pool):
            magic = float(np.float32(1.5 * 2 ** 23))
            c1 = 6.28125
            c2 = float(np.float32(np.round((2 * np.pi - c1) * 2 ** 20) / 2 ** 20))
            c3 = float(np.float32(2 * np.pi - c1 - c2))
            lim = float(np.nextafter(np.float32(np.pi), np.float32(0)))
            pool.wait_ge(s_rot, 64)
            pool.tensor_copy(cosT[:, :], posi[:, :]).then_inc(s_ang, 1)
            pool.wait_ge(s_ang, 1)
            pool.tensor_tensor(cosT[:, :], cosT[:, :], mcol[:, 0:1].broadcast_to([P, S]), ALU.mult).then_inc(s_ang, 1)
            pool.wait_ge(s_ang, 2)
            pool.tensor_scalar(turns[:, :], cosT[:, :], float(1 / (2 * np.pi)), magic, ALU.mult, ALU.add).then_inc(s_ang, 1)
            pool.wait_ge(s_ang, 3)
            pool.tensor_scalar(turns[:, :], turns[:, :], -magic, None, ALU.add).then_inc(s_ang, 1)
            for k, c in enumerate((c1, c2, c3)):
                pool.wait_ge(s_ang, 4 + 2 * k)
                pool.tensor_scalar(mturn[:, :], turns[:, :], -c, None, ALU.mult).then_inc(s_ang, 1)
                pool.wait_ge(s_ang, 5 + 2 * k)
                pool.tensor_tensor(cosT[:, :], cosT[:, :], mturn[:, :], ALU.add).then_inc(s_ang, 1)
            pool.wait_ge(s_ang, 10)
            pool.tensor_scalar(cosT[:, :], cosT[:, :], lim, -lim, ALU.min, ALU.max).then_inc(s_ang, 1)

        def blk(tb):
            return slice(tb * 512, (tb + 1) * 512)

        def latents_act(act):
            act.wait_ge(s_ang, A_ALL)
            act.activation(sinT[:, :], cosT[:, :], ACT.Sin, scale=mcol[:, 1:2]).then_inc(s_ang, 1)
            act.activation(turns[:, :], cosT[:, :], ACT.Abs).then_inc(s_ang, 1)
            act.wait_ge(s_ang, A_ALL + 2)
            act.activation(cosT[:, :], turns[:, :], ACT.Sin, bias=mcol[:, 2:3], scale=-1.0).then_inc(s_ang, 1)
            act.wait_ge(s_mst[0], 8 * NT + 16)
            act.wait_ge(s_mst[1], 8 * NT + 16)
            act.wait_ge(s_pl, 144)

            def squares(tb):
                if tb >= 2:
                    act.wait_ge(s_pss, tb - 1)
                act.activation(sq3[:, tb % 2, :, :], raw5[:, 0:3, blk(tb)], ACT.Square).then_inc(s_psq, 1)

            def his(tb):
                for k, hi in enumerate((cqh[:, 0, blk(tb)], cqh[:, 1, blk(tb)], ckh[:, blk(tb)])):
                    act.wait_ge(s_pn, 3 * tb + k + 1)
                    act.activation(hi, raw5[:, k, blk(tb)], ACT.Copy).then_inc(s_ph, 1)
            squares(0)
            squares(1)
            act.wait_ge(s_pw, 32)
            act.activation(wqh[:, :, :], wq[:, :, :], ACT.Copy).then_inc(s_pwh, 1)
            act.activation(wkh[:, :, :], wkv[:, :, 0:NOPE], ACT.Copy).then_inc(s_pwh, 1)
            his(0)
            squares(2)
            his(1)
            squares(3)
            his(2)
            his(3)
            act.wait_ge(s_pk, NB + 3)
            act.activation(krh[:, :], raw5[:, 3, :], ACT.Copy).then_inc(s_ph, 1)
            for tb in range(NB):
                if tb:
                    act.wait_ge(s_qn, 64 * tb)
                for n, j in enumerate(Q_NOPE):
                    act.wait_ge(s_qp, 8 * tb + j + 1)
                    act.activation(nst[:, n, :], PS[:, j, :], ACT.Copy).then_inc(s_qa, 1)

        Q_NOPE, Q_ROT, Q_SWAP = (0, 3, 6, 7), (1, 4), (2, 5)
        Q_COL = {**{j: n for n, j in enumerate(Q_NOPE)}, **{j: 4 + n for n, j in enumerate(Q_ROT)},
                 **{j: 6 + n for n, j in enumerate(Q_SWAP)}}

        def latents_pool(pool):
            def rstd(tb):
                pool.wait_ge(s_pr, 2 * tb + 2)
                pool.tensor_tensor(rcol[:, tb, :], rcol[:, tb, :], negh[:, 0:8], ALU.pow).then_inc(s_pk, 1)
            for tb in range(NB):
                rstd(tb)
            pool.wait_ge(s_ang, A_ALL + 3)
            pool.tensor_tensor(raw5[:, 3, :], raw5[:, 3, :], cosT[:, :], ALU.mult).then_inc(s_pk, 1)
            pool.tensor_tensor(raw5[:, 4, :], raw5[:, 4, :], sinT[:, :], ALU.mult).then_inc(s_pk, 1)
            pool.wait_ge(s_pk, NB + 2)
            pool.tensor_tensor(raw5[:, 3, :], raw5[:, 3, :], raw5[:, 4, :], ALU.add).then_inc(s_pk, 1)
            pool.wait_ge(s_ph, 3 * NB + 1)
            pool.tensor_tensor(krl[:, :], raw5[:, 3, :], krh[:, :].bitcast(F32), ALU.subtract).then_inc(s_pk, 1)

        def latents_dve(dve):
            def means(tb):
                dve.wait_ge(s_pss, tb + 1)
                dve.tensor_scalar(rcol[:, tb, 0:4], PS[:, tb % 2, 0:4], 1.0 / QR, EPS, ALU.mult, ALU.add).then_inc(s_pr, 1)
                dve.tensor_scalar(rcol[:, tb, 4:8], PS[:, tb % 2, 4:8], 1.0 / KVR, EPS, ALU.mult, ALU.add).then_inc(s_pr, 1)

            def normed(tb):
                dve.wait_ge(s_prb, tb + 1)
                for k in range(3):
                    dve.scalar_tensor_tensor(raw5[:, k, blk(tb)], raw5[:, k, blk(tb)], mcol[:, 3 + k:4 + k],
                                             PS[:, 2 + 2 * (tb % 2) + k // 2, :], ALU.mult, ALU.mult).then_inc(s_pn, 1)

            def los(tb):
                for k, (hi, lo) in enumerate(((cqh[:, 0, blk(tb)], cql[:, 0, blk(tb)]),
                                              (cqh[:, 1, blk(tb)], cql[:, 1, blk(tb)]), (ckh[:, blk(tb)], ckl[:, blk(tb)]))):
                    dve.wait_ge(s_ph, 3 * tb + k + 1)
                    dve.tensor_tensor(lo, raw5[:, k, blk(tb)], hi.bitcast(F32), ALU.subtract).then_inc(s_plo, 1)
            means(0)
            means(1)
            dve.wait_ge(s_pwh, 2)
            dve.tensor_tensor(wql[:, :, :], wq[:, :, :], wqh[:, :, :].bitcast(F32), ALU.subtract).then_inc(s_pwh, 1)
            dve.tensor_tensor(wkl[:, :, :], wkv[:, :, 0:NOPE], wkh[:, :, :].bitcast(F32), ALU.subtract).then_inc(s_pwh, 1)
            normed(0)
            los(0)
            means(2)
            normed(1)
            los(1)
            means(3)
            normed(2)
            los(2)
            normed(3)
            los(3)
            dve.wait_ge(s_ang, A_ALL + 3)
            for tb in range(NB):
                if tb:
                    dve.wait_ge(s_qr, 128 * tb)
                for r in range(2):
                    n = 6 * tb + 3 * r
                    dve.wait_ge(s_qp, 8 * tb + Q_ROT[r] + 1)
                    dve.tensor_tensor(rst[:, r, :], PS[:, Q_ROT[r], :], cosT[:, blk(tb)], ALU.mult).then_inc(s_qd, 1)
                    dve.wait_ge(s_qp, 8 * tb + Q_SWAP[r] + 1)
                    if n >= 6:
                        dve.wait_ge(s_qd, n - 3)
                    dve.tensor_tensor(rsw[:, r, :], PS[:, Q_SWAP[r], :], sinT[:, blk(tb)], ALU.mult).then_inc(s_qd, 1)
                    dve.wait_ge(s_qd, n + 2)
                    dve.tensor_tensor(rst[:, r, :], rst[:, r, :], rsw[:, r, :], ALU.add).then_inc(s_qd, 1)

        def latents_pe(pe):
            pe.wait_ge(s_mog, NT + 2)
            pe.wait_ge(s_mm, GH * NT + 2)

            def sums(tb):
                pe.wait_ge(s_psq, tb + 1)
                if tb >= 2:
                    pe.wait_ge(s_pr, 2 * (tb - 2) + 2)
                for t in range(4):
                    tok = slice(t * P, (t + 1) * P)
                    for k in range(2):
                        pe.matmul(PS[:, tb % 2, t:t + 1], sq3[:, tb % 2, k, tok], ones[:, 0:1], start=(k == 0), stop=(k == 1))
                    mm = pe.matmul(PS[:, tb % 2, 4 + t:5 + t], sq3[:, tb % 2, 2, tok], ones[:, 0:1], start=True, stop=True)
                mm.then_inc(s_pss, 1)

            def spread(tb):
                pe.wait_ge(s_pk, tb + 1)
                if tb >= 2:
                    pe.wait_ge(s_pn, 3 * (tb - 2) + 3)
                for c in range(8):
                    mm = pe.matmul(PS[:, 2 + 2 * (tb % 2) + c // 4, (c % 4) * P:(c % 4 + 1) * P],
                                   rcol[:, tb, c:c + 1].broadcast_to([P, P]), ident[:, :], start=True, stop=True)
                mm.then_inc(s_prb, 1)
            sums(0)
            sums(1)
            spread(0)
            sums(2)
            spread(1)
            sums(3)
            spread(2)
            spread(3)
            pe.wait_ge(s_pwh, 4)
            pe.wait_ge(s_pr, 2 * NB)
            for tb in range(NB):
                pe.wait_ge(s_plo, 3 * tb + 2)
                for j in range(8):
                    if tb == 0 and 2 <= j < 6:
                        pe.wait_ge(s_pn, 3 * (2 + j // 4) + 3)
                    if tb and j in Q_NOPE:
                        pe.wait_ge(s_qa, 4 * (tb - 1) + Q_COL[j] + 1)
                    if tb and j not in Q_NOPE:
                        pe.wait_ge(s_qd, 6 * (tb - 1) + 3 * (j // 3) + j % 3)
                    c = slice(Q_COL[j] * P, (Q_COL[j] + 1) * P)
                    for k in range(2):
                        pe.matmul(PS[:, j, :], wqh[:, k, c], cqh[:, k, blk(tb)], start=(k == 0), stop=False)
                        pe.matmul(PS[:, j, :], wqh[:, k, c], cql[:, k, blk(tb)], start=False, stop=False)
                        mm = pe.matmul(PS[:, j, :], wql[:, k, c], cqh[:, k, blk(tb)], start=False, stop=(k == 1))
                    mm.then_inc(s_qp, 1)

        def queries_sp(sp):
            for tb in range(NB):
                for j in range(8):
                    if j in Q_NOPE:
                        n = Q_COL[j]
                        sp.wait_ge(s_qa, 4 * tb + n + 1)
                        sp.dma_start(q_all[n * NT + 4 * tb:n * NT + 4 * tb + 4, :, 0, :].rearrange("t p q -> p t q"),
                                     nst[:, n, :].rearrange("p (t q) -> p t q", t=4)).then_inc(s_qn, 16)
                    if j in Q_SWAP:
                        r = Q_SWAP.index(j)
                        sp.wait_ge(s_qd, 6 * tb + 3 * r + 3)
                        for h in range(2):
                            t0 = (2 * r + h) * NT + 4 * tb
                            for half in range(2):
                                sp.dma_start(q_all[t0:t0 + 4, half * ROPE:(half + 1) * ROPE, 1, :].rearrange("t p q -> p t q"),
                                             rst[h * ROPE:(h + 1) * ROPE, r, :].rearrange("p (t q) -> p t q", t=4)
                                             ).then_inc(s_qr, 16)

        s_kp = sem("s_kp")
        s_kh = sem("s_kh")
        s_kl = sem("s_kl")

        def piece_pe(pe, h, n, bank):
            if bank == 7 and 8 * h + n > 8:
                pe.wait_ge(s_kl, 8 * h + n)
            if n < 4:
                pe.matmul(PS[:, bank, :], wkh[:, h, :], ckh[:, blk(n)], start=True, stop=False)
                pe.matmul(PS[:, bank, :], wkh[:, h, :], ckl[:, blk(n)], start=False, stop=False)
                mm = pe.matmul(PS[:, bank, :], wkl[:, h, :], ckh[:, blk(n)], start=False, stop=True)
            else:
                for t in range(4):
                    tok, o = slice((4 * n - 16 + t) * P, (4 * n - 15 + t) * P), PS[:, bank, t * P:(t + 1) * P]
                    pe.matmul(o, ckh[:, tok].bitcast(F32), wkv[:, h, NOPE:], start=True, stop=False)
                    mm = pe.matmul(o, ckl[:, tok].bitcast(F32), wkv[:, h, NOPE:], start=False, stop=True)
            mm.then_inc(s_kp, 1)

        def piece_at(part, h, n):
            return part[h % 2][:, n // 4, blk(n % 4)]

        def piece_act(act, h, n, bank):
            act.wait_ge(s_kp, 8 * h + n + 1)
            act.activation(piece_at(kvh, h, n), PS[:, bank, :], ACT.Copy).then_inc(s_kh, 1)

        def piece_dve(dve, h, n, bank):
            dve.wait_ge(s_kh, 8 * h + n + 1)
            dve.tensor_tensor(piece_at(kvl, h, n), PS[:, bank, :], piece_at(kvh, h, n).bitcast(F32), ALU.subtract
                              ).then_inc(s_kl, 1)

        s_qi = [sem("s_qi0"), sem("s_qi1")]
        s_q = sem("s_q")
        s_S = sem("s_S")
        s_nm = sem("s_nm")
        s_exp = sem("s_exp")
        s_rinv = sem("s_rinv")
        s_dg = sem("s_dg")
        s_T = sem("s_T")
        s_hi = sem("s_hi")
        s_lo = sem("s_lo")
        s_O = sem("s_O")
        s_oe = sem("s_oe")
        s_mlg = sem("s_mlg")
        s_ast = sem("s_ast")
        NP_ = NT // 2

        def heads(eng, step):
            for h in range(MH):
                step(h, 0, False)
                if h < MH - 1:
                    step(h, 1, True)
                with eng.Fori(2 if h < MH - 1 else 1, NP_) as i:
                    step(h, i, False)

        def attn_pe(pe):
            def scores(h, N, u):
                kh, kl = kvh[h % 2][:, 0, :], kvl[h % 2][:, 0, :]
                pe.wait_ge(s_q, N * 3 + 9)
                for b in range(4):
                    pe.wait_ge(s_exp, N * 4 + b + 1)
                    o, c = PS[:, b, :], blk(b)
                    pe.matmul(o, qsl[:, u, 0, :], kh[:, c], start=True, stop=False)
                    pe.matmul(o, qsl[:, u, 0, :], kl[:, c], start=False, stop=False)
                    pe.matmul(o, qsl[:, u, 1, :], kh[:, c], start=False, stop=False)
                    pe.matmul(o, qsl[:, u, 2, :], krh[:, c], start=False, stop=False)
                    pe.matmul(o, qsl[:, u, 2, :], krl[:, c], start=False, stop=True).then_inc(s_S, 1)

            def turn(N, u, chunks):
                pe.wait_ge(s_dg, N + 1)
                for c in chunks:
                    pe.wait_ge(s_exp, N * 4 + c + 5)
                    pe.wait_ge(s_lo, N * 4 + c + 1)
                    for j in range(4):
                        mm = pe.matmul(PS[:, 4 + c % 2, j * P:(j + 1) * P], pb_[:, u, (4 * c + j) * P:(4 * c + j + 1) * P],
                                       diag[:, u, :], start=True, stop=True)
                    mm.then_inc(s_T, 1)

            def values(h, I, half):
                vh, vl = kvh[h % 2][:, 1, :], kvl[h % 2][:, 1, :]
                if half == 0:
                    pe.wait_ge(s_oe, I + 1)
                for c in (2 * half, 2 * half + 1):
                    pe.wait_ge(s_lo, I * 8 + 4 + c + 3)
                    for k in range(4 * c, 4 * c + 4):
                        o, tok = PS[:, 6, 0:2 * P], slice(k * P, (k + 1) * P)
                        pe.matmul(o, vh[:, tok], pth[:, k, :], start=(k == 0), stop=False)
                        pe.matmul(o, vh[:, tok], ptl[:, k, :], start=False, stop=False)
                        mm = pe.matmul(o, vl[:, tok], pth[:, k, :], start=False, stop=(k == NT - 1))
                if half:
                    mm.then_inc(s_O, 1)

            def step(h, i, fill):
                N, I = i * 2 + h * NT, i + h * NP_
                before = not (h == 0 and isinstance(i, int) and i == 0)
                hb = h - 1 if isinstance(i, int) and i == 0 else h

                def piece(n):
                    if fill:
                        piece_pe(pe, h + 1, n, 7)
                scores(h, N, 0)
                piece(0)
                if before:
                    turn(N - 1, 1, (0, 1))
                piece(1)
                if before:
                    turn(N - 1, 1, (2, 3))
                piece(2)
                if before:
                    values(hb, I - 1, 0)
                piece(3)
                scores(h, N + 1, 1)
                piece(4)
                if before:
                    values(hb, I - 1, 1)
                piece(5)
                turn(N, 0, (0, 1))
                piece(6)
                turn(N, 0, (2, 3))
                piece(7)
            pe.wait_ge(s_qa, 4 * NB)
            pe.wait_ge(s_qd, 6 * NB)
            for n in range(8):
                piece_pe(pe, 0, n, n)
            pe.wait_ge(s_kl, 8)
            pe.wait_ge(s_pk, NB + 4)
            heads(pe, step)
            turn(MH * NT - 1, 1, range(4))
            values(MH - 1, MH * NP_ - 1, 0)
            values(MH - 1, MH * NP_ - 1, 1)

        def attn_act(act):
            def exps(N, u, b):
                if b == 0:
                    act.wait_ge(s_nm, N * 6 + 6)
                    act.wait_ge(s_T, N * 4 + 4)
                act.activation(pb_[:, u, blk(b)], PS[:, b, :], ACT.Exp, bias=nm[:, u:u + 1],
                               scale=SM_SCALE, accum_out=rs4[:, u, b:b + 1]).then_inc(s_exp, 1)

            def his(N, I, u, c):
                act.wait_ge(s_T, N * 4 + c + 9)
                if c == 0:
                    act.wait_ge(s_O, I + 1)
                act.activation(pth[:, 4 * c:4 * c + 4, u * P:(u + 1) * P], PS[:, 4 + c % 2, :].rearrange("p (k q) -> p k q", k=4),
                               ACT.Copy).then_inc(s_hi, 1)

            def step(h, i, fill):
                N, I = i * 2 + h * NT, i + h * NP_
                before = not (h == 0 and isinstance(i, int) and i == 0)

                def piece(n):
                    if fill:
                        piece_act(act, h + 1, n, 7)
                for c in range(4):
                    if before:
                        his(N - 1, I - 1, 1, c)
                    exps(N, 0, c)
                    piece(c)
                for b in range(4):
                    exps(N + 1, 1, b)
                    if b == 1:
                        piece(4)
                piece(5)
                for c in range(4):
                    his(N, I, 0, c)
                    if c == 1:
                        piece(6)
                piece(7)
            act.wait_ge(s_qa, 4 * NB)
            act.wait_ge(s_pk, NB + 4)
            act.wait_ge(s_plo, 3 * NB)
            for n in range(8):
                piece_act(act, 0, n, n)
            heads(act, step)
            for c in range(4):
                his(MH * NT - 1, MH * NP_ - 1, 1, c)

        def attn_dve(dve):
            def maxima(N, u):
                for b in range(4):
                    dve.wait_ge(s_S, N * 4 + b + 9)
                    dve.tensor_reduce(mx4[:, u, b:b + 1], PS[:, b, :], AX, ALU.max).then_inc(s_nm, 1)
                dve.wait_ge(s_nm, N * 6 + 4)
                dve.tensor_reduce(mx1[:, u:u + 1], mx4[:, u, :], AX, ALU.max).then_inc(s_nm, 1)
                dve.wait_ge(s_nm, N * 6 + 5)
                dve.tensor_scalar(nm[:, u:u + 1], mx1[:, u:u + 1], -SM_SCALE, None, ALU.mult).then_inc(s_nm, 1)

            def sums(N, u):
                dve.wait_ge(s_exp, N * 4 + 8)
                dve.tensor_reduce(rsm[:, u:u + 1], rs4[:, u, :], AX, ALU.add).then_inc(s_rinv, 1)
                dve.wait_ge(s_rinv, N * 2 + 1)
                dve.reciprocal(rinv[:, u:u + 1], rsm[:, u:u + 1]).then_inc(s_rinv, 1)

            def los(N, u, c):
                dve.wait_ge(s_hi, N * 4 + c + 1)
                o = slice(4 * c, 4 * c + 4), slice(u * P, (u + 1) * P)
                dve.tensor_tensor(ptl[:, o[0], o[1]], PS[:, 4 + c % 2, :].rearrange("p (k q) -> p k q", k=4),
                                  pth[:, o[0], o[1]].bitcast(F32), ALU.subtract).then_inc(s_lo, 1)

            def outs(I):
                dve.wait_ge(s_O, I + 2)
                dve.wait_ge(s_mlg, I * 16 + 16)
                dve.wait_ge(s_ast, I * 16 + 16)
                dve.tensor_tensor(ost[:, :], PS[:, 6, 0:2 * P], mzt[:, :], ALU.mult).then_inc(s_oe, 1)

            def step(h, i, fill):
                N, I = i * 2 + h * NT, i + h * NP_
                before = not (h == 0 and isinstance(i, int) and i == 0)

                def piece(n):
                    if fill:
                        piece_dve(dve, h + 1, n, 7)
                maxima(N, 0)
                for c in range(4):
                    if before:
                        los(N - 1, 1, c)
                    piece(c)
                sums(N, 0)
                maxima(N + 1, 1)
                piece(4)
                if before:
                    outs(I - 1)
                piece(5)
                for c in range(4):
                    los(N, 0, c)
                    if c == 1:
                        piece(6)
                piece(7)
                sums(N + 1, 1)
            dve.wait_ge(s_pk, NB + 4)
            for n in range(8):
                piece_dve(dve, 0, n, n)
            heads(dve, step)
            for c in range(4):
                los(MH * NT - 1, 1, c)
            outs(MH * NP_ - 1)

        def attn_pool(pool):
            def split(N, I, u):
                pool.wait_ge(s_qi[u], I * 16 + 16)
                pool.wait_ge(s_S, N * 4 + 4)
                pool.tensor_tensor(qsl[:, u, 0:3:2, :], qraw[:, u, :, :],
                                   zero[:, 0:1].unsqueeze(1).broadcast_to([P, 2, P]), ALU.add).then_inc(s_q, 1)
                pool.wait_ge(s_q, N * 3 + 7)
                pool.tensor_tensor(qsl[:, u, 1, :], qraw[:, u, 0, :], qsl[:, u, 0, :].bitcast(F32), ALU.subtract).then_inc(s_q, 1)
                pool.wait_ge(s_q, N * 3 + 8)
                pool.tensor_tensor(qsl[ROPE:P, u, 2, :], qraw[ROPE:P, u, 1, :], qsl[ROPE:P, u, 2, :].bitcast(F32), ALU.subtract
                                   ).then_inc(s_q, 1)
                pool.wait_ge(s_q, N * 3 + 9)

            def diagonal(N, u):
                pool.wait_ge(s_rinv, N * 2 + 2)
                pool.wait_ge(s_T, N * 4 + 4)
                pool.tensor_tensor(diag[:, u, :], ident[:, :], rinv[:, u:u + 1].broadcast_to([P, P]), ALU.mult).then_inc(s_dg, 1)

            split(0, 0, 0)
            split(1, 0, 1)
            with pool.Fori(0, MH * NP_ - 1) as I:
                for u in range(2):
                    split(I * 2 + 2 + u, I + 1, u)
                    diagonal(I * 2 + u, u)
            for u in range(2):
                diagonal(MH * NT - 2 + u, u)

        def attn_sp(sp):
            sp.wait_ge(s_qn, 64 * NB)
            sp.wait_ge(s_qr, 128 * NB)

            def query(N, u):
                sp.wait_ge(s_q, N * 3 + 3)
                sp.dma_start(qraw[:, u, :, :], q_all[ds(N, 1), :, :, :].rearrange("a p w q -> (a p) w q")).then_inc(s_qi[u], 16)

            def gates(h, i, I):
                sp.wait_ge(s_oe, I + 1)
                sp.dma_start(mzt[:, :], projT[h * 2 + T_MZ, :, ds(i * (2 * P), 2 * P)]
                             ).then_inc(s_mlg, 16)

            def store(h, i, I):
                sp.wait_ge(s_oe, I + 2)
                sp.dma_start(mixT[h + GH, :, ds(i * (2 * P), 2 * P)], ost[:, :]
                             ).then_inc(s_ast, 16)

            def step(h, i, last):
                I = i + h * NP_
                if not last:
                    for u in range(2):
                        query(I * 2 + 2 + u, u)
                if not isinstance(i, int) or i:
                    store(h, i - 1, I - 1)
                elif h:
                    store(h - 1, NP_ - 1, I - 1)
                gates(h, i, I)
            for u in range(2):
                query(u, u)
            for h in range(MH):
                step(h, 0, False)
                with sp.Fori(1, NP_ - (h == MH - 1)) as i:
                    step(h, i, False)
            step(MH - 1, NP_ - 1, True)
            store(MH - 1, NP_ - 1, MH * NP_ - 1)

        OK = (KD, CT)
        O_G = 4
        OF = (2, 1)
        OX = (H0 + 64 * K, X0)
        O_W = [dict(h=at("ow_h%d" % l, H0, [P, OK[l], D], F32R), lo=at("ow_l%d" % l, H0 + OK[l] * 4 * K, [P, OK[l], D], F32R),
                    f=at("of_%d" % l, OX[l], [P, OF[l], OK[l], P]), fh=at("of_h%d" % l, OX[l] + 8 * K, [P, 2, OK[l], P], F32R),
                    fl=at("of_l%d" % l, OX[l] + 24 * K, [P, 2, OK[l], P], F32R),
                    gh=at("og_h%d" % l, OX[l] + 32 * K, [P, 2, 512], F32R),
                    gl=at("og_l%d" % l, OX[l] + 36 * K, [P, 2, 512], F32R),
                    x=at("oxt%d" % l, OX[l] + 40 * K, [P, 2, D]),
                    y=at("oy%d" % l, OX[l] + 48 * K, [P, 2, D]),
                    wr=at("owr%d" % l, OX[l] + 56 * K, [P, 2, D]),
                    gr=at("ogr%d" % l, OX[l] + 64 * K, [P, 2, 512])) for l in range(2)]
        ors = small[:, 48:50]
        ossq = small[:, 50:52]

        s_owr = [sem("s_owr0"), sem("s_owr1")]
        s_owh = sem("s_owh")
        s_owl = sem("s_owl")
        s_of = [sem("s_of0"), sem("s_of1")]
        s_ox = [sem("s_ox0"), sem("s_ox1")]
        s_ofh = sem("s_ofh")
        s_ofl = sem("s_ofl")
        s_ok = sem("s_ok")
        s_om = sem("s_om")
        s_osq = sem("s_osq")
        s_or = sem("s_or")
        s_oz = sem("s_oz")
        s_ost = [sem("s_ost0"), sem("s_ost1")]

        def o_c(l, k):
            return OK[0] * l + k

        def o_f(l, t):
            return (OK[0] + NT - O_G) * l + OK[l] + t - O_G

        def tile_loop(eng, step, last=NT):
            with eng.Fori(O_G // 2 + 1, last // 2) as i:
                for u in range(2):
                    step(i * 2 + u, i, u)

        def out_sp(sp, l, out, between=None):
            feat, res, w, o = (mixT, sgT)[l], (a["x"], x1)[l], a[("woe", "woo")[l]], O_W[l]
            for k in range(OK[l]):
                c = o_c(l, k)
                if k >= 2:
                    sp.wait_ge(s_owl, c - 1)
                    sp.wait_ge(s_ofl, o_f(l, O_G) - OK[l] + k - 1)
                sp.dma_start(o["wr"][:, c % 2, :], w[k]).then_inc(s_owr[c % 2], 16)
                sp.dma_start(o["gr"][:, c % 2, :], feat[k, :, 0:512]).then_inc(s_owr[c % 2], 16)

            def load_f(t, u):
                sp.wait_ge(s_ofl, o_f(l, t) + 1 - OF[l])
                sp.dma_start(o["f"][:, u % OF[l], :, :], feat[:, :, ds(t * P, P)].rearrange("k p c -> p k c")
                             ).then_inc(s_of[u], 16)

            def load_x(t, u):
                sp.wait_ge(s_oz, (NT * l + t) * 2 + 2)
                sp.dma_start(o["x"][:, u, :], res[ds(t * P, P), :]).then_inc(s_ox[u], 16)

            def store(t, u):
                sp.wait_ge(s_oz, (NT * l + t) * 2 + 6)
                sp.dma_start(out[ds(t * P, P), :], o["y"][:, u, :]).then_inc(s_ost[u], 16)

            def step(t, i, u):
                load_f(t, u)
                store(t - 2, u)
                load_x(t, u)
            load_f(4, 0)
            load_x(0, 0)
            load_x(1, 1)
            load_f(5, 1)
            for t in range(O_G):
                store(t, t % 2)
                load_x(t + 2, t % 2)
            tile_loop(sp, step, NT - 4 if between else NT)
            if between:
                between()
                for t in range(NT - 4, NT):
                    step(t, t // 2, t % 2)
            for t in (NT - 2, NT - 1):
                store(t, t % 2)

        def out_act(act, l, between=None):
            o = O_W[l]
            for k in range(OK[l]):
                c = o_c(l, k)
                act.wait_ge(s_owr[c % 2], 32 * (c // 2 + 1))
                act.activation(o["h"][:, k, :], o["wr"][:, c % 2, :], ACT.Copy).then_inc(s_owh, 1)
                if k >= 2:
                    act.wait_ge(s_ok, c - 1)
                act.activation(o["gh"][:, c % 2, :], o["gr"][:, c % 2, :], ACT.Copy).then_inc(s_ofh, 1)

            def split(t, i, u):
                act.wait_ge(s_of[u], (6 * l + i - 1) * 16)
                if isinstance(t, int) and t < O_G + 2:
                    if t == O_G + 1:
                        act.wait_ge(s_ok, o_c(l, OK[l]))
                else:
                    act.wait_ge(s_om, NT * l + t - 1)
                act.activation(o["fh"][:, u, :, :], o["f"][:, u % OF[l], :, :], ACT.Copy).then_inc(s_ofh, 1)

            def squares(t, i, u, bank=None):
                act.wait_ge(s_om, NT * l + t + 1)
                if l or not isinstance(t, int) or t >= 2:
                    act.wait_ge(s_ost[u], (i + NT // 2 * l) * 16)
                b = 4 * u if bank is None else bank
                act.activation(o["y"][:, u, :], PS[:, b:b + 2, :].rearrange("p b f -> p (b f)"), ACT.Square,
                               scale=D ** -0.5, accum_out=ossq[:, u:u + 1]).then_inc(s_osq, 1)

            def step(t, i, u):
                split(t, i, u)
                squares(t - 2, i - 1, u)
            split(4, 2, 0)
            squares(0, 0, 0, 0)
            squares(1, 0, 1, 2)
            split(5, 2, 1)
            squares(2, 1, 0, 4)
            squares(3, 1, 1, 6)
            tile_loop(act, step)
            if between:
                between()
            squares(NT - 2, NT // 2 - 1, 0)
            squares(NT - 1, NT // 2 - 1, 1)

        def out_pool(pool, l, between=None):
            o = O_W[l]
            for k in range(OK[l]):
                c = o_c(l, k)
                pool.wait_ge(s_ofh, o_f(l, O_G) - OK[l] + k + 1)
                pool.tensor_tensor(o["gl"][:, c % 2, :], o["gr"][:, c % 2, :], o["gh"][:, c % 2, :].bitcast(F32),
                                   ALU.subtract).then_inc(s_ofl, 1)

            def split(t, i, u):
                pool.wait_ge(s_ofh, o_f(l, t) + 1)
                pool.tensor_tensor(o["fl"][:, u, :, :], o["f"][:, u % OF[l], :, :], o["fh"][:, u, :, :].bitcast(F32),
                                   ALU.subtract).then_inc(s_ofl, 1)

            def rstd(t, i, u):
                n = NT * l + t
                pool.wait_ge(s_osq, n + 1)
                pool.tensor_tensor(ors[:, u:u + 1], ossq[:, u:u + 1], eps, ALU.add).then_inc(s_or, 1)
                pool.wait_ge(s_or, n * 2 + 1)
                pool.tensor_tensor(ors[:, u:u + 1], ors[:, u:u + 1], negh[:, 0:1], ALU.pow).then_inc(s_or, 1)

            def step(t, i, u):
                split(t, i, u)
                rstd(t - 2, i - 1, u)
            split(4, 2, 0)
            rstd(0, 0, 0)
            rstd(1, 0, 1)
            split(5, 2, 1)
            rstd(2, 1, 0)
            rstd(3, 1, 1)
            tile_loop(pool, step)
            if between:
                between()
            rstd(NT - 2, NT // 2 - 1, 0)
            rstd(NT - 1, NT // 2 - 1, 1)

        def out_dve(dve, l, between=None):
            o = O_W[l]
            for k in range(OK[l]):
                c = o_c(l, k)
                dve.wait_ge(s_owh, c + 1)
                dve.tensor_tensor(o["lo"][:, k, :], o["wr"][:, c % 2, :], o["h"][:, k, :].bitcast(F32), ALU.subtract
                                  ).then_inc(s_owl, 1)

            def tile(t, i, u, bank=None):
                n, b = NT * l + t, 4 * u if bank is None else bank
                dve.wait_ge(s_or, n * 2 + 2)
                dve.scalar_tensor_tensor(o["y"][:, u, :], PS[:, b:b + 2, :].rearrange("p b f -> p (b f)"),
                                         ors[:, u:u + 1], gate[:, l, :], ALU.mult, ALU.mult).then_inc(s_oz, 1)
                dve.wait_ge(s_oz, n * 2 + 5)
                dve.wait_ge(s_ox[u], (i + NT // 2 * l) * 16 + 16)
                dve.tensor_tensor(o["y"][:, u, :], o["y"][:, u, :], o["x"][:, u, :], ALU.add).then_inc(s_oz, 1)
            for t in range(O_G):
                tile(t, t // 2, t % 2, 2 * t)
            with dve.Fori(O_G // 2, NT // 2 - 1) as i:
                for u in range(2):
                    tile(i * 2 + u, i, u)
            if between:
                between()
            tile(NT - 2, NT // 2 - 1, 0)
            tile(NT - 1, NT // 2 - 1, 1)

        def out_pe(pe, l):
            w = O_W[l]
            for k in range(OK[l]):
                c = o_c(l, k)
                pe.wait_ge(s_owl, c + 1)
                pe.wait_ge(s_ofl, o_f(l, O_G) - OK[l] + k + 1)
                for t in range(O_G):
                    tok = slice(t * P, (t + 1) * P)
                    for half in range(2):
                        o, f = PS[:, 2 * t + half, :], slice(half * 512, half * 512 + 512)
                        pe.matmul(o, w["gh"][:, c % 2, tok], w["h"][:, k, f], start=(k == 0), stop=False)
                        pe.matmul(o, w["gh"][:, c % 2, tok], w["lo"][:, k, f], start=False, stop=False)
                        mm = pe.matmul(o, w["gl"][:, c % 2, tok], w["h"][:, k, f], start=False, stop=(k == OK[l] - 1))
                    if k == OK[l] - 1:
                        mm.then_inc(s_om, 1)
                if k < OK[l] - 1:
                    mm.then_inc(s_ok, 1)
            pe.wait_ge(s_om, NT * l + O_G)
            pe.sem_inc(s_ok, 1)

            def tile(t, u):
                n = NT * l + t
                pe.wait_ge(s_ofl, o_f(l, t) + 1)
                if isinstance(t, int):
                    pe.wait_ge(s_oz, (NT * l + 2 * u) * 2 + 6)
                else:
                    pe.wait_ge(s_oz, n * 2 + 2)
                for k in range(OK[l]):
                    for half in range(2):
                        o, c = PS[:, 4 * u + half, :], slice(half * 512, half * 512 + 512)
                        pe.matmul(o, w["fh"][:, u, k, :], w["h"][:, k, c], start=(k == 0), stop=False)
                        pe.matmul(o, w["fh"][:, u, k, :], w["lo"][:, k, c], start=False, stop=False)
                        mm = pe.matmul(o, w["fl"][:, u, k, :], w["h"][:, k, c], start=False, stop=(k == OK[l] - 1))
                mm.then_inc(s_om, 1)
            for u in range(2):
                tile(O_G + u, u)
            with pe.Fori(O_G // 2 + 1, NT // 2) as i:
                for u in range(2):
                    tile(i * 2 + u, u)

        NV = SGW // 512
        vsr = at("vsr", X0, [P, KD, 512])
        vsh = at("vsh", X0 + 16 * K, [P, KD, 512], F32R)
        vsl = at("vsl", X0 + 32 * K, [P, KD, 512], F32R)
        vev = at("vev", X0 + 48 * K, [P, 4, 512])
        vst = at("vst", X0 + 56 * K, [P, NT, NV, 6])
        vmv = at("vmv", X0 + 66 * K, [P, NT, 2])
        vrs = at("vrs", X0 + 66 * K + 128, [P, NT])
        vnm = at("vnm", X0 + 66 * K + 192, [P, NT])

        s_vr = sem("s_vr")
        s_vhi = sem("s_vhi")
        s_vlo = sem("s_vlo")
        s_vk = sem("s_vk")
        s_vp = sem("s_vp")
        s_vev = sem("s_vev")
        s_vbn = sem("s_vbn")
        s_vst = [sem("s_vst%d" % j) for j in range(4)]
        s_vs = sem("s_vs")

        def v_sp(sp):
            def load(n):
                sp.wait_ge(s_vlo, n * KD)
                sp.dma_start(vsr[:, :, :], a["wv"][ds(n, 1), :, :].rearrange("a p (k c) -> (a p) k c", k=KD)).then_inc(s_vr, 16)

            def stores(n):
                for t in range(NT):
                    sp.wait_ge(s_vev, n * NT + t + 3)
                    sp.dma_start(sg_v[t * P:(t + 1) * P, ds(n * 512, 512)], vev[:, t % 4, :]).then_inc(s_vst[t % 4], 16)
            load(0)
            with sp.Fori(0, NV - 1) as n:
                load(n + 1)
                stores(n)
            stores(NV - 1)

        def v_act(act):
            def split(n):
                act.wait_ge(s_vr, n * 16 + 16)
                for k in range(KD):
                    act.wait_ge(s_vk, n * KD + k + 1)
                    act.activation(vsh[:, k, :], vsr[:, k, :], ACT.Copy).then_inc(s_vhi, 1)

            def evac(n, t):
                act.wait_ge(s_vp, n * NT + t + 1)
                act.wait_ge(s_vbn, n * NT + t + 1)
                act.wait_ge(s_vst[t % 4], n * 64 + 16 * (t // 4))
                act.activation(vev[:, t % 4, :], PS[:, t % 2, :], ACT.Gelu).then_inc(s_vev, 1)
            split(0)
            with act.Fori(0, NV - 1) as n:
                for t in range(NT - 1):
                    evac(n, t)
                split(n + 1)
                evac(n, NT - 1)
            for t in range(NT):
                evac(NV - 1, t)

        def v_dve(dve):
            def split(n):
                for k in range(KD):
                    dve.wait_ge(s_vhi, n * KD + k + 1)
                    dve.tensor_tensor(vsl[:, k, :], vsr[:, k, :], vsh[:, k, :].bitcast(F32), ALU.subtract).then_inc(s_vlo, 1)

            def stats(n, t):
                dve.wait_ge(s_vev, n * NT + t + 3)
                dve.bn_stats(vst[:, t, ds(n, 1), :].rearrange("p a s -> p (a s)"), vev[:, t % 4, :]).then_inc(s_vbn, 1)
            split(0)
            with dve.Fori(0, NV - 1) as n:
                for t in range(NT - 1):
                    stats(n, t)
                split(n + 1)
                stats(n, NT - 1)
            for t in range(NT):
                stats(NV - 1, t)
            dve.wait_ge(s_vbn, NV * NT + 4)
            for t in range(NT):
                dve.bn_aggr(vmv[:, t, :], vst[:, t, :, :].rearrange("p n s -> p (n s)")).then_inc(s_vs, 1)
            dve.wait_ge(s_vs, NT + 2)
            dve.scalar_tensor_tensor(vnm[:, :], vmv[:, :, 0], -1.0, vrs[:, :], ALU.mult, ALU.mult).then_inc(s_vs, 1)

        def v_pool(pool):
            pool.wait_ge(s_vs, NT)
            pool.tensor_scalar(vrs[:, :], vmv[:, :, 1], EPS, None, ALU.add).then_inc(s_vs, 1)
            pool.wait_ge(s_vs, NT + 1)
            pool.tensor_tensor(vrs[:, :], vrs[:, :], negh[:, 0:NT], ALU.pow).then_inc(s_vs, 1)

        def v_pe(pe):
            with pe.Fori(0, NV) as n:
                for t in range(NT):
                    pe.wait_ge(s_vev, n * NT + t + 1)
                    tok, o = slice(t * P, (t + 1) * P), PS[:, t % 2, :]
                    for k in range(KD):
                        if t == 0:
                            pe.wait_ge(s_vlo, n * KD + k + 1)
                        pe.matmul(o, hTh[:, k, tok], vsh[:, k, :], start=(k == 0), stop=False)
                        pe.matmul(o, hTh[:, k, tok], vsl[:, k, :], start=False, stop=False)
                        mm = pe.matmul(o, hTl[:, k, tok], vsh[:, k, :], start=False, stop=(k == KD - 1))
                        if t == NT - 1:
                            if k < KD - 1:
                                mm.then_inc(s_vk, 1)
                            else:
                                mm.then_inc(s_vp, 1)
                        elif k == KD - 1:
                            mm.then_inc(s_vp, 1)
                pe.wait_ge(s_vp, n * NT + NT)
                pe.sem_inc(s_vk, 1)

        uT = at("uT", X0 + 48 * K, [P, S])
        mT = at("mT", X0 + 56 * K, [P, S])
        zT = at("zT", X0, [P, 2, 512])
        vm = at("vm", X0 + 4 * K, [P, NT, P])
        sw = at("sw", X0 + 12 * K, [P, SG_G * P])
        srow = at("srow", X0 + 16 * K, [P, SG_G * P])
        sbs = at("sbs", X0 + 20 * K, [P, SG_G * P])
        sbias = at("sbias", X0 + 64 * K, [P, P])
        sgg = at("sgg", X0 + 65 * K, [P, CT])
        sgb = at("sgb", X0 + 65 * K + 64, [P, CT])

        s_uc = sem("s_uc")
        s_us = sem("s_us")
        s_uv = sem("s_uv")
        s_uvn = sem("s_uvn")
        s_uu = sem("s_uu")
        s_uz = sem("s_uz")
        s_um = sem("s_um")
        s_ub = sem("s_ub")
        s_ume = sem("s_ume")
        s_umu = sem("s_umu")
        s_umz = sem("s_umz")
        s_ust = sem("s_ust")

        def uz_sp(sp):
            for j in range(4):
                sp.wait_ge(s_vst[j], 16 * NV * NT // 4)
            sp.wait_ge(s_vp, NV * NT)
            for dst, src in ((sw[:, :], a["sgw"]), (sbs[:, :], a["sgbs"].broadcast_to([P, SG_G * P])),
                             (sgg[:, :], a["sgg"]), (sgb[:, :], a["sgb"])):
                sp.dma_start(dst, src).then_inc(s_uc, 16)
            for s in range(2):
                tile_load(sp, "wuz", N_TILES + s, 0, s)

            def load_v(c):
                sp.wait_ge(s_um, c * 4)
                sp.dma_start(vm[:, :, :], sg_v[:, ds(c * P, P)].rearrange("(t p) c -> p t c", p=P)).then_inc(s_uv, 16)

            def store(c):
                sp.wait_ge(s_umz, c * 4 + 6)
                sp.dma_start(sgT[ds(c, 1), :, :].rearrange("a p f -> p (a f)"), mT[:, :]).then_inc(s_ust, 16)
            load_v(0)
            with sp.Fori(0, CT - 1) as c:
                tile_load(sp, "wuz", c * 2 + N_TILES + 2, c + 1, 0)
                load_v(c + 1)
                tile_load(sp, "wuz", c * 2 + N_TILES + 3, c + 1, 1)
                store(c)
            store(CT - 1)

        def uz_pool(pool):
            with pool.Fori(0, CT) as c:
                tile_split(pool, c * 2 + N_TILES, c + NPAIR, 0)
                tile_split(pool, c * 2 + N_TILES + 1, c + NPAIR, 1)

        def uz_act(act):
            act.wait_ge(s_vs, NT + 3)
            with act.Fori(0, CT) as c:
                act.wait_ge(s_uv, c * 16 + 16)
                for t in range(NT):
                    act.activation(vm[:, t, :], vm[:, t, :], ACT.Identity, bias=vnm[:, t:t + 1], scale=vrs[:, t:t + 1]
                                   ).then_inc(s_uvn, 1)
                for tb in range(NB):
                    act.wait_ge(s_pb, c * 8 + 4 * N_TILES + tb + 9)
                    act.wait_ge(s_umu, c * 4)
                    act.activation(uT[:, tb * 512:(tb + 1) * 512], PS[:, tb, :], ACT.Gelu).then_inc(s_uu, 1)
                for tb in range(NB):
                    act.wait_ge(s_pb, c * 8 + 4 * N_TILES + 4 + tb + 9)
                    act.wait_ge(s_umz, c * 4 + tb + 1)
                    act.activation(zT[:, tb % 2, :], PS[:, tb, :], ACT.Silu).then_inc(s_uz, 1)

        def uz_dve(dve):
            dve.wait_ge(s_us, 1)
            dve.tensor_copy(srow[:, :], PS[:, 4:6, :].rearrange("p b f -> p (b f)")).then_inc(s_us, 1)
            dve.wait_ge(s_us, 2)
            dve.wait_ge(s_uc, 64)
            with dve.Fori(0, CT // 2) as grp:
                for half in range(2):
                    c = grp * 2 + half
                    g = ds(grp * P, P)
                    dve.wait_ge(s_ume, c * 4 + 4)
                    dve.scalar_tensor_tensor(sbias[:, :], srow[:, g], sgb[:, ds(c, 1)], sbs[:, g], ALU.mult, ALU.add
                                             ).then_inc(s_ub, 1)
                    dve.wait_ge(s_ub, c + 1)
                    dve.wait_ge(s_ust, c * 16)
                    for tb in range(NB):
                        b = slice(tb * 512, (tb + 1) * 512)
                        dve.wait_ge(s_um, c * 4 + tb + 1)
                        dve.scalar_tensor_tensor(mT[:, b].rearrange("p (t i) -> p t i", t=4),
                                                 PS[:, 4 + tb, :].rearrange("p (t i) -> p t i", t=4), sgg[:, ds(c, 1)],
                                                 sbias[:, :].unsqueeze(1).broadcast_to([P, 4, P]), ALU.mult, ALU.add
                                                 ).then_inc(s_ume, 1)
                    for tb in range(NB):
                        b = slice(tb * 512, (tb + 1) * 512)
                        dve.wait_ge(s_ume, c * 4 + tb + 5)
                        dve.wait_ge(s_uu, c * 4 + tb + 1)
                        dve.tensor_tensor(mT[:, b], mT[:, b], uT[:, b], ALU.mult).then_inc(s_umu, 1)
                    for tb in range(NB):
                        b = slice(tb * 512, (tb + 1) * 512)
                        dve.wait_ge(s_umu, c * 4 + tb + 1)
                        dve.wait_ge(s_uz, c * 4 + tb + 5)
                        dve.tensor_tensor(mT[:, b], mT[:, b], zT[:, tb % 2, :], ALU.mult).then_inc(s_umz, 1)

        def uz_pe(pe):
            pe.wait_ge(s_uc, 64)
            for j in range(2):
                mm = pe.matmul(PS[:, 4 + j, :], ones[:, :], sw[:, j * 512:(j + 1) * 512], start=True, stop=True)
            mm.then_inc(s_us, 1)
            pe.wait_ge(s_us, 2)
            pe.wait_ge(s_vev, NV * NT + 2)
            with pe.Fori(0, CT // 2) as grp:
                for half in range(2):
                    c = grp * 2 + half
                    pe.wait_ge(s_wlo, c * 2 + N_TILES + 3)
                    for tb in range(NB):
                        pe.wait_ge(s_uz, c * 4 + tb + 1)
                        tile_block(pe, 0, tb, tb)
                    for t in range(NT):
                        if t % 4 == 0:
                            pe.wait_ge(s_ume, c * 4 + t // 4 + 1)
                        pe.wait_ge(s_uvn, c * 16 + t + 1)
                        mm = pe.matmul(PS[:, 4 + t // 4, t % 4 * P:t % 4 * P + P], vm[:, t, :], sw[:, ds(grp * P, P)],
                                       start=True, stop=True)
                        if t % 4 == 3:
                            mm.then_inc(s_um, 1)
                    pe.wait_ge(s_wlo, c * 2 + N_TILES + 4)
                    for tb in range(NB):
                        pe.wait_ge(s_uu, c * 4 + tb + 1)
                        tile_block(pe, 1, tb, tb)

        block = ctx.enter_context(nc.Block())

        @block.sync
        def _(sp):
            const_load(sp)
            mod_rows(sp, 0)
            norm_load(sp, 0, range(0, 2))
            for k in range(KD):
                mod_slice(sp, 0, k)
            norm_load(sp, 0, range(2, 4))
            proj_sp(sp)
            gates_sp(sp)
            rot_sp(sp)
            back_sp(sp)
            sp.sem_inc(s_mst[0], 16)
            sp.sem_inc(s_mst[1], 16)
            main_sp(sp)
            sp.sem_inc(s_ast, 16)
            queries_sp(sp)
            attn_sp(sp)
            sp.wait_ge(s_ast, 16 * MH * NP_ + 16)
            out_sp(sp, 0, x1, lambda: norm_load(sp, 1, range(4, 6)))
            norm_load(sp, 1, range(6, 8))
            sp.wait_ge(s_tp, 64)
            sp.wait_ge(s_hl, 64)
            v_sp(sp)
            uz_sp(sp)
            sp.wait_ge(s_ust, 16 * CT)
            out_sp(sp, 1, out)
            for u in range(2):
                sp.wait_ge(s_ost[u], 16 * NT)
        @block.gpsimd
        def _(pool):
            const_pool(pool)
            pool.sem_inc(s_wlo, 2)
            pool.wait_ge(s_set, 4)
            norm_pool_front(pool, 0)
            norm_pool(pool, 0)
            proj_pool(pool)
            pool.sem_inc(s_mkf, 2)
            rot_pool(pool)
            main_pool(pool)
            latents_pool(pool)
            pool.sem_inc(s_q, 6)
            attn_pool(pool)
            out_pool(pool, 0, lambda: norm_pool_front(pool, 4))
            norm_pool(pool, 1)
            v_pool(pool)
            uz_pool(pool)
            out_pool(pool, 1)
        @block.scalar
        def _(act):
            act.sem_inc(s_pev[0], 4)
            const_act(act)
            norm_act_front(act, 0)
            norm_act(act, 0)
            proj_act(act)
            gates_act(act)
            back_act(act)
            act.sem_inc(s_mkT, 2)
            act.sem_inc(s_mor, 2)
            main_act(act)
            act.sem_inc(s_exp, 4)
            latents_act(act)
            attn_act(act)
            out_act(act, 0, lambda: norm_act_front(act, 4))
            norm_act(act, 1)
            act.sem_inc(s_vev, 2)
            v_act(act)
            act.sem_inc(s_uz, 4)
            uz_act(act)
            out_act(act, 1)
        @block.vector
        def _(dve):
            dve.sem_inc(s_pev[1], 4)
            mod_start(dve, 0)
            dve.wait_ge(s_csl, 1)
            dve.wait_ge(s_gp, 32)
            norm_dve_front(dve, 0)
            for k in range(KD):
                mod_sum(dve, 0, k)
            mod_end(dve, 0)
            norm_dve(dve, 0)
            proj_dve(dve)
            mod_end(dve, 1)
            dve.sem_inc(s_bk, 2)
            gates_dve(dve)
            back_dve(dve)
            dve.sem_inc(s_mqf, 4)
            dve.sem_inc(s_ms, 4)
            dve.sem_inc(s_mm, 2)
            dve.sem_inc(s_ma, 2)
            dve.sem_inc(s_mog, 2)
            main_dve(dve)
            dve.sem_inc(s_lo, 2)
            dve.sem_inc(s_oe, 1)
            latents_dve(dve)
            attn_dve(dve)
            dve.sem_inc(s_oz, 4)
            out_dve(dve, 0, lambda: norm_dve_front(dve, 4))
            norm_dve(dve, 1)
            dve.sem_inc(s_vbn, 4)
            v_dve(dve)
            dve.sem_inc(s_ume, 4)
            dve.sem_inc(s_umz, 2)
            uz_dve(dve)
            out_dve(dve, 1)
        @block.tensor
        def _(pe):
            pe.sem_inc(s_pb, 8)
            mod_pe(pe, 0)
            norm_pe(pe, 0)
            proj_pe(pe)
            pe.wait_ge(s_pev[0], 4 * NPAIR + 4)
            pe.wait_ge(s_pev[1], 4 * NPAIR + 4)
            mod_pe(pe, 1)
            pe.sem_inc(s_bt, 2)
            gates_pe(pe)
            back_pe(pe)
            pe.sem_inc(s_mkt, 2)
            pe.sem_inc(s_mc, 2)
            pe.sem_inc(s_mlv, 8)
            pe.sem_inc(s_mo, 2)
            pe.sem_inc(s_mrb, 2)
            main_pe(pe)
            pe.sem_inc(s_S, 8)
            pe.sem_inc(s_T, 8)
            pe.sem_inc(s_O, 1)
            latents_pe(pe)
            attn_pe(pe)
            out_pe(pe, 0)
            norm_pe(pe, 1)
            pe.sem_inc(s_vk, 8)
            v_pe(pe)
            uz_pe(pe)
            out_pe(pe, 1)


def lay_out(x, c, positions, w_mod, b_mod, g_pre, g_post, w_in_e, gla_w_gate_f, gla_b_gate_f,
            gla_w_gate_b, gla_b_gate_b, gla_g_norm, mla_g_q, mla_w_uq, mla_g_kv, mla_w_ukv, w_out_e,
            w_in_o, sg_g_norm, sg_b_norm, sg_w_s, sg_b_s, w_out_o):
    f = np.float32
    c_ = np.ascontiguousarray

    def tile(w, cols):
        return w[:, cols].reshape(-1, P, len(cols)).transpose(1, 0, 2).reshape(P, -1)

    we = np.concatenate([w_in_e[0], np.zeros((D, 1), f)], axis=1)
    pad = np.full(P - 2 * RANK - ROPE, we.shape[1] - 1)
    r = np.arange
    kr = O_KR + r(ROPE)
    silu = [O_GZ + P * i + r(P) for i in range(4)] + [O_MZ + P * i + r(P) for i in range(4)]
    raw = [P * i + r(P) for i in range(8)]
    cols = [t for pair in zip(silu, raw) for t in pair]
    cols += [np.concatenate([O_GA + r(2 * RANK), kr, pad]), O_CQ + r(P), O_CQ + P + r(P), O_CKV + r(P)]
    wT = np.stack([tile(we, t) for t in cols])

    w2 = np.zeros((2 * RANK, 4 * P), f)
    w2[:RANK, :2 * P] = gla_w_gate_f[0]
    w2[RANK:, 2 * P:] = gla_w_gate_b[0]
    b2 = np.concatenate([gla_b_gate_f[0], gla_b_gate_b[0]]).reshape(4, P).T

    qo = (NOPE + ROPE) * r(MH)[:, None]
    rp = NOPE + r(ROPE)
    wq = np.concatenate([(qo + r(NOPE)).ravel(), (qo + rp).ravel(), (qo + np.roll(rp, ROPE // 2)).ravel()])

    j, i = np.meshgrid(r(P), r(P), indexing="ij")
    masks = [((j // (2 * s) == i // (2 * s)) & (j // s != i // s)) for s in LEVELS] + [i == j]
    inv = f(1) / (10000.0 ** (r(0, ROPE, 2) / ROPE)).astype(f)
    cst = np.concatenate([np.eye(P, dtype=f)] + [m.astype(f) for m in masks] +
                         [np.tile(inv, 4)[:, None], np.where(r(P) % ROPE < ROPE // 2, -1, 1).astype(f)[:, None],
                          np.full((P, 1), np.pi / 2, f)], axis=1)
    uz = [tile(w_in_o[0], o + P * n + r(P)) for n in range(CT) for o in (0, 2 * SGW)]
    return {
        "x": c_(x[0]), "cvec": c_(c[0].reshape(KD, P).T), "pos": c_(positions),
        "wmod": c_(w_mod), "bmod": c_(b_mod), "gpre": c_(g_pre.reshape(2, KD, P).transpose(2, 0, 1)), "gpost": c_(g_post),
        "wT": c_(wT), "w2": w2, "b2": c_(b2), "gnorm": c_(gla_g_norm[0][:, None]),
        "gq": c_(mla_g_q[0].reshape(2, P).T), "gkv": c_(mla_g_kv[0][:, None]),
        "wq": c_(tile(mla_w_uq[0], wq).reshape(P, 2, D)), "wkv": c_(mla_w_ukv[0].reshape(P, MH, NOPE + MV)),
        "woe": c_(w_out_e[0].reshape(KD, P, D)), "woo": c_(w_out_o[0].reshape(CT, P, D)),
        "wv": c_(np.stack([tile(w_in_o[0], SGW + 512 * n + r(512)) for n in range(4)])),
        "wuz": c_(np.stack(uz)),
        "sgg": c_(sg_g_norm[0].reshape(CT, P).T), "sgb": c_(sg_b_norm[0].reshape(CT, P).T),
        "sgw": c_(sg_w_s[0].transpose(2, 0, 1).reshape(P, SG_G * P)), "sgbs": c_(sg_b_s[0].reshape(1, SG_G * P)),
        "cst": c_(cst),
    }


def kernel(**inputs):
    import numpy as _np
    import concourse.bacc as _bacc
    from concourse import mybir as _mybir
    from concourse.bass_utils import run_bass_kernel_spmd as _run

    arrays = lay_out(**{k: _np.asarray(v) for k, v in inputs.items()})
    nc = _bacc.Bacc("TRN2", target_bir_lowering=False, num_devices=1)
    a = {n: nc.dram_tensor(n, v.shape, _mybir.dt.from_np(v.dtype), kind="ExternalInput").ap() for n, v in arrays.items()}
    out = nc.dram_tensor("out", (S, D), F32, kind="ExternalOutput").ap()
    emit(nc, a, out)
    r = _run(nc, [arrays], core_ids=[0])
    return r.results[0]["out"].reshape(1, S, D)
```

```python
from contextlib import ExitStack

import numpy as np

import concourse.bass as bass
from concourse import mybir

F32 = mybir.dt.float32
F32R = mybir.dt.float32r
I32 = mybir.dt.int32
ALU = mybir.AluOpType
ACT = mybir.ActivationFunctionType
AX = mybir.AxisListType.X
ds = bass.ds

P = 128
D = 1024
S = 2048
KD = D // P
NT = S // P
NB = S // 512
EPS = 1e-6
TAU = 16.0
GH, DK, DV, RANK = 4, 64, 128, 16
MH, NOPE, ROPE, MV = 4, 128, 64, 128
QR, KVR = 256, 128
SGW = 2048
CT = SGW // P
SG_G = 8
LEVELS = [64, 32, 16, 8, 4, 2, 1]
NLV = len(LEVELS)
SM_SCALE = float(NOPE + ROPE) ** -0.5

O_GQ, O_GK, O_GV = 0, 256, 512
O_GA, O_GZ = 1024, 1056
O_CQ, O_CKV, O_KR, O_MZ = 1568, 1824, 1952, 2016

T_GZ, T_MZ, T_GQ, T_GK, T_GV = 0, 8, 1, 5, 9
T_GA, T_CQ, T_CKV = 16, 17, 19
O_RKR = 2 * RANK
N_TILES = 20
NPAIR = N_TILES // 2
NSILU = 8

C_ID, C_MASK = 0, P
C_INVF = C_MASK + (NLV + 1) * P
C_N = C_INVF + 3


def emit(nc, a, out):
    def scratch(name, shape):
        return nc.dram_tensor(name, shape, F32, kind="Internal").ap()

    projT = scratch("projT", (N_TILES, P, S))
    cumT = scratch("cumT", (4, P, S))
    mixT = scratch("mixT", (KD, P, S))
    q_all = scratch("q_all", (MH * NT, P, 2, P))
    x1 = scratch("x1", (S, D))
    gla_v = scratch("gla_v", (NT, P, GH * DV))
    gla_sb = scratch("gla_sb", (NT, P, GH * DV))
    sg_v = scratch("sg_v", (S, SGW))
    sgT = scratch("sgT", (CT, P, S))

    with ExitStack() as ctx:
        def sem(name):
            return ctx.enter_context(nc.semaphore(name))

        def at(name, off, shape, dt=F32):
            return nc.alloc_sbuf_tensor_at(name, shape, dt, offset=off)

        K = 1024
        base = (nc.sbuf_base + 63) // 64 * 64
        ident = at("ident", base, [P, P])
        ones = at("ones", base + 512, [P, P])
        mod_a = at("mod_a", base + 1024, [P, 2, KD])
        mod_b = at("mod_b", base + 1088, [P, 2, KD])
        cvec = at("cvec", base + 1152, [P, KD])
        gpre = at("gpre", base + 1184, [P, 2, KD])
        small = at("small", base + 1248, [P, 80])
        gate = at("gate", base + 1568, [P, 2, D])
        negh = at("negh", base + 1568 + 8 * K, [P, 16])
        zero = at("zero", base + 1632 + 8 * K, [P, 8])
        eps = small[:, 52:53]
        H0 = base + 1664 + 8 * K
        hTh = at("hTh", H0, [P, KD, S], F32R)
        hTl = at("hTl", H0 + 64 * K, [P, KD, S], F32R)
        X0 = H0 + 128 * K
        macc = at("macc", X0, [P, 3 * D])
        mw = at("mw", X0 + 12 * K, [P, 2, 3 * D // 2])
        mw0 = at("mw0", X0 + 8 * K, [P, 2, 2 * D])
        maccg = at("maccg", X0 + 64 * K, [P, D])
        xt = at("xt", X0 + 24 * K, [P, 2, 4, D])
        nj = at("nj", X0 + 56 * K, [P, D])
        nt32 = at("nt32", X0 + 60 * K, [P, 4, 512])
        wraw = at("wraw", X0 + 24 * K, [P, 2, D])
        whi = at("whi", X0 + 32 * K, [P, 2, KD, P], F32R)
        wlo = at("wlo", X0 + 40 * K, [P, 2, KD, P], F32R)
        pev = at("pev", X0 + 48 * K, [P, 2, S])

        PS = ctx.enter_context(nc.psum_tensor("PS", [P, 8, 512], F32))

        s_const = sem("s_const")
        s_set = sem("s_set")
        s_csl = sem("s_csl")

        def const_load(sp):
            sp.dma_start(cvec[:, :], a["cvec"]).then_inc(s_const, 16)
            sp.dma_start(ident[:, :], a["cst"][:, C_ID:C_ID + P]).then_inc(s_const, 16)
            sp.dma_start(gpre[:, :, :], a["gpre"]).then_inc(s_const, 16)

        def const_pool(pool):
            pool.memset(ones[:, :], 1.0).then_inc(s_set, 1)
            pool.memset(negh[:, :], -0.5).then_inc(s_set, 1)
            pool.memset(zero[:, :], 0.0).then_inc(s_set, 1)
            pool.memset(eps, EPS).then_inc(s_set, 1)

        def const_act(act):
            act.wait_ge(s_const, 48)
            act.activation(cvec[:, :], cvec[:, :], ACT.Silu).then_inc(s_csl, 1)

        s_gp = sem("s_gp")
        s_mw = [sem("s_mw0"), sem("s_mw1")]
        s_mz = sem("s_mz")
        s_macc = sem("s_macc")
        s_mps = sem("s_mps")
        s_mod = sem("s_mod")

        MOD_0 = [(0, 0, 2048)]
        MOD_1 = [(1, 0, 1536), (1, 1536, 3072), (0, 2048, 2560), (0, 2560, 3072)]

        def mod_acc(part):
            l, a0, a1 = part
            return maccg[:, a0 - 2048:a1 - 2048] if l == 0 and a0 >= 2048 else macc[:, a0:a1]

        def mod_rows(sp, l):
            sp.dma_start(gate[:, l, :], a["gpost"][l:l + 1, :].broadcast_to([P, D])).then_inc(s_gp, 16)
            sp.wait_ge(s_mz, 2 * l + 1)
            if l == 0:
                sp.dma_start(macc[0:1, 0:2048], a["bmod"][0:1, 0:2048]).then_inc(s_gp, 16)
            else:
                sp.dma_start(macc[0:1, :], a["bmod"][1:2, :]).then_inc(s_gp, 16)
                sp.dma_start(maccg[0:1, :], a["bmod"][0:1, 2048:3072]).then_inc(s_gp, 16)

        def mod_slot(parts, first, j):
            if len(parts) == 1:
                return first % 2, mw0[:, first % 2, :]
            return j % 2, mw[:, j % 2, 0:parts[j][2] - parts[j][1]]

        def mod_slice(sp, parts, first, k):
            for j, (l, a0, a1) in enumerate(parts):
                if not isinstance(first, int) or first + j >= 2:
                    sp.wait_ge(s_macc, first + j - 1)
                s, slot = mod_slot(parts, first, j)
                sp.dma_start(slot, a["wmod"][l:l + 1, ds(k * P, P), a0:a1].rearrange("a p f -> (a p) f")).then_inc(s_mw[s], 16)

        def mod_start(dve, l):
            if l:
                dve.wait_ge(s_mps, 1)
                dve.wait_ge(s_hl, 32)
                dve.memset(maccg[:, :], 0.0).then_inc(s_mz, 1)
            dve.memset(macc[:, :], 0.0).then_inc(s_mz, 1)

        def mod_sum(dve, parts, first, half, k):
            for j, part in enumerate(parts):
                s, slot = mod_slot(parts, first, j)
                dve.wait_ge(s_mw[s], (half + j // 2 + 1) * 16)
                if not isinstance(first, int) or first + j >= 1:
                    dve.wait_ge(s_macc, first + j - (len(parts) > 1))
                acc = mod_acc(part)
                dve.scalar_tensor_tensor(acc, slot, cvec[:, ds(k, 1)], acc, ALU.mult, ALU.add).then_inc(s_macc, 1)

        def mod_pe(pe, l):
            pe.wait_ge(s_macc, KD + l * 4 * KD)
            pe.wait_ge(s_set, 1)
            for j in range(2 * KD):
                mm = pe.matmul(PS[:, 0, j:j + 1], macc[:, j * P:(j + 1) * P], ones[:, 0:1], start=True, stop=True)
            if l:
                for bank, src in ((1, macc[:, 2048:2560]), (2, macc[:, 2560:3072]), (3, maccg[:, 0:512]), (4, maccg[:, 512:1024])):
                    mm = pe.matmul(PS[:, bank, :], ones[:, :], src, start=True, stop=True)
            mm.then_inc(s_mps, 1)

        def mod_end(dve, l):
            dve.wait_ge(s_mps, l + 1)
            dve.scalar_tensor_tensor(mod_a[:, l, :], PS[:, 0, KD:2 * KD], 1.0, gpre[:, l, :], ALU.add, ALU.mult
                                     ).then_inc(s_mod, 1)
            dve.tensor_copy(mod_b[:, l, :], PS[:, 0, 0:KD]).then_inc(s_mod, 1)
            if l:
                for bank, m, j in ((1, 1, 0), (2, 1, 1), (3, 0, 0), (4, 0, 1)):
                    g = gate[:, m, j * 512:(j + 1) * 512]
                    dve.tensor_tensor(g, PS[:, bank, :], g, ALU.mult).then_inc(s_mod, 1)

        s_x = [sem("s_x0"), sem("s_x1")]
        s_sq = sem("s_sq")
        s_rs = sem("s_rs")
        s_xn = sem("s_xn")
        s_tp = sem("s_tp")
        s_hh = sem("s_hh")
        s_h32 = sem("s_h32")
        s_hl = sem("s_hl")

        def norm_load(sp, l, groups):
            src = a["x"] if l == 0 else x1
            for g in groups:
                q = g % 4
                if g >= 2:
                    sp.wait_ge(s_tp, 8 * (g - 1))
                if l:
                    for u in range(2):
                        sp.wait_ge(s_ost[u], 32 * (q + 1))
                sp.dma_start(xt[:, g % 2, :, :], src[q * 512:(q + 1) * 512, :].rearrange("(t p) d -> p t d", p=P)
                             ).then_inc(s_x[g % 2], 16)

        def norm_act_front(act, g):
            act.wait_ge(s_x[g % 2], 16 * (g // 2 + 1))
            for t in range(4):
                n = 4 * g + t
                if n:
                    act.wait_ge(s_sq, n)
                c = 32 + 4 * (g % 2) + t
                act.activation(nj[:, :], xt[:, g % 2, t, :], ACT.Square, accum_out=small[:, c:c + 1]).then_inc(s_sq, 1)

        def norm_act(act, l):
            for g in range(4 * l, 4 * l + 4):
                for k in range(KD):
                    m = 8 * g + k
                    act.wait_ge(s_tp, m + 1)
                    if m == 32 * l:
                        act.wait_ge(s_mod, 2 * l + 2)
                    if m >= 4:
                        act.wait_ge(s_hl, m - 3)
                    act.activation(nt32[:, m % 4, :], PS[:, k, :], ACT.Identity, bias=mod_b[:, l, k:k + 1],
                                   scale=mod_a[:, l, k:k + 1]).then_inc(s_h32, 1)
                if g % 4 < 2:
                    norm_act_front(act, g + 2)

        def h_block(m):
            return (m % 8, slice((m // 8 % 4) * 512, (m // 8 % 4 + 1) * 512))

        def norm_pool_front(pool, g):
            c = slice(32 + 4 * (g % 2), 36 + 4 * (g % 2))
            r = slice(40 + 4 * (g % 2), 44 + 4 * (g % 2))
            pool.wait_ge(s_sq, 4 * (g + 1))
            if g >= 2:
                pool.wait_ge(s_xn, 4 * (g - 1))
            pool.tensor_scalar(small[:, r], small[:, c], 1.0 / D, EPS, ALU.mult, ALU.add).then_inc(s_rs, 1)
            pool.wait_ge(s_rs, 2 * g + 1)
            pool.tensor_tensor(small[:, r], small[:, r], negh[:, 0:4], ALU.pow).then_inc(s_rs, 1)

        def norm_pool(pool, l):
            for g in range(4 * l, 4 * l + 4):
                for m in range(8 * g, 8 * g + 8):
                    k, b = h_block(m)
                    pool.wait_ge(s_h32, m + 1)
                    pool.tensor_tensor(hTh[:, k, b], nt32[:, m % 4, :], zero[:, 0:1].broadcast_to([P, 512]), ALU.add
                                       ).then_inc(s_hh, 1)
                if g % 4 < 2:
                    norm_pool_front(pool, g + 2)

        def norm_dve_front(dve, g):
            dve.wait_ge(s_rs, 2 * g + 2)
            for t in range(4):
                r = 40 + 4 * (g % 2) + t
                dve.tensor_scalar(xt[:, g % 2, t, :], xt[:, g % 2, t, :], small[:, r:r + 1], None, ALU.mult
                                  ).then_inc(s_xn, 1)

        def norm_dve(dve, l):
            for g in range(4 * l, 4 * l + 4):
                for m in range(8 * g, 8 * g + 8):
                    k, b = h_block(m)
                    dve.wait_ge(s_hh, m + 1)
                    dve.tensor_tensor(hTl[:, k, b], nt32[:, m % 4, :], hTh[:, k, b].bitcast(F32), ALU.subtract
                                      ).then_inc(s_hl, 1)
                if g % 4 < 2:
                    norm_dve_front(dve, g + 2)

        def norm_pe(pe, l):
            pe.wait_ge(s_const, 48)
            for g in range(4 * l, 4 * l + 4):
                pe.wait_ge(s_xn, 4 * (g + 1))
                for k in range(KD):
                    m = 8 * g + k
                    if g % 4:
                        pe.wait_ge(s_h32, m - 7)
                    elif l == 0 and k == 0:
                        pe.wait_ge(s_mod, 2)
                    elif l and k in (0, 4):
                        pe.wait_ge(s_oz, 2 * NT + k // 2 + 2)
                    for t in range(4):
                        mm = pe.transpose(PS[:, k, t * P:(t + 1) * P], xt[:, g % 2, t, k * P:(k + 1) * P], ident[:, :])
                    mm.then_inc(s_tp, 1)

        s_wr = [sem("s_wr0"), sem("s_wr1")]
        s_whi = sem("s_whi")
        s_wlo = sem("s_wlo")
        s_pb = sem("s_pb")
        s_pev = [sem("s_pev0"), sem("s_pev1")]
        s_pst = [sem("s_pst0"), sem("s_pst1")]

        def tile_load(sp, name, g, i, s):
            sp.wait_ge(s_wlo, g + 1)
            sp.dma_start(wraw[:, s, :], a[name][ds(2 * i + s, 1), :, :].rearrange("a p f -> p (a f)")
                         ).then_inc(s_wr[s], 16)

        def tile_split(pool, g, h, s):
            hi = whi[:, s, :, :].rearrange("p k c -> p (k c)")
            lo = wlo[:, s, :, :].rearrange("p k c -> p (k c)")
            pool.wait_ge(s_wr[s], (h + 1) * 16)
            pool.wait_ge(s_pb, 4 * g + 4)
            pool.tensor_tensor(hi, wraw[:, s, :], zero[:, 0:1].broadcast_to([P, D]), ALU.add).then_inc(s_whi, 1)
            pool.wait_ge(s_whi, g + 1)
            pool.tensor_tensor(lo, wraw[:, s, :], hi.bitcast(F32), ALU.subtract).then_inc(s_wlo, 1)

        def tile_block(pe, s, tb, bank):
            b = slice(tb * 512, (tb + 1) * 512)
            for k in range(KD):
                pe.matmul(PS[:, bank, :], whi[:, s, k, :], hTh[:, k, b], start=(k == 0), stop=False)
                pe.matmul(PS[:, bank, :], whi[:, s, k, :], hTl[:, k, b], start=False, stop=False)
                mm = pe.matmul(PS[:, bank, :], wlo[:, s, k, :], hTh[:, k, b], start=False, stop=(k == KD - 1))
            mm.then_inc(s_pb, 1)

        def proj_sp(sp):
            def store(i):
                sp.wait_ge(s_pev[1], 4 * i + 8)
                sp.dma_start(projT[ds(2 * i + 1, 1), :, :].rearrange("a p f -> p (a f)"), pev[:, 1, :]
                             ).then_inc(s_pst[1], 16)
            sp.wait_ge(s_tp, 32)
            sp.wait_ge(s_sq, 16)
            sp.wait_ge(s_hl, 32)
            for s in range(2):
                tile_load(sp, "wT", s, 0, s)
            mod_rows(sp, 1)
            with sp.Fori(0, NSILU) as i:
                for s in range(2):
                    tile_load(sp, "wT", 2 * i + 2 + s, i + 1, s)
                store(i)
                mod_slice(sp, MOD_1, i * 4 + KD, i)
            with sp.Fori(NSILU, NPAIR - 1) as i:
                for s in range(2):
                    tile_load(sp, "wT", 2 * i + 2 + s, i + 1, s)
                store(i)
            store(NPAIR - 1)

        def proj_pool(pool):
            pool.wait_ge(s_hl, 32)
            with pool.Fori(0, NPAIR) as i:
                for s in range(2):
                    tile_split(pool, 2 * i + s, i, s)

        def proj_pe(pe):
            pe.wait_ge(s_hl, 32)
            pe.wait_ge(s_hh, 32)
            with pe.Fori(0, NPAIR) as i:
                for s in range(2):
                    pe.wait_ge(s_wlo, 2 * i + s + 3)
                    for tb in range(NB):
                        pe.wait_ge(s_pev[s], 4 * i + tb + 1)
                        tile_block(pe, s, tb, 4 * s + tb)

        def proj_act(act):
            def tile(i, func):
                act.wait_ge(s_pst[0], 16 * i + 1)
                for tb in range(NB):
                    act.wait_ge(s_pb, 8 * i + tb + 9)
                    act.activation(pev[:, 0, tb * 512:(tb + 1) * 512], PS[:, tb, :], func).then_inc(s_pev[0], 1)
                act.wait_ge(s_pev[0], 4 * i + 8)
                act.dma_start(projT[ds(2 * i, 1), :, :].rearrange("a p f -> p (a f)"), pev[:, 0, :]
                              ).then_inc(s_pst[0], 16)
            with act.Fori(0, NSILU) as i:
                tile(i, ACT.Silu)
            with act.Fori(NSILU, NPAIR) as i:
                tile(i, ACT.Copy)

        def proj_dve(dve):
            def tile(i):
                dve.wait_ge(s_pst[1], 16 * i + 1)
                for tb in range(NB):
                    dve.wait_ge(s_pb, 8 * i + 4 + tb + 9)
                    dve.tensor_copy(pev[:, 1, tb * 512:(tb + 1) * 512], PS[:, 4 + tb, :]).then_inc(s_pev[1], 1)
            mod_start(dve, 1)
            dve.wait_ge(s_gp, 80)
            with dve.Fori(0, NSILU) as i:
                tile(i)
                mod_sum(dve, MOD_1, i * 4 + KD, i * 2 + KD // 2, i)
            with dve.Fori(NSILU, NPAIR) as i:
                tile(i)

        G0 = H0
        gmask = at("gmask", G0, [P, (NLV + 1) * P])
        gw2 = at("gw2", G0 + 4 * K, [2 * RANK, 4 * P])
        gb2 = at("gb2", G0 + 6 * K, [P, 4])
        ggn = at("ggn", G0 + 6 * K + 32, [P, 1])
        gtot = at("gtot", G0 + 6 * K + 64, [P, 4, NT])
        gtots = at("gtots", G0 + 6 * K + 320, [P, 4, NT])
        G1 = G0 + 7 * K
        ga = at("ga", G1, [2 * RANK, S])
        greset = at("greset", G1 + 8 * K, [P, S])
        gt1 = at("gt1", G1 + 16 * K, [P, 2, S])
        gt2 = at("gt2", G1 + 32 * K, [P, 2, S])
        gcum = at("gcum", G1 + 48 * K, [P, S])
        kt = at("kt", G1, [P, 2, 2, P])
        et = at("et", G1 + 2 * K, [P, 2, 2, P])
        vt = at("vt", G1 + 4 * K, [P, 2, GH, P])
        vv = at("vv", G1 + 8 * K, [P, 2, GH * DV])
        xe = at("xe", G1 + 12 * K, [P, 2, 2, P])
        kb2 = at("kb2", G1 + 14 * K, [P, 2, 2, P])
        kfT = at("kfT", G1 + 21 * K, [P, 2, 2 * P])
        st = at("st", G1 + 17 * K, [P, 2, GH, DV])
        G2 = G1 + 40 * K
        m_k = at("m_k", G2, [P, 4, 2, P])
        m_q = at("m_q", G2 + 4 * K, [P, 4, 2, P])
        m_f = at("m_f", G2 + 8 * K, [P, 4, 2, P])
        m_e = at("m_e", G2 + 12 * K, [P, 4, 2, P])
        m_v = at("m_v", G2 + 16 * K, [P, 4, GH * DV])
        m_s = at("m_s", G2 + 24 * K, [P, 4, GH, DV])
        m_z = at("m_z", G2 + 32 * K, [P, 4, GH, P])
        m_x = at("m_x", G2 + 40 * K, [P, 2, 3, 2, P])
        m_kf = at("m_kf", G2 + 46 * K, [P, 2, 2, P])
        m_kT = at("m_kT", G2 + 48 * K, [P, 2, 2 * P])
        m_st = at("m_st", G2 + 50 * K, [P, 2, GH, DV])
        xa = at("xa", G2 + 54 * K, [P, 2, 2, NLV, 2, P])
        tmp_l = at("tmp_l", G2 + 82 * K, [P, 2, NLV + 1, P])
        attT = at("attT", G2 + 90 * K, [P, 2, GH, P])
        qf = at("qf", G2 + 94 * K, [P, 2, 2, 2, P])
        osq = at("osq", G2 + 98 * K, [P, GH * P])
        orr = at("orr", G2 + 100 * K, [P, GH * P])
        og = at("og", G2 + 102 * K, [P, 2, GH, P])
        ocol = at("ocol", G2 + 106 * K, [P, 2, GH])

        s_gc = sem("s_gc")
        s_gm = sem("s_gm")
        s_gl = sem("s_gl")
        s_ga = sem("s_ga")
        s_gmin = sem("s_gmin")
        s_gcum = sem("s_gcum")
        s_gtot = sem("s_gtot")
        s_gst = sem("s_gst")

        def gates_sp(sp):
            sp.wait_ge(s_pst[0], 16 * NPAIR + 1)
            sp.wait_ge(s_pst[1], 16 * NPAIR + 1)
            sp.wait_ge(s_pb, 8 + 4 * N_TILES)
            for dst, src in ((ga[:, :], projT[T_GA, 0:2 * RANK, :]), (gw2[:, :], a["w2"]), (gb2[:, :], a["b2"]),
                             (ggn[:, :], a["gnorm"]), (gmask[:, :], a["cst"][:, C_MASK:C_INVF])):
                sp.dma_start(dst, src).then_inc(s_gc, 16)
            rot_sp(sp)
            for n in range(4):
                sp.wait_ge(s_gcum, (1, 2, 3, 5)[n])
                sp.dma_start(cumT[n], gcum[:, :]).then_inc(s_gst, 16)

        def gates_pe(pe):
            pe.wait_ge(s_gc, 80)
            pe.wait_ge(s_mod, 8)
            for n in range(4):
                for tb in range(NB):
                    if n >= 2:
                        pe.wait_ge(s_gmin, 5 * (n - 2) + tb + 1)
                    pe.matmul(PS[:, 4 * (n % 2) + tb, :], gw2[:, n * P:(n + 1) * P], ga[:, tb * 512:(tb + 1) * 512],
                              start=True, stop=True).then_inc(s_gl, 1)

        def gates_act(act):
            act.wait_ge(s_gc, 80)
            act.wait_ge(s_gm, 3)
            for n in range(4):
                if n >= 2:
                    act.wait_ge(s_gmin, 5 * (n - 1))
                for tb in range(NB):
                    act.wait_ge(s_gl, 4 * n + tb + 1)
                    act.activation(gt1[:, n % 2, tb * 512:(tb + 1) * 512], PS[:, 4 * (n % 2) + tb, :], ACT.Abs,
                                   bias=gb2[:, n:n + 1]).then_inc(s_ga, 1)
                act.wait_ge(s_ga, 6 * n + 4)
                act.activation(gt1[:, n % 2, :], gt1[:, n % 2, :], ACT.Exp, scale=-1.0).then_inc(s_ga, 1)
                act.wait_ge(s_ga, 6 * n + 5)
                act.activation(gt1[:, n % 2, :], gt1[:, n % 2, :], ACT.Ln, bias=1.0).then_inc(s_ga, 1)
            act.wait_ge(s_gtot, 4)
            act.activation(gtot[:, :, :], gtots[:, :, :], ACT.Exp).then_inc(s_gtot, 1)

        def gates_dve(dve):
            dve.wait_ge(s_pb, 8 + 4 * N_TILES)
            dve.memset(greset[:, :], 1.0).then_inc(s_gm, 1)
            dve.wait_ge(s_gm, 1)
            dve.memset(greset[:, 0:S:P], 0.0).then_inc(s_gm, 1)
            dve.memset(gcum[:, 0:1], 0.0).then_inc(s_gm, 1)
            for n in range(4):
                for tb in range(NB):
                    dve.wait_ge(s_ga, 6 * n + tb + 1)
                    if n >= 2:
                        dve.wait_ge(s_gtot, n - 1)
                    dve.tensor_scalar(gt2[:, n % 2, tb * 512:(tb + 1) * 512], PS[:, 4 * (n % 2) + tb, :], gb2[:, n:n + 1], 0.0,
                                      ALU.add, ALU.min).then_inc(s_gmin, 1)
                dve.wait_ge(s_gmin, 5 * n + 4)
                dve.wait_ge(s_ga, 6 * n + 6)
                dve.tensor_tensor(gt2[:, n % 2, :], gt2[:, n % 2, :], gt1[:, n % 2, :], ALU.subtract).then_inc(s_gmin, 1)
                dve.wait_ge(s_gmin, 5 * n + 5)
                dve.wait_ge(s_gm, 3)
                if n:
                    dve.wait_ge(s_gst, 16 * n)
                if n == 2:
                    dve.memset(gcum[:, 0:1], 0.0).then_inc(s_gm, 1)
                    dve.wait_ge(s_gm, 4)
                if n < 2:
                    dve.tensor_tensor_scan(gcum[:, :], greset[:, :], gt2[:, n % 2, :], 0.0, ALU.mult, ALU.add
                                           ).then_inc(s_gcum, 1)
                    dve.wait_ge(s_gcum, n + 1)
                    dve.tensor_scalar(gtots[:, n, :], gcum[:, P - 1:S:P], 1.0 / TAU, None, ALU.mult).then_inc(s_gtot, 1)
                else:
                    dve.tensor_tensor_scan(gcum[:, 1:S], gt2[:, n % 2, 0:S - 1], greset[:, 1:S], 0.0, ALU.add, ALU.mult
                                           ).then_inc(s_gcum, 1)
                    dve.wait_ge(s_gcum, 2 * n - 1)
                    dve.tensor_tensor(gtots[:, n, :], gcum[:, P - 1:S:P], gt2[:, n % 2, P - 1:S:P], ALU.add).then_inc(s_gcum, 1)
                    dve.wait_ge(s_gcum, 2 * n)
                    dve.tensor_scalar(gtots[:, n, :], gtots[:, n, :], 1.0 / TAU, None, ALU.mult).then_inc(s_gtot, 1)

        s_bl = [sem("s_bl0"), sem("s_bl1")]
        s_bx = sem("s_bx")
        s_bk = sem("s_bk")
        s_bt = sem("s_bt")
        s_bkT = sem("s_bkT")
        s_bv = sem("s_bv")
        s_bc = sem("s_bc")
        s_bs = sem("s_bs")
        s_bvs = [sem("s_bvs0"), sem("s_bvs1")]
        s_bss = [sem("s_bss0"), sem("s_bss1")]

        def back_sp(sp):
            sp.wait_ge(s_gst, 64)
            sp.wait_ge(s_gtot, 5)
            with sp.Fori(0, NT // 2) as i:
                for u in range(2):
                    n = 2 * i + u
                    tok = ds(i * (-2 * P) + (NT - 1 - u) * P, P)
                    sp.wait_ge(s_bk, n + 1)
                    sp.wait_ge(s_bt, n + 1)
                    sp.dma_start(kt[:, u, :, :], projT[T_GK:T_GK + 4:2, :, tok].rearrange("h p c -> p h c")).then_inc(s_bl[u], 16)
                    sp.dma_start(et[:, u, :, :], cumT[2:4, :, tok].rearrange("h p c -> p h c")).then_inc(s_bl[u], 16)
                    sp.dma_start(vt[:, u, :, :], projT[T_GV:T_GV + 8:2, :, tok].rearrange("h p c -> p h c")).then_inc(s_bl[u], 16)

        def back_steps(eng, step, ahead):
            ahead(0, 0, 0)
            with eng.Fori(0, NT // 2 - 1) as i:
                ahead(i * 2 + 1, i, 1)
                step(i * 2, i, 0)
                ahead(i * 2 + 2, i + 1, 0)
                step(i * 2 + 1, i, 1)
            i = NT // 2 - 1
            ahead(2 * i + 1, i, 1)
            step(2 * i, i, 0)
            step(2 * i + 1, i, 1)

        def back_act(act):
            def factors(n, i, u):
                act.wait_ge(s_bl[u], i * 48 + 48)
                act.wait_ge(s_bk, n + 1)
                act.activation(xe[:, u, :, :], et[:, u, :, :], ACT.Exp, scale=1.0 / TAU).then_inc(s_bx, 1)

            def step(n, i, u):
                act.wait_ge(s_bt, n + 3)
                act.wait_ge(s_bvs[u], i * 16 + 1)
                act.activation(vv[:, u, :], PS[:, 3 * u + 1, :], ACT.Copy).then_inc(s_bv, 1)
                act.wait_ge(s_bv, n + 1 + 1)
                act.dma_start(gla_v[ds(i * -2 + (NT - 1 - u), 1), :, :].rearrange("a p f -> p (a f)"), vv[:, u, :]
                              ).then_inc(s_bvs[u], 16)
                act.wait_ge(s_bs, n * 4 + 4)
                act.dma_start(gla_sb[ds(i * -2 + (NT - 1 - u), 1), :, :].rearrange("a p f -> p (a f)"),
                              st[:, u, :, :].rearrange("p h v -> p (h v)")).then_inc(s_bss[u], 16)
            back_steps(act, step, factors)

        def state_step(dve, old, new, bank, pair0, tok, done):
            for h in range(GH):
                r = slice(DK * (h % 2), DK * (h % 2) + DK)
                c = (h // 2) * 2 * DV + (h % 2) * DV
                dve.scalar_tensor_tensor(new[r, h, :], old[r, h, :], gtot[r, pair0 + h // 2, tok], PS[r, bank, c:c + DV],
                                         ALU.mult, ALU.add).then_inc(done, 1)

        def back_dve(dve):
            dve.wait_ge(s_gst, 64)
            dve.wait_ge(s_gtot, 4)
            dve.memset(st[:, :, :, :], 0.0).then_inc(s_gm, 1)
            dve.wait_ge(s_gm, 5)
            dve.sem_inc(s_bs, 4)

            def weighted(n, i, u):
                dve.wait_ge(s_bx, n + 1)
                dve.wait_ge(s_bt, n + 1)
                dve.tensor_tensor(kb2[:, u, :, :], kt[:, u, :, :], xe[:, u, :, :], ALU.mult).then_inc(s_bk, 1)

            def step(n, i, u):
                dve.wait_ge(s_bt, n + 3)
                dve.tensor_copy(kfT[:, u, :], PS[:, 3 * u, 0:2 * P]).then_inc(s_bkT, 1)
                dve.wait_ge(s_bc, n + 1)
                dve.wait_ge(s_bss[1 - u], (i + u) * 16 + 1)
                dve.wait_ge(s_bs, n * 4 + 4)
                state_step(dve, st[:, u], st[:, 1 - u], 3 * u + 2, 2, ds(i * -2 + (NT - 1 - u), 1), s_bs)
            back_steps(dve, step, weighted)

        def back_pe(pe):
            pe.wait_ge(s_gmin, 20)

            def turn(n, i, u):
                pe.wait_ge(s_bl[u], i * 48 + 48)
                pe.wait_ge(s_bk, n + 3)
                if isinstance(n, int) and n < 2:
                    pass
                else:
                    pe.wait_ge(s_bkT, n - 1 + 1)
                    pe.wait_ge(s_bv, n - 1 + 1)
                for p in range(2):
                    pe.transpose(PS[:, 3 * u, p * P:(p + 1) * P], kb2[:, u, p, :], ident[:, :])
                for h in range(GH):
                    mm = pe.transpose(PS[:, 3 * u + 1, h * P:(h + 1) * P], vt[:, u, h, :], ident[:, :])
                mm.then_inc(s_bt, 1)

            def step(n, i, u):
                pe.wait_ge(s_bkT, n + 1 + 1)
                pe.wait_ge(s_bv, n + 1 + 1)
                pe.wait_ge(s_bs, n * 4 + 4)
                for p in range(2):
                    mm = pe.matmul(PS[:, 3 * u + 2, p * 2 * DV:(p + 1) * 2 * DV], kfT[:, u, p * P:(p + 1) * P],
                                   vv[:, u, p * 2 * DV:(p + 1) * 2 * DV], start=True, stop=True)
                mm.then_inc(s_bc, 1)
            back_steps(pe, step, turn)

        s_ml = [sem("s_ml%d" % s) for s in range(4)]
        s_mf = sem("s_mf")
        s_me = sem("s_me")
        s_mx = sem("s_mx")
        s_mq = sem("s_mq")
        s_mk = sem("s_mk")
        s_msx = sem("s_msx")
        s_mqf = sem("s_mqf")
        s_mkf = sem("s_mkf")
        s_mkt = sem("s_mkt")
        s_mkT = sem("s_mkT")
        s_mc = sem("s_mc")
        s_ms = sem("s_ms")
        s_mlv = sem("s_mlv")
        s_mm = sem("s_mm")
        s_ma = sem("s_ma")
        s_mo = sem("s_mo")
        s_mos = sem("s_mos")
        s_mss = sem("s_mss")
        s_mrr = sem("s_mrr")
        s_mrb = sem("s_mrb")
        s_mor = sem("s_mor")
        s_mog = sem("s_mog")
        s_mgz = sem("s_mgz")
        s_mst = [sem("s_mst0"), sem("s_mst1")]

        def near(tile, d):
            t, q, s = tile
            return (t + d, q + (s + d) // 4, (s + d) % 4)

        def main_tiles(eng, step):
            with eng.Fori(0, NT // 4 - 1) as i:
                for u in range(1, 5):
                    step((i * 4 + u, i + u // 4, u % 4), False)
            for t in range(NT - 3, NT):
                step((t, t // 4, t % 4), t == NT - 1)

        def halves(tile, s):
            v = tile.rearrange("p h (b c s) -> p h b c s", c=2, s=s)
            n = P // (2 * s)
            return (v[:, :, :, 0, :], v[:, :, :, 1, :], v[:, :, :, 0, s - 1:s].broadcast_to([P, 2, n, s]),
                    v[:, :, :, 1, 0:1].broadcast_to([P, 2, n, s]))

        def main_sp(sp):
            def load(tile, parts=(0, 1)):
                t, q, s = tile
                tok = ds(t * P, P)
                if 0 in parts:
                    for dst, src in ((m_q, projT[T_GQ:T_GQ + 4:2, :, tok]), (m_k, projT[T_GK:T_GK + 4:2, :, tok]),
                                     (m_f, cumT[0:2, :, tok]), (m_e, cumT[2:4, :, tok]), (m_z, projT[T_GZ:T_GZ + 8:2, :, tok])):
                        sp.dma_start(dst[:, s, :, :], src.rearrange("h p c -> p h c")).then_inc(s_ml[s], 16)
                if 1 in parts:
                    sp.dma_start(m_v[:, s, :], gla_v[ds(t, 1), :, :].rearrange("a p f -> p (a f)")).then_inc(s_ml[s], 16)
                    sp.dma_start(m_s[:, s, :, :].rearrange("p h v -> p (h v)"),
                                 gla_sb[ds(t, 1), :, :].rearrange("a p f -> p (a f)")).then_inc(s_ml[s], 16)

            def store(tile):
                t, q, s = tile
                sp.wait_ge(s_mgz, t + 1)
                sp.dma_start(mixT[0:GH, :, ds(t * P, P)].rearrange("h p c -> p h c"), og[:, s % 2, :, :]
                             ).then_inc(s_mst[s % 2], 16)

            for t in range(4):
                load((t, 0, t), (0,))
            for q in range(2):
                sp.wait_ge(s_bvs[q], 16 * (NT // 2) + 1)
                sp.wait_ge(s_bss[q], 16 * (NT // 2) + 1)
            for t in range(4):
                load((t, 0, t), (1,))
            sp.wait_ge(s_bc, NT)
            sp.wait_ge(s_bs, 4 * NT + 4)
            latents_sp(sp)
            with sp.Fori(0, NT // 4 - 1) as i:
                for u in range(4):
                    tile = (i * 4 + u, i, u)
                    store(tile)
                    load(near(tile, 4))
            for t in range(NT - 4, NT):
                store((t, t // 4, t % 4))

        def main_act(act):
            def factors(tile):
                t, q, s = tile
                p = s % 2
                act.wait_ge(s_ml[s], q * 112 + 112)
                act.wait_ge(s_mqf, t * 2 + 2)
                act.wait_ge(s_mkf, t + 1)
                act.activation(m_x[:, p, 0, :, :], m_f[:, s, :, :], ACT.Exp, scale=1.0 / TAU).then_inc(s_msx, 1)
                for h in range(2):
                    act.activation(m_x[:, p, 1, h, :], m_e[:, s, h, :], ACT.Exp, bias=gtots[:, 2 + h, ds(t, 1)],
                                   scale=-1.0 / TAU).then_inc(s_msx, 1)
                    act.activation(m_x[:, p, 2, h, :], m_f[:, s, h, :], ACT.Exp, bias=gtots[:, h, ds(t, 1)],
                                   scale=-1.0 / TAU).then_inc(s_msx, 1)

            def decays(tile):
                t, q, s = tile
                act.wait_ge(s_mf, t * (2 * NLV) + 2 * NLV)
                act.wait_ge(s_me, t * (2 * NLV) + 2 * NLV)
                act.activation(xa[:, s % 2], xa[:, s % 2], ACT.Exp, scale=1.0 / TAU).then_inc(s_mx, 1)

            def turned(tile):
                t, q, s = tile
                act.wait_ge(s_mkt, t + 3)
                act.wait_ge(s_mc, t + 1)
                act.activation(m_kT[:, s % 2, :], PS[:, 6, 0:2 * P], ACT.Copy).then_inc(s_mkT, 1)

            def squares(tile):
                t, q, s = tile
                act.wait_ge(s_mo, t + 3)
                act.wait_ge(s_mss, t)
                act.activation(osq[:, :], PS[:, 4, :], ACT.Square).then_inc(s_mos, 1)

            def rstd(tile):
                t, q, s = tile
                act.wait_ge(s_mrb, t + 3)
                act.wait_ge(s_mog, t + 2)
                act.activation(orr[:, :], PS[:, 7, :], ACT.Copy).then_inc(s_mor, 1)

            def step(tile, last):
                turned(tile)
                if not last:
                    factors(near(tile, 1))
                rstd(near(tile, -1))
                if not last:
                    decays(near(tile, 1))
                squares(tile)
            factors((0, 0, 0))
            decays((0, 0, 0))
            turned((0, 0, 0))
            factors((1, 0, 1))
            decays((1, 0, 1))
            squares((0, 0, 0))
            main_tiles(act, step)
            rstd((NT - 1, NT // 4 - 1, 3))

        def main_dve(dve):
            dve.memset(m_st[:, 0, :, :], 0.0).then_inc(s_gm, 1)
            dve.memset(m_st[:, 1, :, :], 0.0).then_inc(s_gm, 1)
            dve.tensor_scalar(ggn[:, :], ggn[:, :], float(DK) ** -0.5, None, ALU.mult).then_inc(s_gm, 1)
            dve.wait_ge(s_gm, 8)

            def distances(tile):
                t, q, s = tile
                dve.wait_ge(s_ml[s], q * 112 + 112)
                dve.wait_ge(s_mlv, t * 4 + 4)
                for l, w in enumerate(LEVELS):
                    left, right, mid, _ = halves(m_f[:, s, :, :], w)
                    ql, qr, _, _ = halves(xa[:, s % 2, 0, l, :, :], w)
                    kl, _, _, _ = halves(xa[:, s % 2, 1, l, :, :], w)
                    dve.tensor_tensor(qr, right, mid, ALU.subtract).then_inc(s_mf, 1)
                    dve.tensor_tensor(kl, mid, left, ALU.subtract).then_inc(s_mf, 1)

            def q_states(tile):
                t, q, s = tile
                dve.wait_ge(s_msx, t * 5 + 5)
                dve.wait_ge(s_mo, t + 1)
                for d in range(2):
                    dve.tensor_tensor(qf[:, s % 2, d, :, :], m_q[:, s, :, :], m_x[:, s % 2, d, :, :], ALU.mult
                                      ).then_inc(s_mqf, 1)

            def q_levels(tile):
                t, q, s = tile
                x = xa[:, s % 2, 0, :, :, :].rearrange("p l h c -> p l (h c)")
                dve.wait_ge(s_mx, t + 1)
                dve.tensor_tensor(x, x, m_q[:, s, :, :].rearrange("p h c -> p (h c)").unsqueeze(1)
                                  .broadcast_to([P, NLV, 2 * P]), ALU.mult).then_inc(s_mq, 1)

            def matrix(tile, h):
                t, q, s = tile
                b = 2 * (h % 2)
                dve.wait_ge(s_mlv, t * 4 + h + 9)
                dve.wait_ge(s_ma, t * 4 + h + 1)
                dve.tensor_tensor(tmp_l[:, h % 2, :, :].rearrange("p l c -> p (l c)"),
                                  PS[:, b:b + 2, :].rearrange("p b c -> p (b c)"), gmask[:, :], ALU.mult
                                  ).then_inc(s_mm, 1)
                dve.wait_ge(s_mm, t * 4 + h + 3)
                dve.wait_ge(s_mo, t + 1)
                dve.tensor_reduce(attT[:, s % 2, h, :], tmp_l[:, h % 2, :, :].rearrange("p l c -> p c l"), AX, ALU.add
                                  ).then_inc(s_ma, 1)

            def state(tile):
                t, q, s = tile
                dve.wait_ge(s_mc, t + 3)
                dve.wait_ge(s_mo, t + 2)
                dve.wait_ge(s_ms, t * 4 + 4)
                state_step(dve, m_st[:, s % 2], m_st[:, 1 - s % 2], 5, 0, ds(t, 1), s_ms)

            def mean(tile):
                t, q, s = tile
                dve.wait_ge(s_mss, t + 1)
                dve.wait_ge(s_mrb, t + 1)
                dve.tensor_scalar(ocol[:, s % 2, :], PS[:, 7, 0:GH], 1.0 / (DK * DV), EPS, ALU.mult, ALU.add).then_inc(s_mrr, 1)

            def normed(tile):
                t, q, s = tile
                dve.wait_ge(s_mor, t + 3)
                dve.wait_ge(s_mst[s % 2], q * 32 + (16 * (s // 2) + 16))
                dve.scalar_tensor_tensor(og[:, s % 2, :, :].rearrange("p h c -> p (h c)"), PS[:, 4, :], ggn[:, 0:1], orr[:, :],
                                         ALU.mult, ALU.mult).then_inc(s_mog, 1)

            def step(tile, last):
                if not last:
                    distances(near(tile, 1))
                mean(near(tile, -1))
                matrix(tile, 0)
                matrix(tile, 1)
                normed(near(tile, -1))
                if not last:
                    q_states(near(tile, 1))
                    q_levels(near(tile, 1))
                matrix(tile, 2)
                matrix(tile, 3)
                state(tile)
            distances((0, 0, 0))
            q_states((0, 0, 0))
            q_levels((0, 0, 0))
            distances((1, 0, 1))
            matrix((0, 0, 0), 0)
            matrix((0, 0, 0), 1)
            q_states((1, 0, 1))
            q_levels((1, 0, 1))
            matrix((0, 0, 0), 2)
            matrix((0, 0, 0), 3)
            state((0, 0, 0))
            main_tiles(dve, step)
            mean((NT - 1, NT // 4 - 1, 3))
            normed((NT - 1, NT // 4 - 1, 3))

        def main_pool(pool):
            def distances(tile, levels):
                t, q, s = tile
                pool.wait_ge(s_ml[s], q * 112 + 112)
                pool.wait_ge(s_mlv, t * 4 + 4)
                for l in levels:
                    left, right, _, mid = halves(m_e[:, s, :, :], LEVELS[l])
                    ql, _, _, _ = halves(xa[:, s % 2, 0, l, :, :], LEVELS[l])
                    _, kr, _, _ = halves(xa[:, s % 2, 1, l, :, :], LEVELS[l])
                    pool.tensor_tensor(ql, mid, left, ALU.subtract).then_inc(s_me, 1)
                    pool.tensor_tensor(kr, right, mid, ALU.subtract).then_inc(s_me, 1)

            def k_state(tile):
                t, q, s = tile
                pool.wait_ge(s_msx, t * 5 + 5)
                pool.wait_ge(s_mkt, t + 1)
                pool.tensor_tensor(m_kf[:, s % 2, :, :], m_k[:, s, :, :], m_x[:, s % 2, 2, :, :], ALU.mult).then_inc(s_mkf, 1)

            def k_levels(tile):
                t, q, s = tile
                x = xa[:, s % 2, 1, :, :, :].rearrange("p l h c -> p l (h c)")
                pool.wait_ge(s_mx, t + 1)
                pool.tensor_tensor(x, x, m_k[:, s, :, :].rearrange("p h c -> p (h c)").unsqueeze(1)
                                   .broadcast_to([P, NLV, 2 * P]), ALU.mult).then_inc(s_mk, 1)

            def rstd(tile):
                t, q, s = tile
                pool.wait_ge(s_mrr, t * 2 + 1)
                pool.tensor_tensor(ocol[:, s % 2, :], ocol[:, s % 2, :], negh[:, 0:GH], ALU.pow).then_inc(s_mrr, 1)

            def gated(tile):
                t, q, s = tile
                pool.wait_ge(s_mog, t + 3)
                pool.tensor_tensor(og[:, s % 2, :, :], og[:, s % 2, :, :], m_z[:, s, :, :], ALU.mult).then_inc(s_mgz, 1)

            def step(tile, last):
                if not last:
                    distances(near(tile, 1), range(0, 3))
                rstd(near(tile, -1))
                if not last:
                    distances(near(tile, 1), range(3, NLV))
                    k_state(near(tile, 1))
                gated(near(tile, -1))
                if not last:
                    k_levels(near(tile, 1))
            for t in range(2):
                distances((t, 0, t), range(NLV))
                k_state((t, 0, t))
                k_levels((t, 0, t))
            main_tiles(pool, step)
            rstd((NT - 1, NT // 4 - 1, 3))
            gated((NT - 1, NT // 4 - 1, 3))

        def main_pe(pe):
            pe.wait_ge(s_bs, 4 * NT + 4)
            pe.wait_ge(s_bkT, NT + 1)
            pe.wait_ge(s_bv, NT + 1)

            def turn(tile):
                t, q, s = tile
                pe.wait_ge(s_mkf, t + 3)
                pe.wait_ge(s_mkT, t + 2)
                for p in range(2):
                    mm = pe.transpose(PS[:, 6, p * P:(p + 1) * P], m_kf[:, s % 2, p, :], ident[:, :])
                mm.then_inc(s_mkt, 1)

            def levels(tile, h):
                t, q, s = tile
                r, p, b = slice(DK * (h % 2), DK * (h % 2) + DK), h // 2, 2 * (h % 2)
                if h == 0:
                    pe.wait_ge(s_mq, t + 1)
                    pe.wait_ge(s_mk, t + 1)
                pe.wait_ge(s_mm, t * 4 + h + 1)
                for l in range(NLV + 1):
                    kk = xa[r, s % 2, 1, l, p, :] if l < NLV else m_k[r, s, p, :]
                    qq = xa[r, s % 2, 0, l, p, :] if l < NLV else m_q[r, s, p, :]
                    mm = pe.matmul(PS[:, b + l // 4, (l % 4) * P:(l % 4 + 1) * P], kk, qq, start=True, stop=True)
                mm.then_inc(s_mlv, 1)

            def contribution(tile):
                t, q, s = tile
                pe.wait_ge(s_mkT, t + 3)
                pe.wait_ge(s_ms, t * 4 + 4)
                for p in range(2):
                    mm = pe.matmul(PS[:, 5, p * 2 * DV:(p + 1) * 2 * DV], m_kT[:, s % 2, p * P:(p + 1) * P],
                                   m_v[:, s, p * 2 * DV:(p + 1) * 2 * DV], start=True, stop=True)
                mm.then_inc(s_mc, 1)

            def outputs(tile, h):
                t, q, s = tile
                o = PS[:, 4, h * P:(h + 1) * P]
                if h == 0:
                    pe.wait_ge(s_mog, t + 2)
                    pe.wait_ge(s_mqf, t * 2 + 6)
                pe.wait_ge(s_ma, t * 4 + h + 3)
                pe.matmul(o, m_v[:, s, h * DV:(h + 1) * DV], attT[:, s % 2, h, :], start=True, stop=False)
                pe.matmul(o, m_st[:, s % 2, h, :], qf[:, s % 2, 0, h // 2, :], start=False, stop=False)
                mm = pe.matmul(o, m_s[:, s, h, :], qf[:, s % 2, 1, h // 2, :], start=False, stop=True)
                if h == GH - 1:
                    mm.then_inc(s_mo, 1)

            def sums(tile):
                t, q, s = tile
                pe.wait_ge(s_mos, t + 1)
                pe.wait_ge(s_mor, t + 2)
                for h in range(GH):
                    mm = pe.matmul(PS[:, 7, h:h + 1], osq[:, h * P:(h + 1) * P], ones[:, 0:1], start=True, stop=True)
                mm.then_inc(s_mss, 1)

            def spread(tile):
                t, q, s = tile
                pe.wait_ge(s_mrr, t * 2 + 2)
                for h in range(GH):
                    mm = pe.matmul(PS[:, 7, h * P:(h + 1) * P], ocol[:, s % 2, h:h + 1].broadcast_to([P, P]), ident[:, :],
                                   start=True, stop=True)
                mm.then_inc(s_mrb, 1)

            def step(tile, last, first=False):
                if not first:
                    sums(near(tile, -1))
                levels(tile, 1)
                if not first:
                    spread(near(tile, -1))
                contribution(tile)
                levels(tile, 2)
                outputs(tile, 0)
                levels(tile, 3)
                outputs(tile, 1)
                if not last:
                    turn(near(tile, 1))
                    levels(near(tile, 1), 0)
                outputs(tile, 2)
                outputs(tile, 3)
            turn((0, 0, 0))
            levels((0, 0, 0), 0)
            step((0, 0, 0), False, first=True)
            main_tiles(pe, step)
            sums((NT - 1, NT // 4 - 1, 3))
            spread((NT - 1, NT // 4 - 1, 3))

        M0 = H0
        raw5 = at("raw5", M0 + 7 * K, [P, 5, S])
        cqh = at("cqh", M0 + 47 * K, [P, 2, S], F32R)
        cql = at("cql", M0 + 63 * K, [P, 2, S], F32R)
        ckh = at("ckh", M0 + 79 * K, [P, S], F32R)
        ckl = at("ckl", M0 + 87 * K, [P, S], F32R)
        krh = at("krh", M0 + 95 * K, [P, S], F32R)
        krl = at("krl", M0 + 103 * K, [P, S], F32R)
        wqh = at("wqh", M0 + 111 * K, [P, 2, D], F32R)
        wql = at("wql", M0 + 119 * K, [P, 2, D], F32R)
        sq3 = at("sq3", M0 + 127 * K, [P, 2, 3, 512])
        nst = at("nst", M0 + 139 * K, [P, MH, 512])
        rst = at("rst", M0 + 147 * K, [P, 2, 512])
        rsw = at("rsw", M0 + 151 * K, [P, 2, 512])
        wq = at("wq", M0 + 156 * K, [P, 2, D])
        cosT = at("cosT", M0 + 164 * K, [P, S])
        turns = at("turns", M0 + 172 * K, [P, S])
        sinT = at("sinT", M0 + 180 * K, [P, S])
        posi = at("posi", M0 + 180 * K, [P, S], I32)
        mturn = at("mturn", M0 + 156 * K, [P, S])
        wkv = at("wkv", M0 + 188 * K, [P, MH, NOPE + MV])
        wkh = at("wkh", M0 + 192 * K, [P, MH, NOPE], F32R)
        wkl = at("wkl", M0 + 194 * K, [P, MH, NOPE], F32R)
        mcol = at("mcol", M0 + 196 * K, [P, 8])
        rcol = at("rcol", M0 + 196 * K + 32, [P, NB, 8])
        kvh = [at("kvh%d" % s, M0 + 32 * s * K, [P, 2, S], F32R) for s in range(2)]
        kvl = [at("kvl%d" % s, M0 + (32 * s + 16) * K, [P, 2, S], F32R) for s in range(2)]
        pb_ = at("pb_", M0 + 111 * K, [P, 2, S])
        pth = at("pth", M0 + 127 * K, [P, NT, 2 * P], F32R)
        ptl = at("ptl", M0 + 143 * K, [P, NT, 2 * P], F32R)
        qraw = at("qraw", M0 + 164 * K, [P, 2, 2, P])
        qsl = at("qsl", M0 + 166 * K, [P, 2, 3, P], F32R)
        diag = at("diag", M0 + 169 * K, [P, 2, P])
        mzt = at("mzt", M0 + 170 * K, [P, 2 * P])
        ost = at("ost", M0 + 171 * K, [P, 2 * P])
        mx4 = at("mx4", M0 + 172 * K, [P, 2, 4])
        rs4 = at("rs4", M0 + 172 * K + 32, [P, 2, 4])
        mx1 = at("mx1", M0 + 172 * K + 64, [P, 2])
        nm = at("nm", M0 + 172 * K + 96, [P, 2])
        rsm = at("rsm", M0 + 172 * K + 128, [P, 2])
        rinv = at("rinv", M0 + 172 * K + 160, [P, 2])

        s_rot = sem("s_rot")
        s_ang = sem("s_ang")
        s_pl = sem("s_pl")
        s_pw = sem("s_pw")
        s_pwh = sem("s_pwh")
        s_psq = sem("s_psq")
        s_pss = sem("s_pss")
        s_pr = sem("s_pr")
        s_prb = sem("s_prb")
        s_pn = sem("s_pn")
        s_ph = sem("s_ph")
        s_pk = sem("s_pk")
        s_plo = sem("s_plo")
        s_qp = sem("s_qp")
        s_qa = sem("s_qa")
        s_qd = sem("s_qd")
        s_qn = sem("s_qn")
        s_qr = sem("s_qr")

        def rot_sp(sp):
            sp.dma_start(posi[:, :], a["pos"].broadcast_to([P, S])).then_inc(s_rot, 16)
            sp.dma_start(mcol[:, 0:3], a["cst"][:, C_INVF:C_N]).then_inc(s_rot, 16)
            sp.dma_start(mcol[:, 3:5], a["gq"]).then_inc(s_rot, 16)
            sp.dma_start(mcol[:, 5:6], a["gkv"]).then_inc(s_rot, 16)
            sp.dma_start(wkv[:, :, :], a["wkv"]).then_inc(s_pw, 16)

        def latents_sp(sp):
            sp.dma_start(raw5[:, 0:3, :], projT[T_CQ:T_CQ + 3].rearrange("n p c -> p n c")).then_inc(s_pl, 16)
            for k, r in ((3, 0), (4, 1)):
                for half in range(4):
                    src = O_RKR + ROPE // 2 * ((half + r) % 2)
                    sp.dma_start(raw5[half * 32:half * 32 + 32, k, :], projT[T_GA, src:src + 32, :]).then_inc(s_pl, 16)
            sp.wait_ge(s_ang, A_ALL)
            sp.dma_start(wq[:, :, :], a["wq"]).then_inc(s_pw, 16)

        A_ALL = 11

        def rot_pool(pool):
            magic = float(np.float32(1.5 * 2 ** 23))
            c1 = 6.28125
            c2 = float(np.float32(np.round((2 * np.pi - c1) * 2 ** 20) / 2 ** 20))
            c3 = float(np.float32(2 * np.pi - c1 - c2))
            lim = float(np.nextafter(np.float32(np.pi), np.float32(0)))
            pool.wait_ge(s_rot, 64)
            pool.tensor_copy(cosT[:, :], posi[:, :]).then_inc(s_ang, 1)
            pool.wait_ge(s_ang, 1)
            pool.tensor_tensor(cosT[:, :], cosT[:, :], mcol[:, 0:1].broadcast_to([P, S]), ALU.mult).then_inc(s_ang, 1)
            pool.wait_ge(s_ang, 2)
            pool.tensor_scalar(turns[:, :], cosT[:, :], float(1 / (2 * np.pi)), magic, ALU.mult, ALU.add).then_inc(s_ang, 1)
            pool.wait_ge(s_ang, 3)
            pool.tensor_scalar(turns[:, :], turns[:, :], -magic, None, ALU.add).then_inc(s_ang, 1)
            for k, c in enumerate((c1, c2, c3)):
                pool.wait_ge(s_ang, 4 + 2 * k)
                pool.tensor_scalar(mturn[:, :], turns[:, :], -c, None, ALU.mult).then_inc(s_ang, 1)
                pool.wait_ge(s_ang, 5 + 2 * k)
                pool.tensor_tensor(cosT[:, :], cosT[:, :], mturn[:, :], ALU.add).then_inc(s_ang, 1)
            pool.wait_ge(s_ang, 10)
            pool.tensor_scalar(cosT[:, :], cosT[:, :], lim, -lim, ALU.min, ALU.max).then_inc(s_ang, 1)

        def rot_act(act):
            act.wait_ge(s_ang, A_ALL)
            act.activation(sinT[:, :], cosT[:, :], ACT.Sin, scale=mcol[:, 1:2]).then_inc(s_ang, 1)
            act.activation(turns[:, :], cosT[:, :], ACT.Abs).then_inc(s_ang, 1)
            act.wait_ge(s_ang, A_ALL + 2)
            act.activation(cosT[:, :], turns[:, :], ACT.Sin, bias=mcol[:, 2:3], scale=-1.0).then_inc(s_ang, 1)

        def blk(tb):
            return slice(tb * 512, (tb + 1) * 512)

        def latents_act(act):
            act.wait_ge(s_mst[0], 8 * NT + 16)
            act.wait_ge(s_mst[1], 8 * NT + 16)
            act.wait_ge(s_pl, 144)

            def squares(tb):
                if tb >= 2:
                    act.wait_ge(s_pss, tb - 1)
                act.activation(sq3[:, tb % 2, :, :], raw5[:, 0:3, blk(tb)], ACT.Square).then_inc(s_psq, 1)

            def his(tb):
                for k, hi in enumerate((cqh[:, 0, blk(tb)], cqh[:, 1, blk(tb)], ckh[:, blk(tb)])):
                    act.wait_ge(s_pn, 3 * tb + k + 1)
                    act.activation(hi, raw5[:, k, blk(tb)], ACT.Copy).then_inc(s_ph, 1)
            squares(0)
            squares(1)
            act.wait_ge(s_pw, 32)
            act.activation(wqh[:, :, :], wq[:, :, :], ACT.Copy).then_inc(s_pwh, 1)
            act.activation(wkh[:, :, :], wkv[:, :, 0:NOPE], ACT.Copy).then_inc(s_pwh, 1)
            his(0)
            squares(2)
            his(1)
            squares(3)
            his(2)
            his(3)
            act.wait_ge(s_pk, NB + 3)
            act.activation(krh[:, :], raw5[:, 3, :], ACT.Copy).then_inc(s_ph, 1)
            for tb in range(NB):
                if tb:
                    act.wait_ge(s_qn, 64 * tb)
                for n, j in enumerate(Q_NOPE):
                    act.wait_ge(s_qp, 8 * tb + j + 1)
                    act.activation(nst[:, n, :], PS[:, j, :], ACT.Copy).then_inc(s_qa, 1)

        Q_NOPE, Q_ROT, Q_SWAP = (0, 3, 6, 7), (1, 4), (2, 5)
        Q_COL = {**{j: n for n, j in enumerate(Q_NOPE)}, **{j: 4 + n for n, j in enumerate(Q_ROT)},
                 **{j: 6 + n for n, j in enumerate(Q_SWAP)}}

        def latents_pool(pool):
            def rstd(tb):
                pool.wait_ge(s_pr, 2 * tb + 2)
                pool.tensor_tensor(rcol[:, tb, :], rcol[:, tb, :], negh[:, 0:8], ALU.pow).then_inc(s_pk, 1)
            for tb in range(NB):
                rstd(tb)
            pool.wait_ge(s_ang, A_ALL + 3)
            pool.tensor_tensor(raw5[:, 3, :], raw5[:, 3, :], cosT[:, :], ALU.mult).then_inc(s_pk, 1)
            pool.tensor_tensor(raw5[:, 4, :], raw5[:, 4, :], sinT[:, :], ALU.mult).then_inc(s_pk, 1)
            pool.wait_ge(s_pk, NB + 2)
            pool.tensor_tensor(raw5[:, 3, :], raw5[:, 3, :], raw5[:, 4, :], ALU.add).then_inc(s_pk, 1)
            pool.wait_ge(s_ph, 3 * NB + 1)
            pool.tensor_tensor(krl[:, :], raw5[:, 3, :], krh[:, :].bitcast(F32), ALU.subtract).then_inc(s_pk, 1)

        def latents_dve(dve):
            def means(tb):
                dve.wait_ge(s_pss, tb + 1)
                dve.tensor_scalar(rcol[:, tb, 0:4], PS[:, tb % 2, 0:4], 1.0 / QR, EPS, ALU.mult, ALU.add).then_inc(s_pr, 1)
                dve.tensor_scalar(rcol[:, tb, 4:8], PS[:, tb % 2, 4:8], 1.0 / KVR, EPS, ALU.mult, ALU.add).then_inc(s_pr, 1)

            def normed(tb):
                dve.wait_ge(s_prb, tb + 1)
                for k in range(3):
                    dve.scalar_tensor_tensor(raw5[:, k, blk(tb)], raw5[:, k, blk(tb)], mcol[:, 3 + k:4 + k],
                                             PS[:, 2 + 2 * (tb % 2) + k // 2, :], ALU.mult, ALU.mult).then_inc(s_pn, 1)

            def los(tb):
                for k, (hi, lo) in enumerate(((cqh[:, 0, blk(tb)], cql[:, 0, blk(tb)]),
                                              (cqh[:, 1, blk(tb)], cql[:, 1, blk(tb)]), (ckh[:, blk(tb)], ckl[:, blk(tb)]))):
                    dve.wait_ge(s_ph, 3 * tb + k + 1)
                    dve.tensor_tensor(lo, raw5[:, k, blk(tb)], hi.bitcast(F32), ALU.subtract).then_inc(s_plo, 1)
            means(0)
            means(1)
            dve.wait_ge(s_pwh, 2)
            dve.tensor_tensor(wql[:, :, :], wq[:, :, :], wqh[:, :, :].bitcast(F32), ALU.subtract).then_inc(s_pwh, 1)
            dve.tensor_tensor(wkl[:, :, :], wkv[:, :, 0:NOPE], wkh[:, :, :].bitcast(F32), ALU.subtract).then_inc(s_pwh, 1)
            normed(0)
            los(0)
            means(2)
            normed(1)
            los(1)
            means(3)
            normed(2)
            los(2)
            normed(3)
            los(3)
            dve.wait_ge(s_ang, A_ALL + 3)
            for tb in range(NB):
                if tb:
                    dve.wait_ge(s_qr, 128 * tb)
                for r in range(2):
                    n = 6 * tb + 3 * r
                    dve.wait_ge(s_qp, 8 * tb + Q_ROT[r] + 1)
                    dve.tensor_tensor(rst[:, r, :], PS[:, Q_ROT[r], :], cosT[:, blk(tb)], ALU.mult).then_inc(s_qd, 1)
                    dve.wait_ge(s_qp, 8 * tb + Q_SWAP[r] + 1)
                    if n >= 6:
                        dve.wait_ge(s_qd, n - 3)
                    dve.tensor_tensor(rsw[:, r, :], PS[:, Q_SWAP[r], :], sinT[:, blk(tb)], ALU.mult).then_inc(s_qd, 1)
                    dve.wait_ge(s_qd, n + 2)
                    dve.tensor_tensor(rst[:, r, :], rst[:, r, :], rsw[:, r, :], ALU.add).then_inc(s_qd, 1)

        def latents_pe(pe):
            pe.wait_ge(s_mog, NT + 2)
            pe.wait_ge(s_mm, GH * NT + 2)

            def sums(tb):
                pe.wait_ge(s_psq, tb + 1)
                if tb >= 2:
                    pe.wait_ge(s_pr, 2 * (tb - 2) + 2)
                for t in range(4):
                    tok = slice(t * P, (t + 1) * P)
                    for k in range(2):
                        pe.matmul(PS[:, tb % 2, t:t + 1], sq3[:, tb % 2, k, tok], ones[:, 0:1], start=(k == 0), stop=(k == 1))
                    mm = pe.matmul(PS[:, tb % 2, 4 + t:5 + t], sq3[:, tb % 2, 2, tok], ones[:, 0:1], start=True, stop=True)
                mm.then_inc(s_pss, 1)

            def spread(tb):
                pe.wait_ge(s_pk, tb + 1)
                if tb >= 2:
                    pe.wait_ge(s_pn, 3 * (tb - 2) + 3)
                for c in range(8):
                    mm = pe.matmul(PS[:, 2 + 2 * (tb % 2) + c // 4, (c % 4) * P:(c % 4 + 1) * P],
                                   rcol[:, tb, c:c + 1].broadcast_to([P, P]), ident[:, :], start=True, stop=True)
                mm.then_inc(s_prb, 1)
            sums(0)
            sums(1)
            spread(0)
            sums(2)
            spread(1)
            sums(3)
            spread(2)
            spread(3)
            pe.wait_ge(s_pwh, 4)
            pe.wait_ge(s_pr, 2 * NB)
            for tb in range(NB):
                pe.wait_ge(s_plo, 3 * tb + 2)
                for j in range(8):
                    if tb == 0 and 2 <= j < 6:
                        pe.wait_ge(s_pn, 3 * (2 + j // 4) + 3)
                    if tb and j in Q_NOPE:
                        pe.wait_ge(s_qa, 4 * (tb - 1) + Q_COL[j] + 1)
                    if tb and j not in Q_NOPE:
                        pe.wait_ge(s_qd, 6 * (tb - 1) + 3 * (j // 3) + j % 3)
                    c = slice(Q_COL[j] * P, (Q_COL[j] + 1) * P)
                    for k in range(2):
                        pe.matmul(PS[:, j, :], wqh[:, k, c], cqh[:, k, blk(tb)], start=(k == 0), stop=False)
                        pe.matmul(PS[:, j, :], wqh[:, k, c], cql[:, k, blk(tb)], start=False, stop=False)
                        mm = pe.matmul(PS[:, j, :], wql[:, k, c], cqh[:, k, blk(tb)], start=False, stop=(k == 1))
                    mm.then_inc(s_qp, 1)

        def queries_sp(sp):
            for tb in range(NB):
                for j in range(8):
                    if j in Q_NOPE:
                        n = Q_COL[j]
                        sp.wait_ge(s_qa, 4 * tb + n + 1)
                        sp.dma_start(q_all[n * NT + 4 * tb:n * NT + 4 * tb + 4, :, 0, :].rearrange("t p q -> p t q"),
                                     nst[:, n, :].rearrange("p (t q) -> p t q", t=4)).then_inc(s_qn, 16)
                    if j in Q_SWAP:
                        r = Q_SWAP.index(j)
                        sp.wait_ge(s_qd, 6 * tb + 3 * r + 3)
                        for h in range(2):
                            t0 = (2 * r + h) * NT + 4 * tb
                            for half in range(2):
                                sp.dma_start(q_all[t0:t0 + 4, half * ROPE:(half + 1) * ROPE, 1, :].rearrange("t p q -> p t q"),
                                             rst[h * ROPE:(h + 1) * ROPE, r, :].rearrange("p (t q) -> p t q", t=4)
                                             ).then_inc(s_qr, 16)

        s_kp = sem("s_kp")
        s_kh = sem("s_kh")
        s_kl = sem("s_kl")

        def piece_pe(pe, h, n, bank):
            if bank == 7 and 8 * h + n > 8:
                pe.wait_ge(s_kl, 8 * h + n)
            if n < 4:
                pe.matmul(PS[:, bank, :], wkh[:, h, :], ckh[:, blk(n)], start=True, stop=False)
                pe.matmul(PS[:, bank, :], wkh[:, h, :], ckl[:, blk(n)], start=False, stop=False)
                mm = pe.matmul(PS[:, bank, :], wkl[:, h, :], ckh[:, blk(n)], start=False, stop=True)
            else:
                for t in range(4):
                    tok, o = slice((4 * n - 16 + t) * P, (4 * n - 15 + t) * P), PS[:, bank, t * P:(t + 1) * P]
                    pe.matmul(o, ckh[:, tok].bitcast(F32), wkv[:, h, NOPE:], start=True, stop=False)
                    mm = pe.matmul(o, ckl[:, tok].bitcast(F32), wkv[:, h, NOPE:], start=False, stop=True)
            mm.then_inc(s_kp, 1)

        def piece_at(part, h, n):
            return part[h % 2][:, n // 4, blk(n % 4)]

        def piece_act(act, h, n, bank):
            act.wait_ge(s_kp, 8 * h + n + 1)
            act.activation(piece_at(kvh, h, n), PS[:, bank, :], ACT.Copy).then_inc(s_kh, 1)

        def piece_dve(dve, h, n, bank):
            dve.wait_ge(s_kh, 8 * h + n + 1)
            dve.tensor_tensor(piece_at(kvl, h, n), PS[:, bank, :], piece_at(kvh, h, n).bitcast(F32), ALU.subtract
                              ).then_inc(s_kl, 1)

        s_qi = [sem("s_qi0"), sem("s_qi1")]
        s_q = sem("s_q")
        s_S = sem("s_S")
        s_nm = sem("s_nm")
        s_exp = sem("s_exp")
        s_rinv = sem("s_rinv")
        s_dg = sem("s_dg")
        s_T = sem("s_T")
        s_hi = sem("s_hi")
        s_lo = sem("s_lo")
        s_O = sem("s_O")
        s_oe = sem("s_oe")
        s_mlg = sem("s_mlg")
        s_ast = sem("s_ast")
        NP_ = NT // 2

        def heads(eng, step):
            for h in range(MH):
                step(h, 0, False)
                if h < MH - 1:
                    step(h, 1, True)
                with eng.Fori(2 if h < MH - 1 else 1, NP_) as i:
                    step(h, i, False)

        def attn_pe(pe):
            def scores(h, N, u, banks):
                kh, kl = kvh[h % 2][:, 0, :], kvl[h % 2][:, 0, :]
                pe.wait_ge(s_q, N * 3 + 9)
                for b in banks:
                    pe.wait_ge(s_exp, N * 4 + b + 1)
                    o, c = PS[:, b, :], blk(b)
                    pe.matmul(o, qsl[:, u, 0, :], kh[:, c], start=True, stop=False)
                    pe.matmul(o, qsl[:, u, 0, :], kl[:, c], start=False, stop=False)
                    pe.matmul(o, qsl[:, u, 1, :], kh[:, c], start=False, stop=False)
                    pe.matmul(o, qsl[:, u, 2, :], krh[:, c], start=False, stop=False)
                    pe.matmul(o, qsl[:, u, 2, :], krl[:, c], start=False, stop=True).then_inc(s_S, 1)

            def turn(N, u, c):
                pe.wait_ge(s_dg, N + 1)
                pe.wait_ge(s_exp, N * 4 + c + 5)
                pe.wait_ge(s_lo, N * 4 + c + 1)
                for j in range(4):
                    mm = pe.matmul(PS[:, 4 + c % 2, j * P:(j + 1) * P], pb_[:, u, (4 * c + j) * P:(4 * c + j + 1) * P],
                                   diag[:, u, :], start=True, stop=True)
                mm.then_inc(s_T, 1)

            def values(h, I, half):
                vh, vl = kvh[h % 2][:, 1, :], kvl[h % 2][:, 1, :]
                if half == 0:
                    pe.wait_ge(s_oe, I + 1)
                for c in (2 * half, 2 * half + 1):
                    pe.wait_ge(s_lo, I * 8 + 4 + c + 3)
                    for k in range(4 * c, 4 * c + 4):
                        o, tok = PS[:, 6, 0:2 * P], slice(k * P, (k + 1) * P)
                        pe.matmul(o, vh[:, tok], pth[:, k, :], start=(k == 0), stop=False)
                        pe.matmul(o, vh[:, tok], ptl[:, k, :], start=False, stop=False)
                        mm = pe.matmul(o, vl[:, tok], pth[:, k, :], start=False, stop=(k == NT - 1))
                mm.then_inc(s_O, 1)

            def step(h, i, fill):
                I = i + h * NP_
                first = isinstance(i, int) and i == 0
                for u in range(2):
                    N = i * 2 + (h * NT + u)
                    turned = not (h == 0 and first and u == 0)
                    before = not (h == 0 and first)
                    hb = h - 1 if first else h

                    def piece(n):
                        if fill:
                            piece_pe(pe, h + 1, 4 * u + n, 7)
                    for b in range(2):
                        scores(h, N, u, (b,))
                        if turned:
                            turn(N - 1, 1 - u, b)
                    piece(0)
                    scores(h, N, u, (2, 3))
                    piece(1)
                    if before:
                        values(hb, I - 1, u)
                    piece(2)
                    if turned:
                        turn(N - 1, 1 - u, 2)
                        turn(N - 1, 1 - u, 3)
                    piece(3)
            pe.wait_ge(s_qa, 4 * NB)
            pe.wait_ge(s_qd, 6 * NB)
            for n in range(8):
                piece_pe(pe, 0, n, n)
            pe.wait_ge(s_kl, 8)
            pe.wait_ge(s_pk, NB + 4)
            heads(pe, step)
            for c in range(4):
                turn(MH * NT - 1, 1, c)
                if c % 2:
                    values(MH - 1, MH * NP_ - 1, c // 2)

        def attn_act(act):
            def exps(N, u, b):
                if b == 0:
                    act.wait_ge(s_nm, N * 6 + 6)
                    act.wait_ge(s_T, N * 4 + 4)
                act.activation(pb_[:, u, blk(b)], PS[:, b, :], ACT.Exp, bias=nm[:, u:u + 1],
                               scale=SM_SCALE, accum_out=rs4[:, u, b:b + 1]).then_inc(s_exp, 1)

            def his(N, J, u, c):
                act.wait_ge(s_T, N * 4 + c + 9)
                act.wait_ge(s_O, J * 2 + (1 if u == 0 and c < 2 else 2))
                act.activation(pth[:, 4 * c:4 * c + 4, u * P:(u + 1) * P], PS[:, 4 + c % 2, :].rearrange("p (k q) -> p k q", k=4),
                               ACT.Copy).then_inc(s_hi, 1)

            def step(h, i, fill):
                I = i + h * NP_
                for u in range(2):
                    N = i * 2 + (h * NT + u)
                    turned = not (h == 0 and isinstance(i, int) and i == 0 and u == 0)

                    def piece(n):
                        if fill:
                            piece_act(act, h + 1, 4 * u + n, 7)

                    def his2(chunks):
                        if turned:
                            for c in chunks:
                                his(N - 1, I - 1 + u, 1 - u, c)
                    his2((0, 1))
                    piece(0)
                    piece(1)
                    for b in range(4):
                        exps(N, u, b)
                    piece(2)
                    his2((2, 3))
                    piece(3)
            act.wait_ge(s_qa, 4 * NB)
            act.wait_ge(s_pk, NB + 4)
            act.wait_ge(s_plo, 3 * NB)
            for n in range(8):
                piece_act(act, 0, n, n)
            heads(act, step)
            for c in range(4):
                his(MH * NT - 1, MH * NP_ - 1, 1, c)

        def attn_dve(dve):
            def maximum(N, u, b):
                dve.wait_ge(s_S, N * 4 + b + 9)
                dve.tensor_reduce(mx4[:, u, b:b + 1], PS[:, b, :], AX, ALU.max).then_inc(s_nm, 1)
                if b == 3:
                    dve.wait_ge(s_nm, N * 6 + 4)
                    dve.tensor_reduce(mx1[:, u:u + 1], mx4[:, u, :], AX, ALU.max).then_inc(s_nm, 1)
                    dve.wait_ge(s_nm, N * 6 + 5)
                    dve.tensor_scalar(nm[:, u:u + 1], mx1[:, u:u + 1], -SM_SCALE, None, ALU.mult).then_inc(s_nm, 1)

            def sums(N, u):
                dve.wait_ge(s_exp, N * 4 + 8)
                dve.tensor_reduce(rsm[:, u:u + 1], rs4[:, u, :], AX, ALU.add).then_inc(s_rinv, 1)
                dve.wait_ge(s_rinv, N * 2 + 1)
                dve.reciprocal(rinv[:, u:u + 1], rsm[:, u:u + 1]).then_inc(s_rinv, 1)

            def los(N, u, c):
                dve.wait_ge(s_hi, N * 4 + c + 1)
                o = slice(4 * c, 4 * c + 4), slice(u * P, (u + 1) * P)
                dve.tensor_tensor(ptl[:, o[0], o[1]], PS[:, 4 + c % 2, :].rearrange("p (k q) -> p k q", k=4),
                                  pth[:, o[0], o[1]].bitcast(F32), ALU.subtract).then_inc(s_lo, 1)

            def outs(I):
                dve.wait_ge(s_O, I * 2 + 4)
                dve.wait_ge(s_mlg, I * 16 + 16)
                dve.wait_ge(s_ast, I * 16 + 16)
                dve.tensor_tensor(ost[:, :], PS[:, 6, 0:2 * P], mzt[:, :], ALU.mult).then_inc(s_oe, 1)

            def step(h, i, fill):
                I = i + h * NP_
                for u in range(2):
                    N = i * 2 + (h * NT + u)
                    first = h == 0 and isinstance(i, int) and i == 0

                    def piece(n):
                        if fill:
                            piece_dve(dve, h + 1, 4 * u + n, 7)

                    def lo(c):
                        if not (first and u == 0):
                            los(N - 1, 1 - u, c)
                    maximum(N, u, 0)
                    lo(0)
                    maximum(N, u, 1)
                    lo(1)
                    piece(0)
                    maximum(N, u, 2)
                    maximum(N, u, 3)
                    piece(1)
                    if u and not first:
                        outs(I - 1)
                    piece(2)
                    sums(N, u)
                    lo(2)
                    lo(3)
                    piece(3)
            dve.wait_ge(s_pk, NB + 4)
            for n in range(8):
                piece_dve(dve, 0, n, n)
            heads(dve, step)
            for c in range(4):
                los(MH * NT - 1, 1, c)
            outs(MH * NP_ - 1)

        def attn_pool(pool):
            def split(N, I, u):
                pool.wait_ge(s_qi[u], I * 16 + 16)
                pool.wait_ge(s_S, N * 4 + 4)
                pool.tensor_tensor(qsl[:, u, 0:3:2, :], qraw[:, u, :, :],
                                   zero[:, 0:1].unsqueeze(1).broadcast_to([P, 2, P]), ALU.add).then_inc(s_q, 1)
                pool.wait_ge(s_q, N * 3 + 7)
                pool.tensor_tensor(qsl[:, u, 1, :], qraw[:, u, 0, :], qsl[:, u, 0, :].bitcast(F32), ALU.subtract).then_inc(s_q, 1)
                pool.wait_ge(s_q, N * 3 + 8)
                pool.tensor_tensor(qsl[ROPE:P, u, 2, :], qraw[ROPE:P, u, 1, :], qsl[ROPE:P, u, 2, :].bitcast(F32), ALU.subtract
                                   ).then_inc(s_q, 1)
                pool.wait_ge(s_q, N * 3 + 9)

            def diagonal(N, u):
                pool.wait_ge(s_rinv, N * 2 + 2)
                pool.wait_ge(s_T, N * 4 + 4)
                pool.tensor_tensor(diag[:, u, :], ident[:, :], rinv[:, u:u + 1].broadcast_to([P, P]), ALU.mult).then_inc(s_dg, 1)

            split(0, 0, 0)
            split(1, 0, 1)
            with pool.Fori(0, MH * NP_ - 1) as I:
                for u in range(2):
                    diagonal(I * 2 + u, u)
                    split(I * 2 + 2 + u, I + 1, u)
            for u in range(2):
                diagonal(MH * NT - 2 + u, u)

        def attn_sp(sp):
            sp.wait_ge(s_qn, 64 * NB)
            sp.wait_ge(s_qr, 128 * NB)

            def query(N, u):
                sp.wait_ge(s_q, N * 3 + 3)
                sp.dma_start(qraw[:, u, :, :], q_all[ds(N, 1), :, :, :].rearrange("a p w q -> (a p) w q")).then_inc(s_qi[u], 16)

            def gates(h, i, I):
                sp.wait_ge(s_oe, I + 1)
                sp.dma_start(mzt[:, :], projT[h * 2 + T_MZ, :, ds(i * (2 * P), 2 * P)]
                             ).then_inc(s_mlg, 16)

            def store(h, i, I):
                sp.wait_ge(s_oe, I + 2)
                sp.dma_start(mixT[h + GH, :, ds(i * (2 * P), 2 * P)], ost[:, :]
                             ).then_inc(s_ast, 16)

            def step(h, i, last):
                I = i + h * NP_
                if not last:
                    for u in range(2):
                        query(I * 2 + 2 + u, u)
                if not isinstance(i, int) or i:
                    store(h, i - 1, I - 1)
                elif h:
                    store(h - 1, NP_ - 1, I - 1)
                gates(h, i, I)
            for u in range(2):
                query(u, u)
            for h in range(MH):
                step(h, 0, False)
                with sp.Fori(1, NP_ - (h == MH - 1)) as i:
                    step(h, i, False)
            step(MH - 1, NP_ - 1, True)

            def last_store():
                store(MH - 1, NP_ - 1, MH * NP_ - 1)
                sp.wait_ge(s_ast, 16 * MH * NP_ + 16)
            return last_store

        OK = (KD, CT)
        O_G = 4
        OF = (2, 1)
        OX = (H0 + 64 * K, X0)
        OL = (24, 32)
        O_W = [dict(h=at("ow_h%d" % l, H0, [P, OK[l], D], F32R), lo=at("ow_l%d" % l, H0 + OK[l] * 4 * K, [P, OK[l], D], F32R),
                    f=at("of_%d" % l, OX[l], [P, OF[l], OK[l], P]), fh=at("of_h%d" % l, OX[l] + 8 * K, [P, 2, OK[l], P], F32R),
                    fl=at("of_l%d" % l, OX[l] + OL[l] * K, [P, 2, OK[l], P], F32R),
                    gh=at("og_h%d" % l, OX[l] + (OL[l] + 8) * K, [P, 2, 512], F32R),
                    gl=at("og_l%d" % l, OX[l] + (OL[l] + 12) * K, [P, 2, 512], F32R),
                    x=at("oxt%d" % l, OX[l] + (40, 48)[l] * K, [P, 2, D]),
                    y=at("oy%d" % l, X0 + (8, 56)[l] * K, [P, 2, D]),
                    wr=at("owr%d" % l, X0 + (46, 24)[l] * K, [P, 2, D]),
                    gr=at("ogr%d" % l, X0 + (54, 64)[l] * K, [P, 2, 512])) for l in range(2)]
        ors = small[:, 48:50]
        ossq = small[:, 50:52]

        s_owr = [sem("s_owr0"), sem("s_owr1")]
        s_owh = sem("s_owh")
        s_owl = sem("s_owl")
        s_of = [sem("s_of0"), sem("s_of1")]
        s_ox = [sem("s_ox0"), sem("s_ox1")]
        s_ofh = sem("s_ofh")
        s_ofl = sem("s_ofl")
        s_ok = sem("s_ok")
        s_om = sem("s_om")
        s_osq = sem("s_osq")
        s_or = sem("s_or")
        s_oz = sem("s_oz")
        s_ost = [sem("s_ost0"), sem("s_ost1")]

        def o_c(l, k):
            return OK[0] * l + k

        def o_f(l, t):
            return (OK[0] + NT - O_G) * l + OK[l] + t - O_G

        def tile_loop(eng, step, last=NT):
            with eng.Fori(O_G // 2 + 1, last // 2) as i:
                for u in range(2):
                    step(i * 2 + u, i, u)

        def out_sp(sp, l, out, between=None, before=None):
            feat, res, w, o = (mixT, sgT)[l], (a["x"], x1)[l], a[("woe", "woo")[l]], O_W[l]
            for k in range(2):
                sp.dma_start(o["wr"][:, k, :], w[k]).then_inc(s_owr[k], 16)
            for k in range(OK[l]):
                c = o_c(l, k)
                if k == 2 and before:
                    before()
                if k >= 2:
                    sp.wait_ge(s_owl, c - 1)
                    sp.wait_ge(s_ofl, o_f(l, O_G) - OK[l] + k - 1)
                    sp.dma_start(o["wr"][:, c % 2, :], w[k]).then_inc(s_owr[c % 2], 16)
                if l:
                    sp.wait_ge(s_ust, 16 * k + 17)
                sp.dma_start(o["gr"][:, c % 2, :], feat[k, :, 0:512]).then_inc(s_owr[c % 2], 16)

            def load_f(t, u):
                sp.wait_ge(s_ofl, o_f(l, t) + 1 - OF[l])
                sp.dma_start(o["f"][:, u % OF[l], :, :], feat[:, :, ds(t * P, P)].rearrange("k p c -> p k c")
                             ).then_inc(s_of[u], 16)

            def load_x(t, u):
                sp.wait_ge(s_oz, (NT * l + t) * 2 + 2)
                sp.dma_start(o["x"][:, u, :], res[ds(t * P, P), :]).then_inc(s_ox[u], 16)

            def store(t, u):
                sp.wait_ge(s_oz, (NT * l + t) * 2 + 6)
                sp.dma_start(out[ds(t * P, P), :], o["y"][:, u, :]).then_inc(s_ost[u], 16)

            def step(t, i, u):
                if not isinstance(t, int) or t < NT - 1:
                    load_f(t + 1, 1 - u)
                store(t - 2, u)
                load_x(t, u)
            load_f(4, 0)
            load_x(0, 0)
            load_x(1, 1)
            load_f(5, 1)
            for t in range(O_G):
                store(t, t % 2)
                load_x(t + 2, t % 2)
                if t == 1:
                    load_f(6, 0)
            tile_loop(sp, step, NT - 4)
            for t in range(NT - 4, NT):
                step(t, t // 2, t % 2)
                if between and t in (NT - 4, NT - 1):
                    between(t == NT - 1)
            for t in (NT - 2, NT - 1):
                store(t, t % 2)

        def out_act(act, l, between=None):
            o = O_W[l]
            for k in range(OK[l]):
                c = o_c(l, k)
                act.wait_ge(s_owr[c % 2], 32 * (c // 2 + 1))
                act.activation(o["h"][:, k, :], o["wr"][:, c % 2, :], ACT.Copy).then_inc(s_owh, 1)
                if k >= 2:
                    act.wait_ge(s_ok, c - 1)
                act.activation(o["gh"][:, c % 2, :], o["gr"][:, c % 2, :], ACT.Copy).then_inc(s_ofh, 1)

            def split(t, i, u):
                act.wait_ge(s_of[u], (6 * l + i - 1) * 16)
                if isinstance(t, int) and t < O_G + 2:
                    if t == O_G + 1:
                        act.wait_ge(s_ok, o_c(l, OK[l]))
                else:
                    act.wait_ge(s_om, NT * l + t - 1)
                act.activation(o["fh"][:, u, :, :], o["f"][:, u % OF[l], :, :], ACT.Copy).then_inc(s_ofh, 1)

            def squares(t, i, u, bank=None):
                act.wait_ge(s_om, NT * l + t + 1)
                if l or not isinstance(t, int) or t >= 2:
                    act.wait_ge(s_ost[u], (i + NT // 2 * l) * 16)
                b = 4 * u if bank is None else bank
                act.activation(o["y"][:, u, :], PS[:, b:b + 2, :].rearrange("p b f -> p (b f)"), ACT.Square,
                               scale=D ** -0.5, accum_out=ossq[:, u:u + 1]).then_inc(s_osq, 1)

            def step(t, i, u):
                split(t, i, u)
                squares(t - 2, i - 1, u)
            split(4, 2, 0)
            squares(0, 0, 0, 0)
            squares(1, 0, 1, 2)
            split(5, 2, 1)
            squares(2, 1, 0, 4)
            squares(3, 1, 1, 6)
            tile_loop(act, step)
            if between:
                between()
            squares(NT - 2, NT // 2 - 1, 0)
            squares(NT - 1, NT // 2 - 1, 1)

        def out_pool(pool, l, between=None):
            o = O_W[l]
            for k in range(OK[l]):
                c = o_c(l, k)
                pool.wait_ge(s_ofh, o_f(l, O_G) - OK[l] + k + 1)
                pool.tensor_tensor(o["gl"][:, c % 2, :], o["gr"][:, c % 2, :], o["gh"][:, c % 2, :].bitcast(F32),
                                   ALU.subtract).then_inc(s_ofl, 1)

            def split(t, i, u):
                pool.wait_ge(s_ofh, o_f(l, t) + 1)
                pool.tensor_tensor(o["fl"][:, u, :, :], o["f"][:, u % OF[l], :, :], o["fh"][:, u, :, :].bitcast(F32),
                                   ALU.subtract).then_inc(s_ofl, 1)

            def rstd(t, i, u):
                n = NT * l + t
                pool.wait_ge(s_osq, n + 1)
                pool.tensor_tensor(ors[:, u:u + 1], ossq[:, u:u + 1], eps, ALU.add).then_inc(s_or, 1)
                pool.wait_ge(s_or, n * 2 + 1)
                pool.tensor_tensor(ors[:, u:u + 1], ors[:, u:u + 1], negh[:, 0:1], ALU.pow).then_inc(s_or, 1)

            def step(t, i, u):
                split(t, i, u)
                rstd(t - 2, i - 1, u)
            split(4, 2, 0)
            rstd(0, 0, 0)
            rstd(1, 0, 1)
            split(5, 2, 1)
            rstd(2, 1, 0)
            rstd(3, 1, 1)
            tile_loop(pool, step)
            if between:
                between()
            rstd(NT - 2, NT // 2 - 1, 0)
            rstd(NT - 1, NT // 2 - 1, 1)

        def out_dve(dve, l, between=None):
            o = O_W[l]
            for k in range(OK[l]):
                c = o_c(l, k)
                dve.wait_ge(s_owh, c + 1)
                dve.tensor_tensor(o["lo"][:, k, :], o["wr"][:, c % 2, :], o["h"][:, k, :].bitcast(F32), ALU.subtract
                                  ).then_inc(s_owl, 1)

            def tile(t, i, u, bank=None):
                n, b = NT * l + t, 4 * u if bank is None else bank
                dve.wait_ge(s_or, n * 2 + 2)
                dve.scalar_tensor_tensor(o["y"][:, u, :], PS[:, b:b + 2, :].rearrange("p b f -> p (b f)"),
                                         ors[:, u:u + 1], gate[:, l, :], ALU.mult, ALU.mult).then_inc(s_oz, 1)
                dve.wait_ge(s_oz, n * 2 + 5)
                dve.wait_ge(s_ox[u], (i + NT // 2 * l) * 16 + 16)
                dve.tensor_tensor(o["y"][:, u, :], o["y"][:, u, :], o["x"][:, u, :], ALU.add).then_inc(s_oz, 1)
            for t in range(O_G):
                tile(t, t // 2, t % 2, 2 * t)
            with dve.Fori(O_G // 2, NT // 2 - 1) as i:
                for u in range(2):
                    tile(i * 2 + u, i, u)
            if between:
                between()
            tile(NT - 2, NT // 2 - 1, 0)
            tile(NT - 1, NT // 2 - 1, 1)

        def out_pe(pe, l):
            w = O_W[l]
            for k in range(OK[l]):
                c = o_c(l, k)
                pe.wait_ge(s_owl, c + 1)
                pe.wait_ge(s_ofl, o_f(l, O_G) - OK[l] + k + 1)
                for t in range(O_G):
                    tok = slice(t * P, (t + 1) * P)
                    for half in range(2):
                        o, f = PS[:, 2 * t + half, :], slice(half * 512, half * 512 + 512)
                        pe.matmul(o, w["gh"][:, c % 2, tok], w["h"][:, k, f], start=(k == 0), stop=False)
                        pe.matmul(o, w["gh"][:, c % 2, tok], w["lo"][:, k, f], start=False, stop=False)
                        mm = pe.matmul(o, w["gl"][:, c % 2, tok], w["h"][:, k, f], start=False, stop=(k == OK[l] - 1))
                    if k == OK[l] - 1:
                        mm.then_inc(s_om, 1)
                if k < OK[l] - 1:
                    mm.then_inc(s_ok, 1)
            pe.wait_ge(s_om, NT * l + O_G)
            pe.sem_inc(s_ok, 1)

            def tile(t, u):
                n = NT * l + t
                pe.wait_ge(s_ofl, o_f(l, t) + 1)
                if isinstance(t, int):
                    pe.wait_ge(s_oz, (NT * l + 2 * u) * 2 + 6)
                else:
                    pe.wait_ge(s_oz, n * 2 + 2)
                for k in range(OK[l]):
                    for half in range(2):
                        o, c = PS[:, 4 * u + half, :], slice(half * 512, half * 512 + 512)
                        pe.matmul(o, w["fh"][:, u, k, :], w["h"][:, k, c], start=(k == 0), stop=False)
                        pe.matmul(o, w["fh"][:, u, k, :], w["lo"][:, k, c], start=False, stop=False)
                        mm = pe.matmul(o, w["fl"][:, u, k, :], w["h"][:, k, c], start=False, stop=(k == OK[l] - 1))
                mm.then_inc(s_om, 1)
            for u in range(2):
                tile(O_G + u, u)
            with pe.Fori(O_G // 2 + 1, NT // 2) as i:
                for u in range(2):
                    tile(i * 2 + u, u)

        NV = SGW // 512
        vsr = at("vsr", X0, [P, KD, 512])
        vsh = at("vsh", X0 + 16 * K, [P, KD, 512], F32R)
        vsl = at("vsl", X0 + 32 * K, [P, KD, 512], F32R)
        vev = at("vev", X0 + 48 * K, [P, 4, 512])
        vst = at("vst", X0 + 56 * K, [P, NT, NV, 6])
        vmv = at("vmv", X0 + 66 * K, [P, NT, 2])
        vrs = at("vrs", X0 + 66 * K + 128, [P, NT])
        vnm = at("vnm", X0 + 66 * K + 192, [P, NT])

        s_vr = sem("s_vr")
        s_vhi = sem("s_vhi")
        s_vlo = sem("s_vlo")
        s_vk = sem("s_vk")
        s_vp = sem("s_vp")
        s_vev = sem("s_vev")
        s_vbn = sem("s_vbn")
        s_vst = [sem("s_vst%d" % j) for j in range(4)]
        s_vs = sem("s_vs")

        def v_sp(sp):
            def load(n):
                sp.wait_ge(s_vlo, n * KD)
                sp.dma_start(vsr[:, :, :], a["wv"][ds(n, 1), :, :].rearrange("a p (k c) -> (a p) k c", k=KD)).then_inc(s_vr, 16)

            def stores(n):
                for t in range(NT):
                    sp.wait_ge(s_vev, n * NT + t + 3)
                    sp.dma_start(sg_v[t * P:(t + 1) * P, ds(n * 512, 512)], vev[:, t % 4, :]).then_inc(s_vst[t % 4], 16)
            load(0)
            with sp.Fori(0, NV - 1) as n:
                load(n + 1)
                stores(n)
            stores(NV - 1)

        def v_act(act):
            def split(n):
                act.wait_ge(s_vr, n * 16 + 16)
                for k in range(KD):
                    act.wait_ge(s_vk, n * KD + k + 1)
                    act.activation(vsh[:, k, :], vsr[:, k, :], ACT.Copy).then_inc(s_vhi, 1)

            def evac(n, t):
                act.wait_ge(s_vp, n * NT + t + 1)
                act.wait_ge(s_vbn, n * NT + t + 1)
                act.wait_ge(s_vst[t % 4], n * 64 + 16 * (t // 4) + 1)
                act.activation(vev[:, t % 4, :], PS[:, t % 2, :], ACT.Gelu).then_inc(s_vev, 1)
            split(0)
            with act.Fori(0, NV - 1) as n:
                for t in range(NT - 1):
                    evac(n, t)
                split(n + 1)
                evac(n, NT - 1)
            for t in range(NT):
                evac(NV - 1, t)

        def v_dve(dve):
            def split(n):
                for k in range(KD):
                    dve.wait_ge(s_vhi, n * KD + k + 1)
                    dve.tensor_tensor(vsl[:, k, :], vsr[:, k, :], vsh[:, k, :].bitcast(F32), ALU.subtract).then_inc(s_vlo, 1)

            def stats(n, t):
                dve.wait_ge(s_vev, n * NT + t + 3)
                dve.bn_stats(vst[:, t, ds(n, 1), :].rearrange("p a s -> p (a s)"), vev[:, t % 4, :]).then_inc(s_vbn, 1)
            split(0)
            with dve.Fori(0, NV - 1) as n:
                for t in range(NT - 1):
                    stats(n, t)
                split(n + 1)
                stats(n, NT - 1)
            for t in range(NT):
                stats(NV - 1, t)
            dve.wait_ge(s_vbn, NV * NT + 4)
            for t in range(NT):
                dve.bn_aggr(vmv[:, t, :], vst[:, t, :, :].rearrange("p n s -> p (n s)")).then_inc(s_vs, 1)
            dve.wait_ge(s_vs, NT + 2)
            dve.scalar_tensor_tensor(vnm[:, :], vmv[:, :, 0], -1.0, vrs[:, :], ALU.mult, ALU.mult).then_inc(s_vs, 1)

        def v_pool(pool):
            pool.wait_ge(s_vs, NT)
            pool.tensor_scalar(vrs[:, :], vmv[:, :, 1], EPS, None, ALU.add).then_inc(s_vs, 1)
            pool.wait_ge(s_vs, NT + 1)
            pool.tensor_tensor(vrs[:, :], vrs[:, :], negh[:, 0:NT], ALU.pow).then_inc(s_vs, 1)

        def v_pe(pe):
            with pe.Fori(0, NV) as n:
                for t in range(NT):
                    pe.wait_ge(s_vev, n * NT + t + 1)
                    tok, o = slice(t * P, (t + 1) * P), PS[:, t % 2, :]
                    for k in range(KD):
                        if t == 0:
                            pe.wait_ge(s_vlo, n * KD + k + 1)
                        pe.matmul(o, hTh[:, k, tok], vsh[:, k, :], start=(k == 0), stop=False)
                        pe.matmul(o, hTh[:, k, tok], vsl[:, k, :], start=False, stop=False)
                        mm = pe.matmul(o, hTl[:, k, tok], vsh[:, k, :], start=False, stop=(k == KD - 1))
                        if t == NT - 1:
                            if k < KD - 1:
                                mm.then_inc(s_vk, 1)
                            else:
                                mm.then_inc(s_vp, 1)
                        elif k == KD - 1:
                            mm.then_inc(s_vp, 1)
                pe.wait_ge(s_vp, n * NT + NT)
                pe.sem_inc(s_vk, 1)

        uT = at("uT", X0 + 48 * K, [P, S])
        mT = at("mT", X0 + 56 * K, [P, S])
        zT = at("zT", X0, [P, 2, 512])
        vm = at("vm", X0 + 4 * K, [P, NT, P])
        sw = at("sw", X0 + 12 * K, [P, SG_G * P])
        srow = at("srow", X0 + 16 * K, [P, SG_G * P])
        sbs = at("sbs", X0 + 20 * K, [P, SG_G * P])
        sbias = at("sbias", X0 + 64 * K, [P, P])
        sgg = at("sgg", X0 + 65 * K, [P, CT])
        sgb = at("sgb", X0 + 65 * K + 64, [P, CT])

        s_uc = sem("s_uc")
        s_us = sem("s_us")
        s_uv = sem("s_uv")
        s_uvn = sem("s_uvn")
        s_uu = sem("s_uu")
        s_uz = sem("s_uz")
        s_um = sem("s_um")
        s_ub = sem("s_ub")
        s_ume = sem("s_ume")
        s_umu = sem("s_umu")
        s_umz = sem("s_umz")
        s_ust = sem("s_ust")

        def uz_sp(sp):
            for j in range(4):
                sp.wait_ge(s_vst[j], 16 * NV * NT // 4 + 1)
            sp.wait_ge(s_vp, NV * NT)
            for dst, src in ((sw[:, :], a["sgw"]), (sbs[:, :], a["sgbs"].broadcast_to([P, SG_G * P])),
                             (sgg[:, :], a["sgg"]), (sgb[:, :], a["sgb"])):
                sp.dma_start(dst, src).then_inc(s_uc, 16)
            for s in range(2):
                tile_load(sp, "wuz", N_TILES + s, 0, s)

            def load_v(c):
                sp.wait_ge(s_um, c * 4)
                sp.dma_start(vm[:, :, :], sg_v[:, ds(c * P, P)].rearrange("(t p) c -> p t c", p=P)).then_inc(s_uv, 16)

            def store(c):
                sp.wait_ge(s_umz, c * 4 + 6)
                sp.dma_start(sgT[ds(c, 1), :, :].rearrange("a p f -> p (a f)"), mT[:, :]).then_inc(s_ust, 16)
            load_v(0)
            with sp.Fori(0, CT - 1) as c:
                tile_load(sp, "wuz", c * 2 + N_TILES + 2, c + 1, 0)
                load_v(c + 1)
                tile_load(sp, "wuz", c * 2 + N_TILES + 3, c + 1, 1)
                store(c)
            sp.wait_ge(s_wlo, N_TILES + 2 * CT + 2)
            sp.wait_ge(s_ume, 4 * CT + 4)
            return lambda: store(CT - 1)

        def uz_pool(pool):
            with pool.Fori(0, CT) as c:
                tile_split(pool, c * 2 + N_TILES, c + NPAIR, 0)
                tile_split(pool, c * 2 + N_TILES + 1, c + NPAIR, 1)

        def uz_act(act):
            act.wait_ge(s_vs, NT + 3)
            with act.Fori(0, CT) as c:
                act.wait_ge(s_uv, c * 16 + 16)
                for t in range(NT):
                    act.activation(vm[:, t, :], vm[:, t, :], ACT.Identity, bias=vnm[:, t:t + 1], scale=vrs[:, t:t + 1]
                                   ).then_inc(s_uvn, 1)
                for tb in range(NB):
                    act.wait_ge(s_pb, c * 8 + 4 * N_TILES + tb + 9)
                    act.wait_ge(s_umu, c * 4 + 1)
                    act.activation(uT[:, tb * 512:(tb + 1) * 512], PS[:, tb, :], ACT.Gelu).then_inc(s_uu, 1)
                for tb in range(NB):
                    act.wait_ge(s_pb, c * 8 + 4 * N_TILES + 4 + tb + 9)
                    act.wait_ge(s_umz, c * 4 + tb + 1)
                    act.activation(zT[:, tb % 2, :], PS[:, tb, :], ACT.Silu).then_inc(s_uz, 1)

        def uz_dve(dve):
            dve.wait_ge(s_us, 1)
            dve.tensor_copy(srow[:, :], PS[:, 4:6, :].rearrange("p b f -> p (b f)")).then_inc(s_us, 1)
            dve.wait_ge(s_us, 2)
            dve.wait_ge(s_uc, 64)
            with dve.Fori(0, CT // 2) as grp:
                for half in range(2):
                    c = grp * 2 + half
                    g = ds(grp * P, P)
                    dve.wait_ge(s_ume, c * 4 + 4)
                    dve.scalar_tensor_tensor(sbias[:, :], srow[:, g], sgb[:, ds(c, 1)], sbs[:, g], ALU.mult, ALU.add
                                             ).then_inc(s_ub, 1)
                    dve.wait_ge(s_ub, c + 1)
                    dve.wait_ge(s_ust, c * 16 + 1)
                    for tb in range(NB):
                        b = slice(tb * 512, (tb + 1) * 512)
                        dve.wait_ge(s_um, c * 4 + tb + 1)
                        dve.scalar_tensor_tensor(mT[:, b].rearrange("p (t i) -> p t i", t=4),
                                                 PS[:, 4 + tb, :].rearrange("p (t i) -> p t i", t=4), sgg[:, ds(c, 1)],
                                                 sbias[:, :].unsqueeze(1).broadcast_to([P, 4, P]), ALU.mult, ALU.add
                                                 ).then_inc(s_ume, 1)
                    for tb in range(NB):
                        b = slice(tb * 512, (tb + 1) * 512)
                        dve.wait_ge(s_ume, c * 4 + tb + 5)
                        dve.wait_ge(s_uu, c * 4 + tb + 1)
                        dve.tensor_tensor(mT[:, b], mT[:, b], uT[:, b], ALU.mult).then_inc(s_umu, 1)
                    for tb in range(NB):
                        b = slice(tb * 512, (tb + 1) * 512)
                        dve.wait_ge(s_umu, c * 4 + tb + 1 + 1)
                        dve.wait_ge(s_uz, c * 4 + tb + 5)
                        dve.tensor_tensor(mT[:, b], mT[:, b], zT[:, tb % 2, :], ALU.mult).then_inc(s_umz, 1)

        def uz_pe(pe):
            pe.wait_ge(s_uc, 64)
            for j in range(2):
                mm = pe.matmul(PS[:, 4 + j, :], ones[:, :], sw[:, j * 512:(j + 1) * 512], start=True, stop=True)
            mm.then_inc(s_us, 1)
            pe.wait_ge(s_us, 2)
            pe.wait_ge(s_vev, NV * NT + 2)
            with pe.Fori(0, CT // 2) as grp:
                for half in range(2):
                    c = grp * 2 + half
                    pe.wait_ge(s_wlo, c * 2 + N_TILES + 3)
                    for tb in range(NB):
                        pe.wait_ge(s_uz, c * 4 + tb + 1)
                        tile_block(pe, 0, tb, tb)
                    for t in range(NT):
                        if t % 4 == 0:
                            pe.wait_ge(s_ume, c * 4 + t // 4 + 1)
                        pe.wait_ge(s_uvn, c * 16 + t + 1)
                        mm = pe.matmul(PS[:, 4 + t // 4, t % 4 * P:t % 4 * P + P], vm[:, t, :], sw[:, ds(grp * P, P)],
                                       start=True, stop=True)
                        if t % 4 == 3:
                            mm.then_inc(s_um, 1)
                    pe.wait_ge(s_wlo, c * 2 + N_TILES + 4)
                    for tb in range(NB):
                        pe.wait_ge(s_uu, c * 4 + tb + 1)
                        tile_block(pe, 1, tb, tb)

        block = ctx.enter_context(nc.Block())

        @block.sync
        def _(sp):
            sp.sem_inc(s_pst[1], 1)
            const_load(sp)
            mod_rows(sp, 0)
            norm_load(sp, 0, range(0, 2))
            for k in range(KD):
                mod_slice(sp, MOD_0, k, k)
            norm_load(sp, 0, range(2, 4))
            proj_sp(sp)
            gates_sp(sp)
            back_sp(sp)
            sp.sem_inc(s_mst[0], 16)
            sp.sem_inc(s_mst[1], 16)
            main_sp(sp)
            sp.sem_inc(s_ast, 16)
            queries_sp(sp)
            last_store = attn_sp(sp)
            out_sp(sp, 0, x1, lambda j: norm_load(sp, 1, (4 + j,)), last_store)
            norm_load(sp, 1, range(6, 8))
            for j in range(4):
                sp.sem_inc(s_vst[j], 1)
            v_sp(sp)
            sp.sem_inc(s_ust, 1)
            last_store = uz_sp(sp)
            out_sp(sp, 1, out, before=last_store)
            for u in range(2):
                sp.wait_ge(s_ost[u], 16 * NT)

        @block.gpsimd
        def _(pool):
            const_pool(pool)
            pool.sem_inc(s_wlo, 2)
            pool.wait_ge(s_set, 4)
            norm_pool_front(pool, 0)
            norm_pool_front(pool, 1)
            norm_pool(pool, 0)
            proj_pool(pool)
            pool.sem_inc(s_mkf, 2)
            rot_pool(pool)
            main_pool(pool)
            latents_pool(pool)
            pool.sem_inc(s_q, 6)
            attn_pool(pool)
            out_pool(pool, 0, lambda: (norm_pool_front(pool, 4), norm_pool_front(pool, 5)))
            norm_pool(pool, 1)
            v_pool(pool)
            uz_pool(pool)
            out_pool(pool, 1)

        @block.scalar
        def _(act):
            act.sem_inc(s_pev[0], 4)
            act.sem_inc(s_pst[0], 1)
            const_act(act)
            norm_act_front(act, 0)
            norm_act_front(act, 1)
            norm_act(act, 0)
            proj_act(act)
            act.sem_inc(s_bv, 1)
            act.sem_inc(s_bvs[0], 1)
            act.sem_inc(s_bvs[1], 1)
            act.sem_inc(s_bss[0], 1)
            act.sem_inc(s_bss[1], 1)
            gates_act(act)
            back_act(act)
            act.sem_inc(s_mkT, 2)
            act.sem_inc(s_mor, 2)
            rot_act(act)
            main_act(act)
            act.sem_inc(s_exp, 4)
            latents_act(act)
            attn_act(act)
            out_act(act, 0, lambda: (norm_act_front(act, 4), norm_act_front(act, 5)))
            norm_act(act, 1)
            act.sem_inc(s_vev, 2)
            v_act(act)
            act.sem_inc(s_uz, 4)
            uz_act(act)
            out_act(act, 1)

        @block.vector
        def _(dve):
            dve.sem_inc(s_pev[1], 4)
            mod_start(dve, 0)
            dve.wait_ge(s_csl, 1)
            dve.wait_ge(s_gp, 32)
            norm_dve_front(dve, 0)
            norm_dve_front(dve, 1)
            for k in range(KD):
                mod_sum(dve, MOD_0, k, k // 2, k)
            mod_end(dve, 0)
            norm_dve(dve, 0)
            proj_dve(dve)
            mod_end(dve, 1)
            dve.sem_inc(s_bk, 2)
            dve.sem_inc(s_bkT, 1)
            gates_dve(dve)
            back_dve(dve)
            dve.sem_inc(s_mqf, 4)
            dve.sem_inc(s_ms, 4)
            dve.sem_inc(s_mm, 2)
            dve.sem_inc(s_ma, 2)
            dve.sem_inc(s_mog, 2)
            main_dve(dve)
            dve.sem_inc(s_lo, 2)
            dve.sem_inc(s_oe, 1)
            latents_dve(dve)
            attn_dve(dve)
            dve.sem_inc(s_umu, 1)
            dve.sem_inc(s_oz, 4)
            out_dve(dve, 0, lambda: (norm_dve_front(dve, 4), norm_dve_front(dve, 5)))
            norm_dve(dve, 1)
            dve.sem_inc(s_vbn, 4)
            v_dve(dve)
            dve.sem_inc(s_ume, 4)
            dve.sem_inc(s_umz, 2)
            uz_dve(dve)
            out_dve(dve, 1)

        @block.tensor
        def _(pe):
            pe.sem_inc(s_pb, 8)
            mod_pe(pe, 0)
            norm_pe(pe, 0)
            proj_pe(pe)
            pe.wait_ge(s_pev[0], 4 * NPAIR + 4)
            pe.wait_ge(s_pev[1], 4 * NPAIR + 4)
            mod_pe(pe, 1)
            pe.sem_inc(s_bt, 2)
            gates_pe(pe)
            back_pe(pe)
            pe.sem_inc(s_mkt, 2)
            pe.sem_inc(s_mc, 2)
            pe.sem_inc(s_mlv, 8)
            pe.sem_inc(s_mo, 2)
            pe.sem_inc(s_mrb, 2)
            main_pe(pe)
            pe.sem_inc(s_S, 8)
            pe.sem_inc(s_T, 8)
            pe.sem_inc(s_O, 2)
            latents_pe(pe)
            attn_pe(pe)
            out_pe(pe, 0)
            norm_pe(pe, 1)
            pe.sem_inc(s_vk, 8)
            v_pe(pe)
            uz_pe(pe)
            out_pe(pe, 1)


def lay_out(x, c, positions, w_mod, b_mod, g_pre, g_post, w_in_e, gla_w_gate_f, gla_b_gate_f,
            gla_w_gate_b, gla_b_gate_b, gla_g_norm, mla_g_q, mla_w_uq, mla_g_kv, mla_w_ukv, w_out_e,
            w_in_o, sg_g_norm, sg_b_norm, sg_w_s, sg_b_s, w_out_o):
    f = np.float32
    c_ = np.ascontiguousarray

    def tile(w, cols):
        return w[:, cols].reshape(-1, P, len(cols)).transpose(1, 0, 2).reshape(P, -1)

    we = np.concatenate([w_in_e[0], np.zeros((D, 1), f)], axis=1)
    pad = np.full(P - 2 * RANK - ROPE, we.shape[1] - 1)
    r = np.arange
    kr = O_KR + r(ROPE)
    silu = [O_GZ + P * i + r(P) for i in range(4)] + [O_MZ + P * i + r(P) for i in range(4)]
    raw = [P * i + r(P) for i in range(8)]
    cols = [t for pair in zip(silu, raw) for t in pair]
    cols += [np.concatenate([O_GA + r(2 * RANK), kr, pad]), O_CQ + r(P), O_CQ + P + r(P), O_CKV + r(P)]
    wT = np.stack([tile(we, t) for t in cols])

    w2 = np.zeros((2 * RANK, 4 * P), f)
    w2[:RANK, :2 * P] = gla_w_gate_f[0]
    w2[RANK:, 2 * P:] = gla_w_gate_b[0]
    b2 = np.concatenate([gla_b_gate_f[0], gla_b_gate_b[0]]).reshape(4, P).T

    qo = (NOPE + ROPE) * r(MH)[:, None]
    rp = NOPE + r(ROPE)
    wq = np.concatenate([(qo + r(NOPE)).ravel(), (qo + rp).ravel(), (qo + np.roll(rp, ROPE // 2)).ravel()])

    j, i = np.meshgrid(r(P), r(P), indexing="ij")
    masks = [((j // (2 * s) == i // (2 * s)) & (j // s != i // s)) for s in LEVELS] + [i == j]
    inv = f(1) / (10000.0 ** (r(0, ROPE, 2) / ROPE)).astype(f)
    cst = np.concatenate([np.eye(P, dtype=f)] + [m.astype(f) for m in masks] +
                         [np.tile(inv, 4)[:, None], np.where(r(P) % ROPE < ROPE // 2, -1, 1).astype(f)[:, None],
                          np.full((P, 1), np.pi / 2, f)], axis=1)
    uz = [tile(w_in_o[0], o + P * n + r(P)) for n in range(CT) for o in (0, 2 * SGW)]
    return {
        "x": c_(x[0]), "cvec": c_(c[0].reshape(KD, P).T), "pos": c_(positions),
        "wmod": c_(w_mod), "bmod": c_(b_mod), "gpre": c_(g_pre.reshape(2, KD, P).transpose(2, 0, 1)), "gpost": c_(g_post),
        "wT": c_(wT), "w2": w2, "b2": c_(b2), "gnorm": c_(gla_g_norm[0][:, None]),
        "gq": c_(mla_g_q[0].reshape(2, P).T), "gkv": c_(mla_g_kv[0][:, None]),
        "wq": c_(tile(mla_w_uq[0], wq).reshape(P, 2, D)), "wkv": c_(mla_w_ukv[0].reshape(P, MH, NOPE + MV)),
        "woe": c_(w_out_e[0].reshape(KD, P, D)), "woo": c_(w_out_o[0].reshape(CT, P, D)),
        "wv": c_(np.stack([tile(w_in_o[0], SGW + 512 * n + r(512)) for n in range(4)])),
        "wuz": c_(np.stack(uz)),
        "sgg": c_(sg_g_norm[0].reshape(CT, P).T), "sgb": c_(sg_b_norm[0].reshape(CT, P).T),
        "sgw": c_(sg_w_s[0].transpose(2, 0, 1).reshape(P, SG_G * P)), "sgbs": c_(sg_b_s[0].reshape(1, SG_G * P)),
        "cst": c_(cst),
    }


def kernel(**inputs):
    import numpy as _np
    import concourse.bacc as _bacc
    from concourse import mybir as _mybir
    from concourse.bass_utils import run_bass_kernel_spmd as _run

    arrays = lay_out(**{k: _np.asarray(v) for k, v in inputs.items()})
    nc = _bacc.Bacc("TRN2", target_bir_lowering=False, num_devices=1)
    a = {n: nc.dram_tensor(n, v.shape, _mybir.dt.from_np(v.dtype), kind="ExternalInput").ap() for n, v in arrays.items()}
    out = nc.dram_tensor("out", (S, D), F32, kind="ExternalOutput").ap()
    emit(nc, a, out)
    r = _run(nc, [arrays], core_ids=[0])
    return r.results[0]["out"].reshape(1, S, D)
```
